# Optimizing a Trainium2 kernel written in Bass

```python
import math
import jax, jax.numpy as jnp
from jax import lax
import numpy as np

D_MODEL = 1024
BATCH = 1
SEQ = 256
DEPTH = 1

MEM_LEN = 256
MEM_HEADS = 4
MEM_HEAD_DIM = D_MODEL // MEM_HEADS
A_HEADS = 8
A_HEAD_DIM = 64
A_WIDTH = A_HEADS * A_HEAD_DIM
MOBA_BLOCK = 256
MOBA_TOPK = 3
B_HEADS = 4
B_QK_DIM = 64
B_V_DIM = 2 * B_QK_DIM
B_QK_WIDTH = B_HEADS * 2 * B_QK_DIM
B_WIDTH = B_HEADS * B_V_DIM
MIX_WIDTH = A_WIDTH + B_WIDTH
IN_WIDTH = 3 * A_WIDTH + 2 * B_QK_WIDTH + B_WIDTH
IN_SPLITS = [A_WIDTH, 2 * A_WIDTH, 3 * A_WIDTH, 3 * A_WIDTH + B_QK_WIDTH, 3 * A_WIDTH + 2 * B_QK_WIDTH]
N_ATT_HEADS = A_HEADS + B_HEADS
REL_BUCKETS = 32
REL_MAX_DIST = 128
D_FF = -(-8 * D_MODEL // (3 * 256)) * 256
Q_BLOCK = 128
EPS = 1e-6
NEG_INF = -1e30


def rms_norm(x, g):
    xf = x.astype(jnp.float32)
    y = xf * lax.rsqrt(jnp.mean(xf * xf, axis=-1, keepdims=True) + EPS)
    return (y * g.astype(jnp.float32)).astype(x.dtype)

def rel_bucket(dist):
    n = jnp.maximum(dist, 0)
    max_exact = REL_BUCKETS // 2
    log_ratio = jnp.log(jnp.maximum(n, max_exact).astype(jnp.float32) / max_exact) / math.log(REL_MAX_DIST / max_exact)
    large = max_exact + (log_ratio * (REL_BUCKETS - max_exact)).astype(jnp.int32)
    large = jnp.minimum(large, REL_BUCKETS - 1)
    return jnp.where(n < max_exact, n, large)

def moba_attention(q, k, v, table_a):
    B_, S, H, dh = q.shape
    nb = -(-S // MOBA_BLOCK)
    pad = nb * MOBA_BLOCK - S
    topk = min(MOBA_TOPK, nb)
    n_chunks = S // Q_BLOCK
    scale = dh ** -0.5
    bias_ht = table_a.T.astype(jnp.float32)
    h_i = jnp.arange(H)[:, None, None]
    blk_ids = jnp.arange(nb)
    key_off = jnp.arange(MOBA_BLOCK)

    def per_batch(args):
        q1, k1, v1 = args
        kp = jnp.pad(k1, ((0, pad), (0, 0), (0, 0))).reshape(nb, MOBA_BLOCK, H, dh).transpose(2, 0, 1, 3)
        vp = jnp.pad(v1, ((0, pad), (0, 0), (0, 0))).reshape(nb, MOBA_BLOCK, H, dh).transpose(2, 0, 1, 3)
        kmean = jnp.mean(kp.astype(jnp.float32), axis=2)
        qc = q1.reshape(n_chunks, Q_BLOCK, H, dh).transpose(0, 2, 1, 3)

        def per_chunk(args2):
            qblk, c = args2
            t = c * Q_BLOCK + jnp.arange(Q_BLOCK)
            own = t // MOBA_BLOCK
            gate = jnp.einsum('hqd,hnd->hqn', qblk.astype(jnp.float32), kmean)
            gate = jnp.where(blk_ids[None, None, :] < own[None, :, None], gate, NEG_INF)
            _, sel = lax.top_k(gate, topk)
            idx = jnp.concatenate([sel, jnp.broadcast_to(own[None, :, None], (H, Q_BLOCK, 1))], axis=-1)
            k_sel = kp[h_i, idx]
            v_sel = vp[h_i, idx]
            logits = jnp.einsum('hqd,hqtld->hqtl', qblk, k_sel, preferred_element_type=jnp.float32) * scale
            kpos = idx[..., None] * MOBA_BLOCK + key_off
            dist = t[None, :, None, None] - kpos
            logits = logits + bias_ht[h_i[..., None], rel_bucket(dist)]
            slot_ok = jnp.concatenate([jnp.arange(topk)[None, :] < own[:, None],
                                       jnp.ones((Q_BLOCK, 1), dtype=bool)], axis=1)
            mask = slot_ok[None, :, :, None] & (dist >= 0)
            logits = jnp.where(mask, logits, NEG_INF)
            p = jax.nn.softmax(logits.reshape(H, Q_BLOCK, -1), axis=-1).reshape(logits.shape)
            out = jnp.einsum('hqtl,hqtld->hqd', p.astype(v_sel.dtype), v_sel, preferred_element_type=jnp.float32)
            return out.astype(q.dtype)

        outs = lax.map(per_chunk, (qc, jnp.arange(n_chunks)))
        return outs.transpose(0, 2, 1, 3).reshape(S, H, dh)

    return lax.map(per_batch, (q, k, v))

def diff_attention(q, k, v, table_b, lam, subln_g, lambda_init):
    B_, S, H, _, dq = q.shape
    n_chunks = S // Q_BLOCK
    scale = dq ** -0.5
    kt = k.transpose(0, 2, 3, 1, 4)
    vt = v.transpose(0, 2, 1, 3)
    qc = q.reshape(B_, n_chunks, Q_BLOCK, H, 2, dq).transpose(1, 0, 3, 4, 2, 5)
    bias_ht = table_b.T.astype(jnp.float32)
    s_pos = jnp.arange(S)

    def per_chunk(args):
        qblk, c = args
        t = c * Q_BLOCK + jnp.arange(Q_BLOCK)
        dist = t[:, None] - s_pos[None, :]
        bias = bias_ht[:, rel_bucket(dist)]
        logits = jnp.einsum('bhmqd,bhmsd->bhmqs', qblk, kt, preferred_element_type=jnp.float32) * scale
        logits = jnp.where(dist >= 0, logits + bias[None, :, None], NEG_INF)
        p = jax.nn.softmax(logits, axis=-1)
        attn = p[:, :, 0] - lam * p[:, :, 1]
        return jnp.einsum('bhqs,bhsd->bhqd', attn.astype(v.dtype), vt, preferred_element_type=jnp.float32)

    outs = lax.map(per_chunk, (qc, jnp.arange(n_chunks)))
    o = outs.transpose(1, 0, 3, 2, 4).reshape(B_, S, H, -1)
    o = rms_norm(o, subln_g) * (1.0 - lambda_init)
    return o.astype(v.dtype)

def memory_cross_attention(x, mem, norm_g, mem_g, wq, wk, wv, wo):
    B_, S, _ = x.shape
    M = mem.shape[1]
    h = rms_norm(x, norm_g)
    m = rms_norm(mem, mem_g)
    q = (h @ wq).reshape(B_, S, MEM_HEADS, MEM_HEAD_DIM)
    k = (m @ wk).reshape(B_, M, MEM_HEADS, MEM_HEAD_DIM)
    v = (m @ wv).reshape(B_, M, MEM_HEADS, MEM_HEAD_DIM)
    logits = jnp.einsum('bshd,bmhd->bhsm', q, k, preferred_element_type=jnp.float32) * (MEM_HEAD_DIM ** -0.5)
    p = jax.nn.softmax(logits, axis=-1)
    o = jnp.einsum('bhsm,bmhd->bshd', p.astype(v.dtype), v, preferred_element_type=jnp.float32).astype(x.dtype)
    return o.reshape(B_, S, MEM_HEADS * MEM_HEAD_DIM) @ wo

def swiglu(x, norm_g, w_gate, w_up, w_down):
    h = rms_norm(x, norm_g)
    return (jax.nn.silu(h @ w_gate) * (h @ w_up)) @ w_down

def first_inputs(seed: int = 0) -> dict:
    key = jax.random.key(seed)
    ks = jax.random.split(key, 24)
    f32 = jnp.float32

    def w(k, shape, fan_in):
        return jax.random.normal(k, shape, f32) * (fan_in ** -0.5)

    def gain(k, shape):
        return 1.0 + 0.02 * jax.random.normal(k, shape, f32)

    return {
        "x": jax.random.normal(ks[0], (BATCH, SEQ, D_MODEL), f32),
        "mem": jax.random.normal(ks[1], (BATCH, MEM_LEN, D_MODEL), f32),
        "mix_norm_g": gain(ks[2], (DEPTH, D_MODEL)),
        "w_in": w(ks[3], (DEPTH, D_MODEL, IN_WIDTH), D_MODEL),
        "moba_out_g": gain(ks[4], (DEPTH, A_WIDTH)),
        "diff_lambda": 0.1 * jax.random.normal(ks[5], (DEPTH, 4, B_QK_DIM), f32),
        "diff_subln_g": gain(ks[6], (DEPTH, B_V_DIM)),
        "w_out": w(ks[7], (DEPTH, MIX_WIDTH, D_MODEL), MIX_WIDTH),
        "rel_bias_table": 0.5 * jax.random.normal(ks[8], (REL_BUCKETS, N_ATT_HEADS), f32),
        "cross_norm_g": gain(ks[9], (DEPTH, D_MODEL)),
        "mem_norm_g": gain(ks[10], (DEPTH, D_MODEL)),
        "w_cq": w(ks[11], (DEPTH, D_MODEL, MEM_HEADS * MEM_HEAD_DIM), D_MODEL),
        "w_ck": w(ks[12], (DEPTH, D_MODEL, MEM_HEADS * MEM_HEAD_DIM), D_MODEL),
        "w_cv": w(ks[13], (DEPTH, D_MODEL, MEM_HEADS * MEM_HEAD_DIM), D_MODEL),
        "w_co": w(ks[14], (DEPTH, MEM_HEADS * MEM_HEAD_DIM, D_MODEL), MEM_HEADS * MEM_HEAD_DIM),
        "ffn_norm_g": gain(ks[15], (DEPTH, D_MODEL)),
        "w_gate": w(ks[16], (DEPTH, D_MODEL, D_FF), D_MODEL),
        "w_up": w(ks[17], (DEPTH, D_MODEL, D_FF), D_MODEL),
        "w_down": w(ks[18], (DEPTH, D_FF, D_MODEL), D_FF),
        "final_norm_g": gain(ks[19], (D_MODEL,)),
    }

def first_block(x, mem, mix_norm_g, w_in, moba_out_g, diff_lambda, diff_subln_g, w_out, rel_bias_table,
              cross_norm_g, mem_norm_g, w_cq, w_ck, w_cv, w_co, ffn_norm_g, w_gate, w_up, w_down,
              final_norm_g):
    B_, S, _ = x.shape
    table_a = rel_bias_table[:, :A_HEADS]
    table_b = rel_bias_table[:, A_HEADS:]
    for l in range(DEPTH):
        h = rms_norm(x, mix_norm_g[l])
        proj = jnp.einsum('bsd,de->bse', h, w_in[l])
        qa, ka, va, qb, kb, vb = jnp.split(proj, IN_SPLITS, axis=-1)
        oa = moba_attention(qa.reshape(B_, S, A_HEADS, A_HEAD_DIM),
                            ka.reshape(B_, S, A_HEADS, A_HEAD_DIM),
                            va.reshape(B_, S, A_HEADS, A_HEAD_DIM), table_a)
        oa = rms_norm(oa.reshape(B_, S, A_WIDTH), moba_out_g[l])
        lambda_init = 0.8 - 0.6 * math.exp(-0.3 * l)
        lp = diff_lambda[l].astype(jnp.float32)
        lam = jnp.exp(jnp.sum(lp[0] * lp[1])) - jnp.exp(jnp.sum(lp[2] * lp[3])) + lambda_init
        ob = diff_attention(qb.reshape(B_, S, B_HEADS, 2, B_QK_DIM),
                            kb.reshape(B_, S, B_HEADS, 2, B_QK_DIM),
                            vb.reshape(B_, S, B_HEADS, B_V_DIM),
                            table_b, lam, diff_subln_g[l], lambda_init)
        ob = ob.reshape(B_, S, B_WIDTH)
        mixed = jnp.concatenate([oa, ob], axis=-1)
        x = x + jnp.einsum('bse,ed->bsd', mixed, w_out[l])
        x = x + memory_cross_attention(x, mem, cross_norm_g[l], mem_norm_g[l], w_cq[l], w_ck[l], w_cv[l], w_co[l])
        x = x + swiglu(x, ffn_norm_g[l], w_gate[l], w_up[l], w_down[l])
    return rms_norm(x, final_norm_g)


DEPTH_2 = 2

N_A = DEPTH_2 // 2
N_B = DEPTH_2 - N_A
N_MEM = 256
HEAD_DIM = 64
RWKV_HEADS = 12
RWKV_DIM = RWKV_HEADS * HEAD_DIM
MEM_DIM = MEM_HEADS * HEAD_DIM
MIX_WIDTH_2 = RWKV_DIM + MEM_DIM
DECAY_LORA = 64
AAA_LORA = 64
MV_LORA = 32
GATE_LORA = 128
RWKV_IN = 3 * RWKV_DIM + DECAY_LORA + AAA_LORA + GATE_LORA
A_IN = RWKV_IN + MEM_DIM
RWKV_SPLITS = (RWKV_DIM, 2 * RWKV_DIM, 3 * RWKV_DIM, 3 * RWKV_DIM + DECAY_LORA,
               3 * RWKV_DIM + DECAY_LORA + AAA_LORA)
MLA_HEADS = 12
QK_NOPE = 64
QK_ROPE = 32
V_HEAD = 64
Q_LORA = 512
KV_LORA = 256
MLA_DIM = MLA_HEADS * V_HEAD
B_IN = Q_LORA + MEM_DIM
FFN_HIDDEN = ((8 * D_MODEL + 3 * 256 - 1) // (3 * 256)) * 256
ROPE_BASE = 10000.0
NORM_EPS = 1e-6
LNX_EPS = 64e-5


def rms_norm_2(x, g, eps=NORM_EPS):
    xf = x.astype(jnp.float32)
    y = xf * lax.rsqrt(jnp.mean(xf * xf, axis=-1, keepdims=True) + eps)
    return (y * g.astype(jnp.float32)).astype(x.dtype)

def token_shift(t):
    return jnp.pad(t, ((0, 0), (1, 0), (0, 0)))[:, :-1]

def l2_normalize(t):
    tf = t.astype(jnp.float32)
    n = jnp.sqrt(jnp.sum(tf * tf, axis=-1, keepdims=True))
    return (tf / jnp.maximum(n, 1e-12)).astype(t.dtype)

def head_group_norm(y, g, b):
    yf = y.astype(jnp.float32)
    mu = jnp.mean(yf, axis=-1, keepdims=True)
    var = jnp.mean(jnp.square(yf - mu), axis=-1, keepdims=True)
    out = (yf - mu) * lax.rsqrt(var + LNX_EPS)
    out = out * g.reshape(RWKV_HEADS, HEAD_DIM).astype(jnp.float32) + b.reshape(RWKV_HEADS, HEAD_DIM).astype(jnp.float32)
    return out.astype(y.dtype)

def swiglu_2(h, w_gu, w_down):
    gate, up = jnp.split(h @ w_gu, 2, axis=-1)
    return (jax.nn.silu(gate) * up) @ w_down

def rope_tables(positions):
    half = QK_ROPE // 2
    inv_freq = ROPE_BASE ** (-jnp.arange(half, dtype=jnp.float32) / half)
    ang = positions.astype(jnp.float32)[..., None] * inv_freq
    return jnp.cos(ang), jnp.sin(ang)

def rope(t, cos, sin):
    tf = t.astype(jnp.float32)
    t1, t2 = jnp.split(tf, 2, axis=-1)
    return jnp.concatenate([t1 * cos - t2 * sin, t2 * cos + t1 * sin], axis=-1).astype(t.dtype)

def rwkv7_scan(r, decay, k, v, a, b):
    dtype = r.dtype
    bsz, _, nh, n = r.shape
    seqs = tuple(jnp.moveaxis(t.astype(jnp.float32), 1, 0) for t in (r, decay, k, v, a, b))

    def step(state, inp):
        r_t, w_t, k_t, v_t, a_t, b_t = inp
        sa = jnp.einsum('bhvk,bhk->bhv', state, a_t)
        state = (state * w_t[:, :, None, :] + sa[..., None] * b_t[:, :, None, :]
                 + v_t[..., None] * k_t[:, :, None, :])
        return state, jnp.einsum('bhvk,bhk->bhv', state, r_t)

    s0 = jnp.zeros((bsz, nh, n, n), jnp.float32)
    _, ys = lax.scan(step, s0, seqs)
    return jnp.moveaxis(ys, 0, 1).astype(dtype)

def memory_attention(q, mem_n, w_kv):
    bsz, n_mem, _ = mem_n.shape
    mkv = mem_n @ w_kv
    mk = mkv[..., :MEM_DIM].reshape(bsz, n_mem, MEM_HEADS, HEAD_DIM)
    mv = mkv[..., MEM_DIM:].reshape(bsz, n_mem, MEM_HEADS, HEAD_DIM)
    s = jnp.einsum('bshd,bmhd->bhsm', q, mk, preferred_element_type=jnp.float32) * (HEAD_DIM ** -0.5)
    p = jax.nn.softmax(s, axis=-1).astype(mv.dtype)
    o = jnp.einsum('bhsm,bmhd->bshd', p, mv)
    return o.reshape(q.shape[0], q.shape[1], MEM_DIM)

def causal_mla_attention(q_nope, q_rope, k_nope, k_rope, v):
    bsz, s_len, nh, _ = q_nope.shape
    nb = s_len // Q_BLOCK
    key_pos = jnp.arange(s_len)
    scale = (QK_NOPE + QK_ROPE) ** -0.5

    def to_blocks(t):
        return jnp.moveaxis(t.reshape((bsz, nb, Q_BLOCK) + t.shape[2:]), 1, 0)

    def block(args):
        qn, qr, blk = args
        s = (jnp.einsum('bqhd,bkhd->bhqk', qn, k_nope, preferred_element_type=jnp.float32)
             + jnp.einsum('bqhd,bkd->bhqk', qr, k_rope, preferred_element_type=jnp.float32)) * scale
        q_pos = blk * Q_BLOCK + jnp.arange(Q_BLOCK)
        s = jnp.where(key_pos[None, :] <= q_pos[:, None], s, -jnp.inf)
        p = jax.nn.softmax(s, axis=-1).astype(v.dtype)
        return jnp.einsum('bhqk,bkhd->bqhd', p, v)

    out = lax.map(block, (to_blocks(q_nope), to_blocks(q_rope), jnp.arange(nb)))
    return jnp.moveaxis(out, 0, 1).reshape(bsz, s_len, nh * v.shape[-1])

def second_inputs(seed: int = 0) -> dict:
    key = jax.random.key(seed)
    keys = iter(jax.random.split(key, 64))

    def nrm(shape, scale):
        return jax.random.normal(next(keys), shape, jnp.float32) * scale

    def gain(shape):
        return 1.0 + nrm(shape, 0.02)

    def unif(shape, lo, hi):
        return jax.random.uniform(next(keys), shape, jnp.float32, lo, hi)

    nv = max(N_A - 1, 0)
    qk_up = MLA_HEADS * (QK_NOPE + QK_ROPE)
    kv_up = MLA_HEADS * (QK_NOPE + V_HEAD)
    return {
        'x': nrm((BATCH, SEQ, D_MODEL), 1.0),
        'mem': nrm((BATCH, N_MEM, D_MODEL), 1.0),
        'positions': (jnp.arange(SEQ, dtype=jnp.int32)[None, :]
                      + jax.random.randint(next(keys), (BATCH, 1), 0, 1024, jnp.int32)),
        'mem_norm_g': gain((D_MODEL,)),
        'a_norm1_g': gain((N_A, D_MODEL)),
        'a_w_in': nrm((N_A, D_MODEL, A_IN), D_MODEL ** -0.5),
        'a_shift_mu': unif((N_A, RWKV_IN), 0.0, 1.0),
        'a_decay_up': nrm((N_A, DECAY_LORA, RWKV_DIM), 0.5 * DECAY_LORA ** -0.5),
        'a_decay_bias': unif((N_A, RWKV_DIM), -6.0, 0.5),
        'a_aaa_up': nrm((N_A, AAA_LORA, RWKV_DIM), AAA_LORA ** -0.5),
        'a_aaa_bias': nrm((N_A, RWKV_DIM), 0.1),
        'a_gate_up': nrm((N_A, GATE_LORA, RWKV_DIM), GATE_LORA ** -0.5),
        'a_k_k': 0.85 + nrm((N_A, RWKV_DIM), 0.05),
        'a_k_a': 1.0 + nrm((N_A, RWKV_DIM), 0.05),
        'a_r_k': nrm((N_A, RWKV_HEADS, HEAD_DIM), 0.1),
        'a_lnx_g': gain((N_A, RWKV_DIM)),
        'a_lnx_b': nrm((N_A, RWKV_DIM), 0.02),
        'a_mem_kv': nrm((N_A, D_MODEL, 2 * MEM_DIM), D_MODEL ** -0.5),
        'a_w_out': nrm((N_A, MIX_WIDTH_2, D_MODEL), MIX_WIDTH_2 ** -0.5),
        'a_norm2_g': gain((N_A, D_MODEL)),
        'a_ffn_gu': nrm((N_A, D_MODEL, 2 * FFN_HIDDEN), D_MODEL ** -0.5),
        'a_ffn_down': nrm((N_A, FFN_HIDDEN, D_MODEL), FFN_HIDDEN ** -0.5),
        'vres_mu': unif((nv, D_MODEL), 0.0, 1.0),
        'vres_down': nrm((nv, D_MODEL, MV_LORA), D_MODEL ** -0.5),
        'vres_up': nrm((nv, MV_LORA, RWKV_DIM), MV_LORA ** -0.5),
        'vres_bias': nrm((nv, RWKV_DIM), 0.1),
        'kv_norm_g': gain((D_MODEL,)),
        'kv_w_down': nrm((D_MODEL, KV_LORA + QK_ROPE), D_MODEL ** -0.5),
        'kv_latent_g': gain((KV_LORA,)),
        'kv_w_up': nrm((KV_LORA, kv_up), KV_LORA ** -0.5),
        'b_norm1_g': gain((N_B, D_MODEL)),
        'b_w_in': nrm((N_B, D_MODEL, B_IN), D_MODEL ** -0.5),
        'b_q_norm_g': gain((N_B, Q_LORA)),
        'b_q_up': nrm((N_B, Q_LORA, qk_up), Q_LORA ** -0.5),
        'b_mem_kv': nrm((N_B, D_MODEL, 2 * MEM_DIM), D_MODEL ** -0.5),
        'b_w_out': nrm((N_B, MIX_WIDTH_2, D_MODEL), MIX_WIDTH_2 ** -0.5),
        'b_norm2_g': gain((N_B, D_MODEL)),
        'b_ffn_gu': nrm((N_B, D_MODEL, 2 * FFN_HIDDEN), D_MODEL ** -0.5),
        'b_ffn_down': nrm((N_B, FFN_HIDDEN, D_MODEL), FFN_HIDDEN ** -0.5),
        'final_norm_g': gain((D_MODEL,)),
    }

def second_block(x, mem, positions, mem_norm_g,
              a_norm1_g, a_w_in, a_shift_mu, a_decay_up, a_decay_bias, a_aaa_up, a_aaa_bias,
              a_gate_up, a_k_k, a_k_a, a_r_k, a_lnx_g, a_lnx_b, a_mem_kv, a_w_out, a_norm2_g,
              a_ffn_gu, a_ffn_down,
              vres_mu, vres_down, vres_up, vres_bias,
              kv_norm_g, kv_w_down, kv_latent_g, kv_w_up,
              b_norm1_g, b_w_in, b_q_norm_g, b_q_up, b_mem_kv, b_w_out, b_norm2_g,
              b_ffn_gu, b_ffn_down,
              final_norm_g):
    bsz, s_len, _ = x.shape

    def heads(t, nh):
        return t.reshape(bsz, s_len, nh, HEAD_DIM)

    mem_n = rms_norm_2(mem, mem_norm_g)
    cos, sin = rope_tables(positions)
    v_first = None
    k_nope = k_rope = v_mla = None

    for layer in range(DEPTH_2):
        if layer < N_A:
            i = layer
            h = rms_norm_2(x, a_norm1_g[i])
            proj = h @ a_w_in[i]
            p_tm, q_mem = proj[..., :RWKV_IN], proj[..., RWKV_IN:]
            p_tm = p_tm + (token_shift(p_tm) - p_tm) * a_shift_mu[i]
            r, k, v, d_lo, a_lo, g_lo = jnp.split(p_tm, RWKV_SPLITS, axis=-1)
            log_w = -jax.nn.softplus(-(a_decay_bias[i] + jnp.tanh(d_lo) @ a_decay_up[i])) - 0.5
            decay = jnp.exp(-jnp.exp(log_w.astype(jnp.float32)))
            lr = jax.nn.sigmoid(a_aaa_bias[i] + a_lo @ a_aaa_up[i])
            gate = jax.nn.sigmoid(g_lo) @ a_gate_up[i]
            if i == 0:
                v_first = v
            else:
                hv = h + (token_shift(h) - h) * vres_mu[i - 1]
                v = v + (v_first - v) * jax.nn.sigmoid(
                    vres_bias[i - 1] + (hv @ vres_down[i - 1]) @ vres_up[i - 1])
            kk = l2_normalize(heads(k * a_k_k[i], RWKV_HEADS))
            k = k * (1.0 + (lr - 1.0) * a_k_a[i])
            rh, kh, vh, lrh = (heads(t, RWKV_HEADS) for t in (r, k, v, lr))
            y = rwkv7_scan(rh, heads(decay, RWKV_HEADS), kh, vh, -kk, kk * lrh)
            y = head_group_norm(y, a_lnx_g[i], a_lnx_b[i])
            y = y + jnp.sum(rh * kh * a_r_k[i], axis=-1, keepdims=True) * vh
            y_mix = y.reshape(bsz, s_len, RWKV_DIM) * gate
            m = memory_attention(heads(q_mem, MEM_HEADS), mem_n, a_mem_kv[i])
            x = x + jnp.concatenate([y_mix, m], axis=-1) @ a_w_out[i]
            x = x + swiglu_2(rms_norm_2(x, a_norm2_g[i]), a_ffn_gu[i], a_ffn_down[i])
        else:
            j = layer - N_A
            if j == 0:
                hk = rms_norm_2(x, kv_norm_g)
                ckr = hk @ kv_w_down
                c_kv = rms_norm_2(ckr[..., :KV_LORA], kv_latent_g)
                k_rope = rope(ckr[..., KV_LORA:], cos, sin)
                kv = (c_kv @ kv_w_up).reshape(bsz, s_len, MLA_HEADS, QK_NOPE + V_HEAD)
                k_nope, v_mla = kv[..., :QK_NOPE], kv[..., QK_NOPE:]
            h = rms_norm_2(x, b_norm1_g[j])
            proj = h @ b_w_in[j]
            c_q = rms_norm_2(proj[..., :Q_LORA], b_q_norm_g[j])
            q_mem = proj[..., Q_LORA:]
            q = (c_q @ b_q_up[j]).reshape(bsz, s_len, MLA_HEADS, QK_NOPE + QK_ROPE)
            q_nope = q[..., :QK_NOPE]
            q_rope = rope(q[..., QK_NOPE:], cos[:, :, None, :], sin[:, :, None, :])
            o = causal_mla_attention(q_nope, q_rope, k_nope, k_rope, v_mla)
            m = memory_attention(heads(q_mem, MEM_HEADS), mem_n, b_mem_kv[j])
            x = x + jnp.concatenate([o, m], axis=-1) @ b_w_out[j]
            x = x + swiglu_2(rms_norm_2(x, b_norm2_g[j]), b_ffn_gu[j], b_ffn_down[j])

    return rms_norm_2(x, final_norm_g)


def setup_inputs(seed=0):
    out = dict(first_inputs(seed))
    for name, value in second_inputs(seed + 1).items():
        if name != "x":
            out[name + "_2"] = value
    return out


def reference(
    x, mem, mix_norm_g, w_in, moba_out_g, diff_lambda, diff_subln_g, w_out, rel_bias_table,
    cross_norm_g, mem_norm_g, w_cq, w_ck, w_cv, w_co, ffn_norm_g, w_gate, w_up, w_down,
    final_norm_g, mem_2, positions_2, mem_norm_g_2, a_norm1_g_2, a_w_in_2, a_shift_mu_2,
    a_decay_up_2, a_decay_bias_2, a_aaa_up_2, a_aaa_bias_2, a_gate_up_2, a_k_k_2, a_k_a_2,
    a_r_k_2, a_lnx_g_2, a_lnx_b_2, a_mem_kv_2, a_w_out_2, a_norm2_g_2, a_ffn_gu_2, a_ffn_down_2,
    vres_mu_2, vres_down_2, vres_up_2, vres_bias_2, kv_norm_g_2, kv_w_down_2, kv_latent_g_2,
    kv_w_up_2, b_norm1_g_2, b_w_in_2, b_q_norm_g_2, b_q_up_2, b_mem_kv_2, b_w_out_2,
    b_norm2_g_2, b_ffn_gu_2, b_ffn_down_2, final_norm_g_2,
):
    x = first_block(
        x, mem, mix_norm_g, w_in, moba_out_g, diff_lambda, diff_subln_g, w_out, rel_bias_table,
        cross_norm_g, mem_norm_g, w_cq, w_ck, w_cv, w_co, ffn_norm_g, w_gate, w_up, w_down,
        final_norm_g,
    )
    return second_block(
        x, mem_2, positions_2, mem_norm_g_2, a_norm1_g_2, a_w_in_2, a_shift_mu_2, a_decay_up_2,
        a_decay_bias_2, a_aaa_up_2, a_aaa_bias_2, a_gate_up_2, a_k_k_2, a_k_a_2, a_r_k_2,
        a_lnx_g_2, a_lnx_b_2, a_mem_kv_2, a_w_out_2, a_norm2_g_2, a_ffn_gu_2, a_ffn_down_2,
        vres_mu_2, vres_down_2, vres_up_2, vres_bias_2, kv_norm_g_2, kv_w_down_2, kv_latent_g_2,
        kv_w_up_2, b_norm1_g_2, b_w_in_2, b_q_norm_g_2, b_q_up_2, b_mem_kv_2, b_w_out_2,
        b_norm2_g_2, b_ffn_gu_2, b_ffn_down_2, final_norm_g_2,
    )


_drawn_inputs = setup_inputs


def setup_inputs(seed=0):
    import zlib

    import numpy as np

    out = dict(_drawn_inputs(seed))
    spreads = {}
    factors = {'moba_out_g': 3.377,
     'diff_subln_g': 3.821,
     'cross_norm_g': 8.0,
     'mem_norm_g': 8.0,
     'ffn_norm_g': 3.448,
     'mem_norm_g_2': 8.0,
     'a_norm1_g_2': 2.951,
     'a_aaa_bias_2': 3.092,
     'a_lnx_g_2': 6.161,
     'a_lnx_b_2': 4.619,
     'a_norm2_g_2': 3.496,
     'kv_norm_g_2': 8.0,
     'kv_latent_g_2': 8.0,
     'b_norm1_g_2': 8.0,
     'b_q_norm_g_2': 8.0,
     'b_norm2_g_2': 4.796,
     'final_norm_g_2': 2.857}
    for name, (base, spread) in spreads.items():
        noise = np.random.default_rng([zlib.crc32(name.encode()), seed]).standard_normal(out[name].shape)
        drawn = base * np.exp(spread * noise) if base else spread * noise
        out[name] = __import__('jax').numpy.asarray(drawn.astype(out[name].dtype))
    for name, factor in factors.items():
        out[name] = (out[name] * factor).astype(out[name].dtype)
    return out
```

```python
import math

import numpy as np

import concourse.bass as bass
from concourse import mybir

F32 = mybir.dt.float32
F32R = mybir.dt.float32r
I32 = mybir.dt.int32
ACT = mybir.ActivationFunctionType
ALU = mybir.AluOpType
AX = mybir.AxisListType

P = 128
S = 256
NT = S // P
D = 1024
KT = D // P
FF = 2816
NPAIR = FF // 256
KB = 1024
NEG = -1e30
EPS = 1e-6
LNX_EPS = 64e-5
RING = 4
UNIT = 2048
AHEAD = 3
A_HEADS, B_HEADS, MEM_HEADS, RW_HEADS, MLA_HEADS = 8, 4, 4, 12, 12
RW = RW_HEADS * 64
RWB = RW // P
SHB = 20
QK = 96
KAPPA = math.exp(-0.5)
LAMBDA_INIT = 0.8 - 0.6 * math.exp(0.0)


class Token:

    def __init__(self, sem, value, rate=0):
        self.sem, self.value, self.rate = sem, value, rate


class Lane:

    def __init__(self, nc, engine, name):
        self.engine, self.sem = engine, nc.alloc_semaphore(name)
        self.count, self.rate, self.round = 0, 0, None
        self.waited = {}

    def wait(self, *tokens):
        for t in tokens:
            if t is None:
                continue
            if isinstance(t, (list, tuple)):
                self.wait(*t)
                continue
            key = (t.sem.name, t.rate)
            if self.waited.get(key, 0) >= t.value:
                continue
            self.waited[key] = t.value
            self.engine.wait_ge(t.sem, t.value if not t.rate else self.round * t.rate + t.value)

    def last(self):
        return Token(self.sem, self.count, self.rate)

    def quiet(self, instruction, *args, after=(), **kw):
        self.wait(after)
        return instruction(*args, **kw)

    def __call__(self, instruction, *args, after=(), **kw):
        self.wait(after)
        instruction(*args, **kw).then_inc(self.sem, 1)
        self.count += 1
        return Token(self.sem, self.count, self.rate)


class Program:
    def __init__(self, nc, t):
        self.nc, self.t = nc, t
        self.PE = Lane(nc, nc.tensor, "pe_done")
        self.V = Lane(nc, nc.vector, "dve_done")
        self.A = Lane(nc, nc.scalar, "act_done")
        self.G = Lane(nc, nc.gpsimd, "pool_done")
        self.SP = Lane(nc, nc.sync, "sp_done")
        self.lanes = (self.PE, self.V, self.A, self.G, self.SP)
        self.loaded = [nc.alloc_semaphore(f"weights_loaded_{s}") for s in range(RING)]
        self.split_done = nc.alloc_semaphore("weights_split")
        self.used = nc.alloc_semaphore("weights_used")
        self.units = []
        self.looping = False
        self.n_split = 0
        self.bank_free = [None] * 8
        self.arena_tensors = 0
        self.gain_free = [None, None]
        self.gain_turn = 0
        self.pending = []

    def sb(self, name, shape, dtype=F32):
        return self.nc.alloc_sbuf_tensor(name, shape, dtype)

    def work(self, name, kb, shape, dtype=F32):
        size = 4 * int(np.prod(shape[1:]))
        assert kb * KB + size <= self.arena_size, (name, kb * KB + size, self.arena_size)
        return self.nc.alloc_sbuf_tensor_at(name, shape, dtype, offset=int(self.arena + kb * KB))

    def ring_token(self, sem, value, rate):
        return Token(sem, value, rate if self.looping else 0)

    def used_token(self, u):
        return self.ring_token(self.used, u + 1, RING)

    def split(self, u):
        s = u % RING
        hi = self.A(self.nc.scalar.activation, self.w_hi[:, s, :], self.w_raw[:, s, :], ACT.Copy,
                    after=(self.ring_token(self.loaded[s], 16 * (u // RING + 1), 16),
                           self.used_token(u - RING) if u >= RING else None))
        self.V.quiet(self.nc.vector.tensor_tensor, self.w_lo[:, s, :], self.w_raw[:, s, :],
                     self.w_hi[:, s, :].bitcast(F32), ALU.subtract, after=(hi,)).then_inc(self.split_done, 1)

    def unit_product(self, spec, k0, nk, nc_, width, first, last, lhs, banks, after=()):
        u = len(self.units)
        self.units.append(spec)
        s = u % RING
        while self.n_split < u + AHEAD and (self.looping or self.n_split < self.total_units):
            self.split(self.n_split)
            self.n_split += 1
        pe, mm = self.PE, self.nc.tensor.matmul
        pe.wait(self.ring_token(self.split_done, u + 1, RING), after)
        segs = [(c, min(512, width - c)) for c in range(0, width, 512)]
        passes = [(k, n) for k in range(nk) for n in range(3)]
        order = ([(k, n, tok) for tok in range(NT) for k, n in passes] if last
                 else [(k, n, tok) for k, n in passes for tok in range(NT)])
        first_tok = None
        for k, n, tok in order:
            x, w = ((0, self.w_hi), (1, self.w_hi), (0, self.w_lo))[n]
            for c, cw in segs:
                o = banks[tok * len(segs) + c // 512]
                m = mm(o[:, 0:cw], lhs[x][:, k0 + k, tok * P:(tok + 1) * P],
                       w[:, s, k * nc_ + c:k * nc_ + c + cw],
                       start=first and k == 0 and n == 0, stop=last and k == nk - 1 and n == 2)
            if last and (k, n, tok) == (nk - 1, 2, 0):
                m.then_inc(pe.sem, 1)
                pe.count += 1
                first_tok = pe.last()
        m.then_inc(self.used, 1)
        return [first_tok, self.used_token(u)]

    def job(self, name, lhs, ready, nk, c0, width, bank_ids, evacuate):
        banks = [self.bank[b] for b in bank_ids]
        pitch = 256 if (width <= 256 and nk == KT) else 512 if width <= 512 else width
        per = min(nk, UNIT // pitch)
        for k in range(0, nk, per):
            n = min(per, nk - k)
            after = ([self.bank_free[b] for b in bank_ids], ready) if k == 0 else ()
            done = self.unit_product(("part", name, k, n, c0, width, pitch), k, n, pitch, width, k == 0, k + n == nk,
                                     lhs, banks, after=after)
            if k + n == nk:
                evacuate(done)
            yield

    def run(self, *jobs):
        for j in jobs:
            for _ in j:
                pass

    def fill(self, units):
        while units > 0 and self.pending:
            try:
                next(self.pending[0])
                units -= 1
            except StopIteration:
                self.pending.pop(0)

    def fill_rest(self):
        self.run(*self.pending)
        self.pending = []

    def rows_of(self, dst, bank_ids, width, into=None):
        def evacuate(done):
            out = []
            for tok in range(NT):
                segs = [(c, min(512, width - c)) for c in range(0, width, 512)]
                for j, (c, w) in enumerate(segs):
                    b = bank_ids[tok * len(segs) + j]
                    t = self.copy(tok, dst(tok)[:, c:c + w], self.bank[b][:, 0:w], (done[tok],))
                    self.bank_free[b] = t
                    out.append(t)
            if into is not None:
                into.extend(out)
        return evacuate

    def loop(self, rounds, body, state):
        before = [lane.count for lane in self.lanes]
        body(0, state)
        grown = [lane.count - b for lane, b in zip(self.lanes, before)]
        rate_of = {lane.sem.name: (lane, g, b) for lane, g, b in zip(self.lanes, grown, before)}
        rate_of[self.used.name] = (None, RING, 0)

        def moved(t, turns):
            if t is None:
                return None
            if isinstance(t, (list, tuple)):
                return [moved(x, turns) for x in t]
            lane, g, b = rate_of[t.sem.name]
            if turns is None:
                return Token(t.sem, t.value, g) if lane is None or t.value > b else t
            return Token(t.sem, t.value + turns * g if t.rate else t.value)

        units, splits = len(self.units), self.n_split
        counts = [lane.count for lane in self.lanes]
        for k in state:
            state[k] = moved(state[k], None)
        self.bank_free = moved(self.bank_free, None)
        self.looping = True
        kept = [dict(lane.waited) for lane in self.lanes]
        with self.nc.Fori(0, rounds - 1) as i:
            for lane, g in zip(self.lanes, grown):
                lane.rate, lane.round = g, i
            body(i + 1, state)
        self.looping = False
        turns = rounds - 2
        for lane, g, c, w in zip(self.lanes, grown, counts, kept):
            assert lane.count - c == g
            lane.count = c + (rounds - 1) * g
            lane.rate, lane.round = 0, None
            lane.waited = w
        for k in state:
            state[k] = moved(state[k], turns)
        self.bank_free = moved(self.bank_free, turns)
        round_units = self.units[units:]
        del self.units[units:]
        for n in range(rounds - 1):
            self.units += [spec[:2] + (spec[2] + 2 * n,) + spec[3:] for spec in round_units]
        self.n_split = splits + (rounds - 1) * RING

    def load_gain(self, name, width=D, parts=1):
        b = self.gain_turn % 2
        self.gain_turn += 1
        sem = self.nc.alloc_semaphore(f"gain_{self.gain_turn}")
        out = self.gains[b][:, 0:width]
        self.G.wait(self.gain_free[b])
        self.nc.gpsimd.dma_start(out, self.t[name].to_broadcast((P, width))).then_inc(sem, 16)
        return out, Token(sem, 16), b

    def inv_rms(self, src, width, eps, ready, out, junk=None):
        if junk is None:
            junk = self.xn
        result = []
        for tok in range(NT):
            a = self.A(self.nc.scalar.activation, junk[:, tok, 0:width], src(tok), ACT.Square,
                       scale=float(width) ** -0.5, accum_out=out[:, tok:tok + 1],
                       after=(ready[tok], self.xn_free, self.rstd_free))
            result.append(self.power(out[:, tok:tok + 1], eps, (a,)))
        return result

    def power(self, ms, eps, ready):
        t = self.G(self.nc.gpsimd.tensor_scalar, ms, ms, eps, None, ALU.add, after=(ready,))
        n = ms.shape[-1]
        return self.G(self.nc.gpsimd.tensor_tensor, ms, ms, self.minus_half[0:ms.shape[0], 0:n], ALU.pow, after=(t,))

    def normalize(self, src, dst, width, gain, rstd, ready, dst_free=None):
        g, g_ready, b = gain
        step = min(width, 512)
        out = []
        for tok in range(NT):
            out.append([self.V(self.nc.vector.scalar_tensor_tensor, out=dst(tok)[:, c:c + step], in0=src(tok)[:, c:c + step],
                               scalar=rstd[:, tok:tok + 1], in1=g[:, c:c + step], op0=ALU.mult, op1=ALU.mult,
                               after=(ready[tok], g_ready, dst_free)) for c in range(0, width, step)])
        self.gain_free[b] = out
        self.rstd_free = out
        return out

    def transposes(self, blocks, ready, evacuate, banks=(4, 5, 6, 7), per=4):
        tokens, n = [], 0
        while n < len(blocks):
            now = blocks[n:n + per]
            b = banks[(n // per) % len(banks)]
            for j, (src, rows) in enumerate(now):
                self.PE.wait(ready, self.bank_free[b])
                m = self.nc.tensor.transpose(self.bank[b][0:rows, j * P:(j + 1) * P], src, self.ident[:, :])
            m.then_inc(self.PE.sem, 1)
            self.PE.count += 1
            done = Token(self.PE.sem, self.PE.count, self.PE.rate)
            read = evacuate(n // per, self.bank[b], done)
            self.bank_free[b] = read
            tokens.append(read)
            n += per
        return tokens

    def copy(self, n, out, in_, after):
        if n % 2:
            return self.A(self.nc.scalar.activation, out, in_, ACT.Copy, after=after)
        return self.V(self.nc.vector.tensor_copy, out, in_, after=after)

    def to_channels(self, src, nk, hi, lo, ready, free=None, banks=(4, 5, 6, 7), before=None):
        out = []
        groups = [(tok, k) for tok in range(NT) for k in range(0, nk, 4)]
        made = {}
        for n, (tok, k0) in enumerate(groups):
            if before is not None:
                for g in groups[n:n + 2]:
                    if g not in made:
                        made[g] = before(g[0], g[1] // 4)
            b, m = banks[n % len(banks)], min(4, nk - k0)
            self.PE.wait(ready, made.get((tok, k0)), self.bank_free[b])
            for j in range(m):
                t = self.nc.tensor.transpose(self.bank[b][:, j * P:(j + 1) * P], src(tok, k0 + j), self.ident[:, :])
            t.then_inc(self.PE.sem, 1)
            self.PE.count += 1
            done = self.PE.last()
            view = self.bank[b][:, 0:m * P].rearrange("p (k t) -> p k t", k=m)
            cols = (slice(None), slice(k0, k0 + m), slice(tok * P, (tok + 1) * P))
            h = self.A(self.nc.scalar.activation, hi[cols], view, ACT.Copy, after=(done, free))
            l = self.V(self.nc.vector.tensor_tensor, lo[cols], view, hi[cols].bitcast(F32), ALU.subtract,
                       after=(h, done, free))
            self.bank_free[b] = [h, l]
            out += [h, l]
        return out

    def norm_to_channels(self, x, width, gain, eps, hi, lo, ready, free=None, rstd_ready=None):
        if len(ready) != NT:
            ready = [ready] * NT
        r = rstd_ready or self.inv_rms(lambda tok: x[:, tok, 0:width], width, eps, ready, self.rstd)
        g, g_ready, b = gain
        step = min(width, 512)
        norms = []
        xn_free = self.xn_free

        def before(tok, n):
            c = slice(n * step, (n + 1) * step)
            norms.append(self.V(self.nc.vector.scalar_tensor_tensor, out=self.xn[:, tok, c], in0=x[:, tok, c],
                                scalar=self.rstd[:, tok:tok + 1], in1=g[:, c], op0=ALU.mult, op1=ALU.mult,
                                after=(r[tok], g_ready, xn_free)))
            return norms[-1]
        t = self.to_channels(lambda tok, k: self.xn[:, tok, k * P:(k + 1) * P], width // P, hi, lo, None, free,
                             before=before)
        self.gain_free[b] = self.rstd_free = norms
        self.xn_free = t
        return t

    def attention(self, heads, stage_qk, spans, scale, bias, v_of, dv, out_of, ready, tag, out_free=None, between=None,
                  combine=None):
        nc, PE, V, A = self.nc, self.PE, self.V, self.A
        off = [0, spans[0]]
        total = sum(spans)
        step = 1 if combine is None else 2
        n = len(heads) // step
        st = {}
        e_size = 384 if total == 384 else 512
        self.e_free = [list(self.e_free)] * 4
        e_free, pt_free, l_free = self.e_free, self.pt_free, self.l_free
        outs = []
        ne = 4 if step == 2 else 2

        def logits_and_exp(i):
            st[i] = {"e": [], "exp": []}
            for j in range(step):
                hh = heads[i * step + j]
                b = 4 + hh % 2
                PE.wait(ready, self.bank_free[b])
                q = stage_qk(hh, self.bank[b], spans, off)
                stat = self.stats[:, (i * step + j) % 4, :]
                sf = self.stat_free[(i * step + j) % 4]
                lb = hh % 2
                if bias is not None:
                    L = self.lbuf[:, lb, 0:total]
                    l = V(nc.vector.scalar_tensor_tensor, out=L, in0=self.bank[b][:, 0:total], scalar=scale,
                          in1=bias(hh), op0=ALU.mult, op1=ALU.add, after=(q, l_free[lb], self.bias_ready))
                    self.bank_free[b] = l
                    k = 1.0
                else:
                    L, l, k = self.bank[b][:, 0:total], q, scale
                mx = [V(nc.vector.tensor_reduce, out=stat[:, tok:tok + 1], in_=L[:, off[tok]:off[tok] + spans[tok]],
                        axis=AX.X, op=ALU.max, negate=True, after=(l, sf)) for tok in range(NT)]
                if k != 1.0:
                    mx = V(nc.vector.tensor_scalar, stat[:, 0:2], stat[:, 0:2], k, None, ALU.mult, after=mx)
                slot = (i * step + j) % ne
                E = self.ebuf[:, slot * e_size:slot * e_size + total]
                ex = [A(nc.scalar.activation, E[:, off[tok]:off[tok] + spans[tok]], L[:, off[tok]:off[tok] + spans[tok]],
                        ACT.Exp, bias=stat[:, tok:tok + 1], scale=k, accum_out=stat[:, 2 + tok:3 + tok],
                        after=(mx, l, e_free[slot])) for tok in range(NT)]
                if bias is None:
                    self.bank_free[b] = ex
                else:
                    l_free[lb] = ex
                st[i]["e"].append((E, slot, stat, (i * step + j) % 4))
                st[i]["exp"].append(ex)

        def weights_transposed(i):
            E, slot, stat, sn = st[i]["e"][0]
            rc = [V(nc.vector.reciprocal, s_[:, 4:6], s_[:, 2:4], after=(x, self.stat_free[m]))
                  for (_, _, s_, m), x in zip(st[i]["e"], st[i]["exp"])]
            if step == 2:
                E1, slot1, stat1, sn1 = st[i]["e"][1]
                m = V(nc.vector.tensor_scalar, stat1[:, 6:8], stat1[:, 4:6], combine[0], None, ALU.mult,
                      after=(rc, combine[1]))
                rc = []
                for tok in range(NT):
                    a, z = off[tok], off[tok] + spans[tok]
                    f = V(nc.vector.tensor_scalar, E1[:, a:z], E1[:, a:z], stat1[:, 6 + tok:7 + tok], None, ALU.mult,
                          after=(m,))
                    rc.append(V(nc.vector.scalar_tensor_tensor, out=E[:, a:z], in0=E[:, a:z],
                                scalar=stat[:, 4 + tok:5 + tok], in1=E1[:, a:z], op0=ALU.mult, op1=ALU.add, after=(f,)))
                e_free[slot1] = rc
                self.stat_free[sn1] = rc
                self.stat_free[sn] = rc
            blocks = [E[:, c:c + P] for c in range(0, total, P)]
            b = 6 + i % 2
            PE.wait(rc if step == 2 else st[i]["exp"], self.bank_free[b])
            for j, blk in enumerate(blocks):
                m = nc.tensor.transpose(self.bank[b][:, j * P:(j + 1) * P], blk, self.ident[:, :])
            m.then_inc(PE.sem, 1)
            PE.count += 1
            done = Token(PE.sem, PE.count)
            e_free[slot] = done
            pt = self.ptbuf[:, (i % 2) * 512:(i % 2) * 512 + total]
            c = A(nc.scalar.activation, pt, self.bank[b][:, 0:total], ACT.Copy, after=(done, pt_free[i % 2]))
            self.bank_free[b] = c
            st[i].update(pt=pt, copied=c, rc=rc, stat=stat, sn=sn)

        def values(i):
            b = 2 + i % 2
            pt = st[i]["pt"]
            PE.wait(st[i]["copied"], self.bank_free[b])
            for tok in range(NT):
                nb = spans[tok] // P
                for j in range(nb):
                    c = off[tok] + j * P
                    m = nc.tensor.matmul(self.bank[b][:, tok * dv:(tok + 1) * dv], pt[:, c:c + P], v_of(heads[i * step], j),
                                         start=j == 0, stop=j == nb - 1)
            m.then_inc(PE.sem, 1)
            PE.count += 1
            done = Token(PE.sem, PE.count)
            pt_free[i % 2] = done
            view = self.bank[b][:, 0:NT * dv].rearrange("p (t d) -> p t d", t=NT)
            if step == 2:
                o = self.A(nc.scalar.activation, out_of(i), view, ACT.Copy, after=(done, out_free))
            else:
                o = V(nc.vector.tensor_tensor, out_of(i), view,
                      st[i]["stat"][:, 4:6].unsqueeze(2).to_broadcast((P, NT, dv)), ALU.mult,
                      after=(done, st[i]["rc"], out_free))
                self.stat_free[st[i]["sn"]] = o
            self.bank_free[b] = o
            outs.append(o)

        for i in range(n + 2):
            if i < n:
                logits_and_exp(i)
            if 1 <= i <= n:
                weights_transposed(i - 1)
            if i >= 2:
                values(i - 2)
            if between is not None and i < n:
                between(i)
        return outs

    def qk_pairs(self, qT, kT, scale_rows=64):
        def stage(h, bank, spans, off):
            p, blk = 64 * (h % 2), h // 2
            for tok in range(NT):
                m = self.nc.tensor.matmul(bank[:, off[tok]:off[tok] + spans[tok]],
                                          qT[p:p + 64, blk, tok * P:(tok + 1) * P],
                                          kT[p:p + 64, blk, 0:spans[tok]], start=True, stop=True)
            m.then_inc(self.PE.sem, 1)
            self.PE.count += 1
            return Token(self.PE.sem, self.PE.count)
        return stage

    def add_residual(self, done, bank_ids, cols):
        out = []
        for tok, b in enumerate(bank_ids):
            o = self.x[:, tok, cols:cols + 512]
            t = self.V(self.nc.vector.tensor_tensor, o, self.bank[b][:, :], o, ALU.add, after=(done[tok], self.x_free))
            self.bank_free[b] = t
            out.append(t)
        return out

    def project_residual(self, name, lhs, ready):
        out = []
        for g in range(2):
            banks = (2 * g, 2 * g + 1)
            self.run(self.job(name, lhs, ready, KT, 512 * g, 512, banks,
                              lambda done: out.append(self.add_residual(done, banks, 512 * g))))
        self.xt_free = self.used_token(len(self.units) - 1)
        return [[out[g][tok] for g in range(2)] for tok in range(NT)]

    def feed_forward(self, gate_up, down, gain, ready):
        nc, PE, V, A = self.nc, self.PE, self.V, self.A
        n = self.norm_to_channels(self.x, D, gain, EPS, self.XH, self.XL, ready, self.xt_free)
        tag = down
        HH = self.work("hidden_hi_" + tag, 24, [P, 2 * NPAIR, S], F32R)
        HL = self.work("hidden_lo_" + tag, 46, [P, 2 * NPAIR, S], F32R)
        act = self.work("silu_" + tag, 69, [P, 2, NT, 256])
        hid = self.work("hidden_" + tag, 73, [P, 2, NT, 256])
        hh = HH[:, :, :].rearrange("p k t -> p (k t)")
        hl = HL[:, :, :].rearrange("p k t -> p (k t)")
        state = {"act0": None, "act1": None, "hid0": None, "hid1": None, "mul0": None, "mul1": None}

        def gate_and_up(p, par):
            banks = (2 * par, 2 * par + 1)
            free = [self.bank_free[b] for b in banks]
            first = self.unit_product(("pair",) + (gate_up, p, 0), 0, 4, 512, 512, True, False, (self.XH, self.XL),
                                      [self.bank[b] for b in banks], after=(free, n if not self.looping else None))
            done = self.unit_product(("pair",) + (gate_up, p, 4), 4, 4, 512, 512, False, True, (self.XH, self.XL),
                                     [self.bank[b] for b in banks])
            mul = []
            for tok in range(NT):
                b = banks[tok]
                a = A(nc.scalar.activation, act[:, par, tok, :], self.bank[b][:, 0:256], ACT.Silu,
                      after=(done[tok], state[f"mul{par}"]))
                m = V(nc.vector.tensor_tensor, hid[:, par, tok, :], act[:, par, tok, :], self.bank[b][:, 256:512],
                      ALU.mult, after=(a, done[tok], state[f"hid{par}"]))
                self.bank_free[b] = [a, m]
                mul.append(m)
            state[f"mul{par}"] = mul
            return done

        def hidden_to_channels(at, par):
            b = 4 + par
            PE.wait(state[f"mul{par}"], self.bank_free[b])
            for c in range(2):
                for tok in range(NT):
                    m = nc.tensor.transpose(self.bank[b][:, (2 * c + tok) * P:(2 * c + tok + 1) * P],
                                            hid[:, par, tok, c * P:(c + 1) * P], self.ident[:, :])
            m.then_inc(PE.sem, 1)
            PE.count += 1
            done = Token(PE.sem, PE.count, PE.rate)
            state[f"hid{par}"] = done
            h = A(nc.scalar.activation, hh[:, at], self.bank[b][:, :], ACT.Copy, after=(done,))
            l = V(nc.vector.tensor_tensor, hl[:, at], self.bank[b][:, :], hh[:, at].bitcast(F32), ALU.subtract,
                  after=(done, h))
            self.bank_free[b] = [h, l]
            return [h, l]

        def two_pairs(i, state):
            pair = 1 if self.looping else i
            gate_and_up(2 * pair + 1, 1)
            hidden_to_channels(bass.ds(i * 1024, 512), 0)
            gate_and_up(2 * pair + 2, 0)
            state["last"] = hidden_to_channels(bass.ds(i * 1024 + 512, 512), 1)

        gate_and_up(0, 0)
        self.loop((NPAIR - 1) // 2, two_pairs, state)
        last = hidden_to_channels(bass.ds((NPAIR - 1) * 512, 512), 0)
        self.xt_free = self.used_token(len(self.units) - 1)
        banks = (0, 1, 2, 3)
        free = [self.bank_free[b] for b in banks]
        for u in range(NPAIR):
            done = self.unit_product(("part", down, 2 * u, 2, 0, D, D), 2 * u, 2, D, D, u == 0, u == NPAIR - 1,
                                     (HH, HL), [self.bank[b] for b in banks],
                                     after=(free, state["last"] if u < NPAIR - 1 else last))
        out = []
        for tok in range(NT):
            out.append([])
            for half in range(2):
                b, o = 2 * tok + half, self.x[:, tok, 512 * half:512 * half + 512]
                self.bank_free[b] = self.V(nc.vector.tensor_tensor, o, self.bank[b][:, :], o, ALU.add, after=(done[tok],))
                out[tok].append(self.bank_free[b])
        return out


def build(nc, t, out_dram, total_units):
    p = Program(nc, t)
    PE, V, A, G, SP = p.PE, p.V, p.A, p.G, p.SP
    p.total_units = total_units
    weights = t["weights"]

    ring_at = nc.sbuf_base + (-nc.sbuf_base) % 64
    place = p.sb("ring_place", [P, RING * UNIT + 16])
    p.w_raw = nc.alloc_sbuf_tensor_at("w_raw", [P, RING, UNIT], F32, offset=ring_at)
    p.w_lo = nc.alloc_sbuf_tensor_at("w_lo", [P, RING, UNIT], F32R, offset=ring_at)
    p.w_hi = p.sb("w_hi", [P, RING, UNIT], F32R)
    p.x = p.sb("x", [P, NT, D])
    p.xn = p.sb("xn", [P, NT, D])
    p.XH = p.sb("x_channels_hi", [P, KT, S], F32R)
    p.XL = p.sb("x_channels_lo", [P, KT, S], F32R)
    p.gains = [p.sb(f"gain_{b}", [P, D]) for b in range(2)]
    p.ident = p.sb("ident", [P, P])
    p.minus_half = p.sb("minus_half", [P, 16])
    p.cols = p.sb("cols", [P, 64])
    p.rstd = p.sb("rstd", [P, 2])
    p.rstd2 = p.sb("rstd2", [P, 16])
    p.stats = p.sb("stats", [P, 4, 8])
    p.lamb = p.sb("lambda_", [P, 8])
    p.sb_masks = p.sb("triangle_masks", [P, 13, P], mybir.dt.bfloat16)
    p.head_of = p.sb("head_of", [P, RWB, RW_HEADS])
    p.head_rk = p.sb("head_r_k", [P, RWB, RW_HEADS])
    p.mid, p.omk, p.state_factor = p.sb("mid", [P, RWB * NT]), p.sb("one_less_k_a", [P, RWB]), p.sb("state_factor", [P, RWB])
    p.rk_rows, p.gn = p.sb("r_k_rows", [P, NT, RW_HEADS]), p.sb("group_norm", [P, 36])
    p.posi, p.posf, p.freq = p.sb("pos_int", [P, NT], I32), p.sb("pos", [P, NT]), p.sb("freq", [P, 16])
    p.cosr, p.sinr = p.sb("cos", [P, NT, 16]), p.sb("sin", [P, NT, 16])
    arena = nc.sbuf_base + (-nc.sbuf_base) % 64
    p.arena, p.arena_size = arena, nc.sbuf_usable_end - arena
    p.lbuf = p.work("logits", 88, [P, 2, 512])
    p.ebuf = p.work("exps", 92, [P, 3 * 512])[:, :]
    p.ptbuf = p.work("weights_t", 84, [P, 2 * 512])[:, :]
    p.bank = [nc.alloc_psum_tensor(f"bank{b}", [P, 512], F32)[:, :] for b in range(8)]
    p.xn_free = p.xt_free = p.x_free = p.bias_ready = None
    p.e_free, p.pt_free, p.l_free, p.stat_free = [None] * 4, [None] * 2, [None] * 2, [None] * 4
    p.rstd_free = p.gn_free = None

    def load_unit(u, slot, round_=None):
        if round_ is None:
            if u >= RING:
                nc.sync.wait_ge(p.used, u - RING + 1)
            src = weights[u]
        else:
            nc.sync.wait_ge(p.used, round_ * RING + slot + 1)
            src = weights[bass.ds((round_ + 1) * RING + slot, 1)].rearrange("a p n -> (a p) n")
        nc.sync.dma_start(p.w_raw[:, slot, :], src).then_inc(p.loaded[slot], 16)

    for u in range(RING):
        load_unit(u, u)
    with nc.sync.Fori(0, total_units // RING - 1) as i:
        for slot in range(RING):
            load_unit(None, slot, i)
    for u in range(total_units // RING * RING, total_units):
        load_unit(u, u % RING)

    io = [nc.alloc_semaphore(f"input_{n}") for n in range(8)]

    def row_major(name):
        return t[name].rearrange("(t p) d -> p t d", p=P)

    nc.scalar.dma_start(p.x[:, :, :], row_major("x")).then_inc(io[0], 16)
    x_ready = Token(io[0], 16)
    mem1 = p.work("mem_rows", 82, [P, NT, D])
    nc.scalar.dma_start(mem1[:, :, :], row_major("mem")).then_inc(io[1], 16)
    mem1_ready = Token(io[1], 16)
    gain_mix = p.load_gain("mix_norm_g")
    gain_mem = p.load_gain("mem_norm_g")

    def identity(m, rows):
        z = G(nc.gpsimd.memset, m, 0.0)
        return G(nc.gpsimd.affine_select, out=m, in_=m, compare_op=ALU.not_equal, fill=1.0, base=0,
                 pattern=[[-1, P]], channel_multiplier=1, after=(z,))

    ident_ready = identity(p.ident[:, :], P)
    half_ready = G(nc.gpsimd.memset, p.minus_half[:, :], -0.5)
    PE.wait(ident_ready)

    wide_masks = p.work("wide_masks", 64, [P, 13, P])
    for dst, name in ((wide_masks[:, :, :], "triangle_masks"), (p.head_of[:, :, :], "head_of")):
        nc.scalar.dma_start(dst, t[name]).then_inc(io[7], 16)
    nc.scalar.dma_start(p.freq[:, :], t["inv_freq"].to_broadcast((P, 16))).then_inc(io[7], 16)
    nc.scalar.dma_start(p.posi[:, :], t["positions_2"].rearrange("a (t p) -> p (a t)", p=P),
                        allow_slow_non_contiguous=True).then_inc(io[7], 16)
    const_ready = pos_ready = Token(io[7], 64)
    masks_ready = V(nc.vector.tensor_copy, p.sb_masks[:, :, :], wide_masks[:, :, :], after=(const_ready,))

    for u in range(AHEAD):
        p.split(u)
    p.n_split = AHEAD

    rows = p.work("vector_rows", 58, [P, P])
    col_of, n_rows, loads = {}, 0, 0
    for name, width in (("a_shift_mu_2", SHB * P), ("a_decay_bias_2", RW), ("a_aaa_bias_2", RW), ("a_k_k_2", RW),
                        ("a_k_a_2", RW), ("a_r_k_2", RW)):
        n = width // P
        nc.scalar.dma_start(rows[n_rows:n_rows + n, :], t[name].rearrange("a (n p) -> (a n) p", p=P)).then_inc(io[2], 16)
        col_of[name] = n_rows
        n_rows += n
        loads += 16
    PE.wait(Token(io[2], loads))
    cols_t = PE(nc.tensor.transpose, p.bank[7][:, 0:n_rows], rows[0:n_rows, :], p.ident[0:n_rows, 0:n_rows])
    cols_ready = V(nc.vector.tensor_copy, p.cols[:, 0:n_rows], p.bank[7][:, 0:n_rows], after=(cols_t,))
    p.bank_free[7] = cols_ready

    def col(name, b):
        return p.cols[:, col_of[name] + b:col_of[name] + b + 1]

    NB, RL = 33, 384
    tab = p.work("bias_table", 59, [NB, A_HEADS + B_HEADS])
    hot = p.work("bias_one_hot", 60, [NB, RL])
    tneg = V(nc.vector.memset, tab[:, :], NEG)
    V.wait(tneg)
    nc.scalar.wait_ge(V.sem, V.count)
    nc.scalar.dma_start(tab[0:NB - 1, :], t["rel_bias_table"]).then_inc(io[3], 16)
    nc.scalar.dma_start(hot[:, :], t["bucket_one_hot"]).then_inc(io[3], 16)
    toep = nc.dram_tensor("bias_rows", (A_HEADS + B_HEADS, P, RL), F32, kind="Internal").ap()
    line = p.work("bias_lines", 40, [P, A_HEADS + B_HEADS, RL])
    tb_ready = [Token(io[3], 32)]
    for h in range(A_HEADS + B_HEADS):
        b = 4 + h % 4
        m = PE(nc.tensor.matmul, p.bank[b][:, 0:RL], tab[:, h:h + 1].to_broadcast((NB, P)), hot[:, :], start=True,
               stop=True, after=(tb_ready, p.bank_free[b]))
        c = p.copy(h, line[:, h, :], p.bank[b][:, 0:RL], (m,))
        p.bank_free[b] = c
        SPQ = nc.scalar
        A.wait(c)
        SPQ.dma_start(toep[h, :, :], line[:, h, :]).then_inc(io[4], 16)
    A.wait(Token(io[4], 16 * (A_HEADS + B_HEADS)))
    bias = p.work("bias", 64, [P, A_HEADS + B_HEADS, 384])
    A.wait(masks_ready)
    for tile, (lo, n) in enumerate(((P, P), (0, S))):
        skew = bass.AP(toep.tensor, P - 1 + lo, [[RL - 1, P], [P * RL, A_HEADS + B_HEADS], [1, n]])
        nc.scalar.dma_start(bias[:, :, tile * P:tile * P + n], skew).then_inc(io[5], 16)
    p.bias_ready = Token(io[5], 32)

    def at_tok(tile_, w=None):
        return lambda tok: tile_[:, tok, :] if w is None else tile_[:, tok, w[0]:w[1]]

    xt = p.norm_to_channels(p.x, D, gain_mix, EPS, p.XH, p.XL, [[x_ready, half_ready]] * NT)
    gain_lambda = p.load_gain("diff_lambda", 256)
    MH, ML = p.work("mem_channels_hi", 24, [P, KT, S], F32R), p.work("mem_channels_lo", 32, [P, KT, S], F32R)
    mt = p.norm_to_channels(mem1, D, gain_mem, EPS, MH, ML, [mem1_ready] * NT)
    gain_moba = p.load_gain("moba_out_g", 512)

    proj = p.work("proj", 40, [P, NT, 6 * 512])
    X = (p.XH, p.XL)

    lg, lg_ready, lgb = gain_lambda
    lv = lg.rearrange("p (a b d) -> p a b d", a=2, b=2)
    lprod = p.work("lambda_product", 84, [P, 2, 64])
    a1 = V(nc.vector.tensor_tensor, lprod[:, :, :], lv[:, :, 0, :], lv[:, :, 1, :], ALU.mult, after=(lg_ready,))
    p.gain_free[lgb] = a1
    a2 = V(nc.vector.tensor_reduce, out=p.lamb[:, 0:2], in_=lprod[:, :, :], axis=AX.X, op=ALU.add, after=(a1,))
    a3 = A(nc.scalar.activation, p.lamb[:, 2:4], p.lamb[:, 0:2], ACT.Exp, after=(a2,))
    a4 = V(nc.vector.tensor_tensor, p.lamb[:, 4:5], p.lamb[:, 3:4], p.lamb[:, 2:3], ALU.subtract, after=(a3,))
    lam_ready = V(nc.vector.tensor_scalar, p.lamb[:, 5:6], p.lamb[:, 4:5], -LAMBDA_INIT, None, ALU.add, after=(a4,))
    p.pt_free = [a2, a2]
    gain_sub = p.load_gain("diff_subln_g", P)

    def in_pair(g, banks, into):
        return p.job("w_in", X, xt, KT, 512 * g, 512, banks,
                     p.rows_of(at_tok(proj, (512 * g, 512 * g + 512)), banks, 512, into))

    def heads_to_channels(src_cols, dst, ready, banks=(4, 5, 6, 7), n_blocks=4, src=None, free=None):
        src = proj if src is None else src
        blocks = [(src[:, tok, src_cols + k * P:src_cols + (k + 1) * P], P) for k in range(n_blocks) for tok in range(NT)]
        turn = [0]

        def evacuate(g, bank, done):
            m = min(2, n_blocks - 2 * g)
            turn[0] += 1
            return p.copy(turn[0], dst[:, 2 * g:2 * g + m, :], bank[:, 0:m * S].rearrange("p (k t) -> p k t", k=m), (done, free))
        return p.transposes(blocks, ready, evacuate, banks)

    qa_rows, va_rows, b_rows = [], [], []
    p.run(in_pair(0, (0, 1), qa_rows), in_pair(1, (2, 3), qa_rows), in_pair(2, (0, 1), va_rows))
    qT, kT = p.work("qT", 8, [P, 4, S]), p.work("kT", 12, [P, 4, S])
    qk = heads_to_channels(0, qT, [qa_rows, mt]) + heads_to_channels(512, kT, [qa_rows, mt])
    p.pending = [in_pair(3, (0, 1), b_rows), in_pair(4, (0, 1), b_rows), in_pair(5, (0, 1), b_rows)]
    oa = p.attention(list(range(A_HEADS)), p.qk_pairs(qT, kT), (P, S), 0.125, lambda h: bias[:, h, :],
                     lambda h, j: proj[:, j, 1024 + 64 * h:1088 + 64 * h], 64, lambda i: p.xn[:, :, 64 * i:64 * i + 64],
                     [qk, va_rows], "a", out_free=p.xn_free, between=lambda i: p.fill(1))
    p.fill_rest()
    p.xt_free = p.used_token(len(p.units) - 1)

    r = p.inv_rms(lambda tok: p.xn[:, tok, 0:512], 512, EPS, [oa] * NT, p.rstd, junk=p.lbuf)
    p.l_free = [[V.last(), A.last()]] * 2
    oa = p.normalize(lambda tok: p.xn[:, tok, 0:512], lambda tok: p.xn[:, tok, 0:512], 512, gain_moba, p.rstd, [(r[tok], oa) for tok in range(NT)])
    gain_cross = p.load_gain("cross_norm_g")

    qk = heads_to_channels(1536, qT, [b_rows, oa]) + heads_to_channels(2048, kT, [b_rows, oa])
    cross_v = p.work("cross_v", 16, [P, NT, D])
    ck_rows, cv_rows = [], []
    M = (MH, ML)
    p.pending = [p.job("w_ck", M, mt, KT, 512 * g, 512, (0, 1),
                       p.rows_of(at_tok(proj, (512 * g, 512 * g + 512)), (0, 1), 512, ck_rows)) for g in range(2)]
    p.pending += [p.job("w_cv", M, mt, KT, 512 * g, 512, (0, 1),
                        p.rows_of(at_tok(cross_v, (512 * g, 512 * g + 512)), (0, 1), 512, cv_rows)) for g in range(2)]
    ob = p.attention(list(range(2 * B_HEADS)), p.qk_pairs(qT, kT), (P, S), 0.125, lambda h: bias[:, A_HEADS + h // 2, :],
                     lambda h, j: proj[:, j, 2560 + 64 * h:2688 + 64 * h], P,
                     lambda i: p.xn[:, :, 512 + P * i:640 + P * i], [qk], "b", between=lambda i: p.fill(2),
                     combine=(p.lamb[:, 5:6], lam_ready))
    p.fill_rest()
    sq = p.lbuf[:, :, :]
    o4 = p.xn[:, :, 512:1024]
    b1 = A(nc.scalar.activation, sq, o4, ACT.Square, scale=float(P) ** -0.5, after=(ob, p.l_free))
    p.l_free = [b1, b1]
    b2 = V(nc.vector.tensor_reduce, out=p.rstd2[:, 0:8], in_=sq.rearrange("p t (h d) -> p (t h) d", h=B_HEADS), axis=AX.X,
           op=ALU.add, after=(b1,))
    p.l_free = [b2, b2]
    b3 = p.power(p.rstd2[:, 0:8], EPS, b2)
    b4 = V(nc.vector.tensor_scalar, p.rstd2[:, 8:16], p.rstd2[:, 0:8], 1.0 - LAMBDA_INIT, None, ALU.mult, after=(b3,))
    g, g_ready, gb = gain_sub
    for tok in range(NT):
        o = o4[:, tok, :].rearrange("p (h d) -> p h d", h=B_HEADS)
        b5 = V(nc.vector.tensor_tensor, o, o, p.rstd2[:, 8 + 4 * tok:12 + 4 * tok].unsqueeze(2).to_broadcast((P, B_HEADS, P)),
               ALU.mult, after=(b4,))
        b5 = V(nc.vector.tensor_tensor, o, o, g.unsqueeze(1).to_broadcast((P, B_HEADS, P)), ALU.mult, after=(b5, g_ready))
    p.gain_free[gb] = b5
    gain_ffn = p.load_gain("ffn_norm_g")
    mixed = p.to_channels(lambda tok, k: p.xn[:, tok, k * P:(k + 1) * P], KT, p.XH, p.XL, (oa, b5), p.xt_free)
    p.xn_free = mixed
    x_done = p.project_residual("w_out", X, mixed)

    cross_kT = p.work("cross_kT", 8, [P, KT, S])
    ckT = heads_to_channels(0, cross_kT, ck_rows, n_blocks=8, free=PE.last())
    xt = p.norm_to_channels(p.x, D, gain_cross, EPS, p.XH, p.XL, x_done, p.xt_free)
    gain_mem2 = p.load_gain("mem_norm_g_2")
    cq, cqT = p.work("cross_q", 40, [P, NT, D]), p.work("cross_qT", 48, [P, KT, S])
    mem2 = p.work("mem2_rows", 56, [P, NT, D])
    A.wait(ckT, PE.last(), V.last())
    nc.scalar.dma_start(mem2[:, :, :], row_major("mem_2")).then_inc(io[6], 16)
    cq_rows = []
    for g in range(2):
        p.run(p.job("w_cq", X, [xt, ckT], KT, 512 * g, 512, (2 * g, 2 * g + 1),
                    p.rows_of(at_tok(cq, (512 * g, 512 * g + 512)), (2 * g, 2 * g + 1), 512, cq_rows)))
    p.xt_free = p.used_token(len(p.units) - 1)
    m2 = p.norm_to_channels(mem2, D, gain_mem2, EPS, MH, ML, [Token(io[6], 16)] * NT)
    qT2 = heads_to_channels(0, cqT, cq_rows, n_blocks=8, src=cq)

    mem_kT = [p.work(f"mem_kT_{n}", 4 * n, [P, 2, S]) for n in range(2)]
    mem_v = [p.work(f"mem_v_{n}", 4 * n + 2, [P, NT, S]) for n in range(2)]
    mk_rows = [p.work(f"mem_k_rows_{n}", 64 + 2 * n, [P, NT, S]) for n in range(2)]
    mem_ready = [[], []]

    def mem_kv(n, name):
        def evacuate(done):
            for tok in range(NT):
                a = A(nc.scalar.activation, mk_rows[n][:, tok, :], p.bank[tok][:, 0:256], ACT.Copy, after=(done[tok],))
                v = V(nc.vector.tensor_copy, mem_v[n][:, tok, :], p.bank[tok][:, 256:512], after=(done[tok], a))
                p.bank_free[tok] = [a, v]
                mem_ready[n] += [a, v]
        return p.job(name, M, m2, KT, 0, 512, (0, 1), evacuate)

    p.pending = [mem_kv(0, "a_mem_kv_2"), mem_kv(1, "b_mem_kv_2")]

    def qk_cross(h, bank, spans, off):
        for tok in range(NT):
            for k in range(2):
                m = nc.tensor.matmul(bank[:, off[tok]:off[tok] + S], cqT[:, 2 * h + k, tok * P:(tok + 1) * P],
                                     cross_kT[:, 2 * h + k, :], start=k == 0, stop=k == 1)
        m.then_inc(PE.sem, 1)
        PE.count += 1
        return Token(PE.sem, PE.count)

    oc = p.attention(list(range(MEM_HEADS)), qk_cross, (S, S), 0.0625, None,
                     lambda h, j: cross_v[:, j, 256 * h:256 * h + 256], 256, lambda i: p.xn[:, :, 256 * i:256 * i + 256],
                     [qT2, ckT, cv_rows], "c", out_free=p.xn_free, between=lambda i: p.fill(1))
    p.fill_rest()
    xt = p.to_channels(lambda tok, k: p.xn[:, tok, k * P:(k + 1) * P], KT, p.XH, p.XL, oc, p.xt_free)
    p.xn_free = xt
    for n in range(2):
        mem_ready[n] += heads_to_channels(0, mem_kT[n], mem_ready[n], n_blocks=2, src=mk_rows[n])
    x_done = p.project_residual("w_co", X, xt)

    x_done = p.feed_forward(("w_gate", "w_up"), "w_down", gain_ffn, x_done)
    gain_final, gain_n1 = p.load_gain("final_norm_g"), p.load_gain("a_norm1_g_2")
    r = p.inv_rms(lambda tok: p.x[:, tok, :], D, EPS, x_done, p.rstd)
    x_done = p.normalize(lambda tok: p.x[:, tok, :], lambda tok: p.x[:, tok, :], D, gain_final, p.rstd, r)

    n1 = p.norm_to_channels(p.x, D, gain_n1, EPS, p.XH, p.XL, x_done, p.xt_free)
    gain_lnx_g, gain_lnx_b = p.load_gain("a_lnx_g_2", RW), p.load_gain("a_lnx_b_2", RW)
    proj2 = p.work("proj2", 8, [P, NT, 2816])
    raw = p.work("raw_channels", 30, [P, SHB, S + 1])
    sh = p.work("shifted", 50.25, [P, SHB, S])
    qmT = p.work("memory_queries", 23, [P, 2, S])
    raw0 = G(nc.gpsimd.memset, raw[:, :, 0:1], 0.0, after=(PE.last(), V.last(), A.last()))
    shifted = [None] * SHB
    qm_ready = []

    def shift_columns(g, rows):
        blocks = list(range(4 * g, min(4 * g + 4, 22)))

        def evacuate(n, bank, done):
            b0 = blocks[2 * n]
            view = bank[:, :].rearrange("p (k t) -> p k t", k=2)
            if b0 >= SHB:
                t = A(nc.scalar.activation, qmT[:, :, :], view, ACT.Copy, after=(done,))
                qm_ready.append(t)
                return t
            t = A(nc.scalar.activation, raw[:, b0:b0 + 2, 1:S + 1], view, ACT.Copy, after=(done,))
            d = V(nc.vector.tensor_tensor, sh[:, b0:b0 + 2, :], raw[:, b0:b0 + 2, 0:S], raw[:, b0:b0 + 2, 1:S + 1],
                  ALU.subtract, after=(t, raw0))
            for b in (b0, b0 + 1):
                shifted[b] = V(nc.vector.scalar_tensor_tensor, out=sh[:, b, :], in0=sh[:, b, :], scalar=col("a_shift_mu_2", b),
                               in1=raw[:, b, 1:S + 1], op0=ALU.mult, op1=ALU.add, after=(d, cols_ready))
            return t
        p.transposes([(proj2[:, tok, b * P:(b + 1) * P], P) for b in blocks for tok in range(NT)], rows, evacuate)

    last_rows = None
    for g in range(6):
        rows, width = [], 512 if g < 5 else 256
        banks = (2 * (g % 2), 2 * (g % 2) + 1)
        p.run(p.job("a_w_in_2", X, n1, KT, 512 * g, width, banks,
                    p.rows_of(at_tok(proj2, (512 * g, 512 * g + width)), banks, width, rows)))
        if g:
            shift_columns(g - 1, last_rows)
        last_rows = rows
    shift_columns(5, last_rows)
    p.xt_free = p.used_token(len(p.units) - 1)

    decay_up = p.work("decay_up", 8, [64, RW])
    aaa_up = p.work("aaa_up", 11, [P, RW])
    gate_up = p.work("gate_up", 14, [P, RW])
    lora = nc.alloc_semaphore("lora_weights")
    G.wait(PE.last(), V.last(), A.last())
    nc.gpsimd.dma_start(decay_up[:, :], t["a_decay_up_2"]).then_inc(lora, 16)
    nc.gpsimd.dma_start(aaa_up[64:P, :], t["a_aaa_up_2"]).then_inc(lora, 16)
    nc.gpsimd.dma_start(gate_up[:, :], t["a_gate_up_2"]).then_inc(lora, 16)
    lora_ready = Token(lora, 48)
    head_of_t = p.work("head_of_t", 29, [RW_HEADS, RW])
    nc.gpsimd.dma_start(head_of_t[:, :], t["head_of_t"]).then_inc(lora, 16)
    lora_ready = Token(lora, 64)

    def memory_attention(n, qT_, ready, tag):
        return p.attention(list(range(MEM_HEADS)), p.qk_pairs(qT_, mem_kT[n]), (S, S), 0.125, None,
                           lambda h, j: mem_v[n][:, j, 64 * h:64 * h + 64], 64,
                           lambda i: p.xn[:, :, RW + 64 * i:RW + 64 * i + 64], [ready, mem_ready[n]], tag, out_free=p.xn_free)

    ma = memory_attention(0, qmT, qm_ready, "m0")
    after_ma = [PE.last(), V.last(), A.last()]

    masks = p.sb_masks
    rB, kB, vB = (sh[:, RWB * n:RWB * (n + 1), :] for n in range(3))
    td = A(nc.scalar.activation, sh[0:64, 18, :], sh[0:64, 18, :], ACT.Tanh, after=(shifted[18],))
    sg = A(nc.scalar.activation, sh[:, 19, :], sh[:, 19, :], ACT.Sigmoid, after=(shifted[19],))
    sig = p.work("decay_sigmoid", 44, [P, RWB, S])
    lr = p.work("learning_rate", 38, [P, RWB, S])
    sig_t, lr_t = [], []
    raw_dead = [x for x in shifted]
    for b in range(RWB):
        for rows0, w, out, bias_name, bank, toks in ((0, decay_up, sig, "a_decay_bias_2", 4 + b % 2, sig_t),
                                                     (64, aaa_up, lr, "a_aaa_bias_2", 6 + b % 2, lr_t)):
            m = PE(nc.tensor.matmul, p.bank[bank][:, 0:S], w[rows0:rows0 + 64, b * P:(b + 1) * P], sh[rows0:rows0 + 64, 18, :],
                   start=True, stop=True, after=(lora_ready, td, shifted[18], p.bank_free[bank]))
            a = A(nc.scalar.activation, out[:, b, :], p.bank[bank][:, 0:S], ACT.Sigmoid, bias=col(bias_name, b),
                  after=(m, raw_dead, cols_ready))
            p.bank_free[bank] = a
            toks.append(a)
    gate = p.work("gate", 17, [P, NT, RW])
    gate_t = []
    for tok in range(NT):
        for j, (c, w) in enumerate(((0, 512), (512, 256))):
            b = 2 * tok + j
            m = PE(nc.tensor.matmul, p.bank[b][:, 0:w], sh[:, 19, tok * P:(tok + 1) * P], gate_up[:, c:c + w], start=True,
                   stop=True, after=(lora_ready, sg, p.bank_free[b]))
            a = A(nc.scalar.activation, gate[:, tok, c:c + w], p.bank[b][:, 0:w], ACT.Copy, after=(m,))
            p.bank_free[b] = a
            gate_t.append(a)

    v_rows = p.work("v_rows", 23, [P, NT, RW])
    td_used = PE.last()

    def rows_back(src, dst, blocks_of, ready, free=None, banks=(4, 5, 6, 7)):
        def evacuate(n, bank, done):
            w = min(4, RWB - 4 * n) * P
            return p.copy(n, dst[:, 512 * n:512 * n + w], bank[:, 0:w], (done, free))
        return p.transposes([(blocks_of(b), P) for b in range(RWB)], ready, evacuate, banks)

    v_t = []
    for tok in range(NT):
        v_t += rows_back(None, v_rows[:, tok, :], lambda b: vB[:, b, tok * P:(tok + 1) * P], shifted[12:18])

    cs = p.work("cumulated", 70.5, [P, RWB, NT, P + 1])
    ones_c = p.work("ones_row", 95, [P, P])
    mid = p.mid
    cs0 = G(nc.gpsimd.memset, cs[:, :, :, 0:1], 0.0, after=after_ma)
    on = G(nc.gpsimd.memset, ones_c[:, :], 1.0, after=after_ma)
    scans = [V(nc.vector.tensor_tensor_scan, out=cs[:, b, c, 1:P + 1], data0=ones_c[:, :], data1=sig[:, b, c * P:(c + 1) * P],
               initial=0.0, op0=ALU.mult, op1=ALU.add, after=(sig_t[b], on, after_ma)) for b in range(RWB) for c in range(NT)]
    csf = cs[:, :, :, :].rearrange("p b c t -> p (b c) t")
    md = V(nc.vector.tensor_copy, mid[:, :], csf[:, :, 64:65].rearrange("p n o -> p (n o)"), after=(scans,))
    cm = V(nc.vector.tensor_tensor, csf, csf, mid[:, :].unsqueeze(2).to_broadcast((P, RWB * NT, P + 1)), ALU.subtract,
           after=(md, cs0))
    down_ = p.work("decay_down", 76.625, [P, RWB, NT, P + 1])
    up_ = p.work("decay_up_exp", 82.75, [P, RWB, NT, P + 1])
    e1 = A(nc.scalar.activation, down_[:, :, :, :], cs[:, :, :, :], ACT.Exp, scale=-KAPPA, after=(cm, after_ma))
    e2 = A(nc.scalar.activation, up_[:, :, :, :], cs[:, :, :, :], ACT.Exp, scale=KAPPA, after=(cm, after_ma))

    def per_channel(name):
        return p.cols[:, col_of[name]:col_of[name] + RWB].unsqueeze(2).to_broadcast((P, RWB, S))

    kk = p.work("removal_key", 32, [P, RWB, S])
    sqk = p.work("removal_key_squares", 88.875, [P, RWB, S])
    k1 = V(nc.vector.tensor_tensor, kk[:, :, :], kB, per_channel("a_k_k_2"), ALU.mult, after=(shifted,))
    k2 = A(nc.scalar.activation, sqk[:, :, :], kk[:, :, :], ACT.Square, after=(k1, after_ma))
    for b in range(RWB):
        PE.wait(k2, p.bank_free[0], const_ready)
        m = nc.tensor.matmul(p.bank[0][0:RW_HEADS, 0:S], p.head_of[:, b, :], sqk[:, b, :], start=b == 0, stop=b == RWB - 1)
    m.then_inc(PE.sem, 1)
    PE.count += 1
    nrm = p.work("inverse_norms", 96, [RW_HEADS, S])
    k3 = V(nc.vector.tensor_scalar, nrm[:, :], p.bank[0][0:RW_HEADS, 0:S], 1e-24, None, ALU.max, after=(PE.last(),))
    p.bank_free[0] = k3
    k4 = A(nc.scalar.activation, nrm[:, :], nrm[:, :], ACT.Sqrt, after=(k3,))
    k4 = V(nc.vector.reciprocal, nrm[:, :], nrm[:, :], after=(k4,))
    kkn = []
    for n in range(3):
        b = 1 + n
        PE.wait(k4, p.bank_free[b])
        for j in range(2):
            m = nc.tensor.matmul(p.bank[b][:, j * S:(j + 1) * S], head_of_t[:, (2 * n + j) * P:(2 * n + j + 1) * P], nrm[:, :],
                                 start=True, stop=True)
        m.then_inc(PE.sem, 1)
        PE.count += 1
        k = kk[:, 2 * n:2 * n + 2, :].rearrange("p k t -> p (k t)")
        o = V(nc.vector.scalar_tensor_tensor, out=k, in0=k, scalar=-1.0, in1=p.bank[b][:, :], op0=ALU.mult, op1=ALU.mult,
              after=(PE.last(), k2))
        p.bank_free[b] = o
        kkn.append(o)

    omk = V(nc.vector.tensor_scalar, p.omk[:, :], p.cols[:, col_of["a_k_a_2"]:col_of["a_k_a_2"] + RWB], -1.0, 1.0, ALU.mult,
            ALU.add, after=(cols_ready,))
    fac = p.work("key_factor", 88.875, [P, RWB, S])
    kf = [V(nc.vector.tensor_scalar, fac[:, b, :], lr[:, b, :], col("a_k_a_2", b), p.omk[:, b:b + 1], ALU.mult, ALU.add,
            after=(lr_t[b], omk, kkn)) for b in range(RWB)]
    kn = V(nc.vector.tensor_tensor, kB, kB, fac[:, :, :], ALU.mult, after=(kf, k1))

    rk = p.work("r_k", 88.875, [P, RWB, S])
    r1 = V(nc.vector.tensor_tensor, rk[:, :, :], rB, kB, ALU.mult, after=(kn, shifted[0:6]))
    rcol = V(nc.vector.tensor_tensor, p.head_rk[:, :, :], p.head_of[:, :, :],
             p.cols[:, col_of["a_r_k_2"]:col_of["a_r_k_2"] + RWB].unsqueeze(2).to_broadcast((P, RWB, RW_HEADS)), ALU.mult,
             after=(cols_ready, const_ready))
    for c in range(NT):
        PE.wait(r1, rcol, p.bank_free[0])
        for b in range(RWB):
            m = nc.tensor.matmul(p.bank[0][:, c * 16:c * 16 + RW_HEADS], rk[:, b, c * P:(c + 1) * P], p.head_rk[:, b, :],
                                 start=b == 0, stop=b == RWB - 1)
    m.then_inc(PE.sem, 1)
    PE.count += 1
    rk_t = V(nc.vector.tensor_copy, p.rk_rows[:, :, :], p.bank[0][:, 0:32].rearrange("p (c h) -> p c h", c=2)[:, :, 0:RW_HEADS],
             after=(PE.last(),))
    p.bank_free[0] = rk_t
    rk_read = PE.last()

    ar = p.work("a_and_r", 62.5, [P, RWB, NT, 2, P])
    o1 = [V(nc.vector.tensor_tensor, ar[:, b, :, 0, :], kk[:, b, :].rearrange("p (c t) -> p c t", c=2),
            down_[:, b, :, 0:P], ALU.mult, after=(e1, e2, kkn, rk_read, v_t, td_used)) for b in range(RWB)]
    o2 = [V(nc.vector.tensor_tensor, ar[:, b, :, 1, :], rB[:, b, :].rearrange("p (c t) -> p c t", c=2),
            down_[:, b, :, 1:P + 1], ALU.mult, after=(e1, e2, r1, rk_read, v_t, td_used)) for b in range(RWB)]
    b1 = V(nc.vector.scalar_tensor_tensor, out=lr[:, :, :], in0=kk[:, :, :], scalar=-1.0, in1=lr[:, :, :], op0=ALU.mult,
           op1=ALU.mult, after=(kf,))
    bt, kt = kk, lr
    o3 = [V(nc.vector.tensor_tensor, bt[:, b, :].rearrange("p (c t) -> p c t", c=2),
            lr[:, b, :].rearrange("p (c t) -> p c t", c=2), up_[:, b, :, 1:P + 1], ALU.mult, after=(e2, b1, o1)) for b in range(RWB)]
    o4_ = [V(nc.vector.tensor_tensor, kt[:, b, :].rearrange("p (c t) -> p c t", c=2),
             kB[:, b, :].rearrange("p (c t) -> p c t", c=2), up_[:, b, :, 1:P + 1], ALU.mult, after=(e2, o3, r1)) for b in range(RWB)]
    sf = V(nc.vector.tensor_tensor, p.state_factor[:, :], down_[:, :, 0, P:P + 1].rearrange("p b o -> p (b o)"),
           up_[:, :, 1, 0:1].rearrange("p b o -> p (b o)"), ALU.mult, after=(e1, e2))

    bt_rows, kt_rows = p.work("b_rows", 8, [P, RW]), p.work("k_rows", 11, [P, RW])
    bk_t = rows_back(None, bt_rows[:, :], lambda b: bt[:, b, 0:P], o3, free=[PE.last()])
    bk_t += rows_back(None, kt_rows[:, :], lambda b: kt[:, b, 0:P], o4_, free=[PE.last()])

    y = p.work("y", 76.625, [P, NT, RW])
    state = p.work("state", 82.75, [P, RWB, 64])
    dead = [o1, o2, o3, o4_, sf, bk_t]
    sets = []
    for n in range(2):
        at = ((44, 52, 54, 56, 58), (89, 60, 14, 29.5, 74.5))[n]
        sets.append(dict(
            lt=p.work(f"upper_{n}", at[0], [P, 4, 4, P]), lab=p.work(f"lab_{n}", at[1], [P, 4, P]),
            x=p.work(f"inverse_{n}", at[2], [P, 4, P]), xt=p.work(f"inverse_t_{n}", at[3], [P, 4, P]),
            w=p.work(f"step_{n}", at[4], [P, 4, P]),
            r=p.work(f"rhs_{n}", 84.5 + 2 * n, [P, 4, 64]), u=p.work(f"u_{n}", 85.5 + 2 * n, [P, 4, 64]), n=n, free=dead))
    state_t = [None] * RWB

    def mask(i):
        return masks[:, i, :].unsqueeze(1).to_broadcast((P, 4, P))

    def counted(m):
        m.then_inc(PE.sem, 1)
        PE.count += 1
        return PE.last()

    def triangles(q, c, g):
        base = 4 * q["n"]
        done = []
        for i in range(4):
            h = 4 * g + i
            par, blk, b = 64 * (h % 2), h // 2, base + h % 2
            rhs = ar[par:par + 64, blk, c, :, :].rearrange("p a t -> p (a t)")
            PE.wait(dead, p.bank_free[b])
            for j, lhs in enumerate((bt, kt)):
                m = nc.tensor.matmul(p.bank[b][:, 256 * j:256 * j + 256], lhs[par:par + 64, blk, c * P:(c + 1) * P], rhs,
                                     start=True, stop=True)
            m = counted(m)
            v = V(nc.vector.tensor_tensor, q["lt"][:, i, :, :], p.bank[b][:, :].rearrange("p (k t) -> p k t", k=4),
                  masks[:, 0:4, :], ALU.mult, after=(m, q["free"], masks_ready))
            p.bank_free[b] = v
            done.append(v)
        for par in range(2):
            b = base + 2 + par
            PE.wait(p.bank_free[b])
            for j in range(2):
                blk, r0 = 2 * g + j, 64 * par
                m = nc.tensor.matmul(p.bank[b][:, j * P:(j + 1) * P], ar[r0:r0 + 64, blk, c, 0, :],
                                     bt[r0:r0 + 64, blk, c * P:(c + 1) * P], start=True, stop=True)
            m = counted(m)
            v = V(nc.vector.tensor_tensor, q["lab"][:, par::2, :], p.bank[b][:, 0:256].rearrange("p (k t) -> p k t", k=2),
                  masks[:, 4:5, :].to_broadcast((P, 2, P)), ALU.mult, after=(m, q["free"]))
            p.bank_free[b] = v
            done.append(v)
        q["tri"] = done
        ib = p.ident[:, :].unsqueeze(1).to_broadcast((P, 4, P))
        a = V(nc.vector.tensor_tensor, q["x"][:, :, :], q["lab"][:, :, :], mask(5), ALU.mult, after=done)
        b_ = V(nc.vector.tensor_tensor, q["xt"][:, :, :], q["lt"][:, :, 0, :], mask(12), ALU.mult, after=done)
        a = V(nc.vector.tensor_tensor, q["x"][:, :, :], q["x"][:, :, :], ib, ALU.add, after=(a,))
        b_ = V(nc.vector.tensor_tensor, q["xt"][:, :, :], q["xt"][:, :, :], ib, ALU.add, after=(b_,))
        q["x_t"], q["xt_t"] = a, b_

    def double_first(q, level):
        b = 4 * q["n"]
        PE.wait(q["x_t"], q["tri"], p.bank_free[b])
        for i in range(4):
            m = nc.tensor.matmul(p.bank[b][:, i * P:(i + 1) * P], q["lt"][:, i, 0, :], q["x"][:, i, :], start=True, stop=True)
        m = counted(m)
        q["w_t"] = V(nc.vector.tensor_tensor, q["w"][:, :, :], p.bank[b][:, :].rearrange("p (k t) -> p k t", k=4),
                     mask(5 + level), ALU.mult, after=(m, q["x_t"], q["xt_t"]))
        p.bank_free[b] = q["w_t"]

    def double_second(q, level):
        b = 4 * q["n"] + 1
        last = level == 6
        PE.wait(q["w_t"], q["xt_t"], p.bank_free[b], p.bank_free[b + 1])
        if not last:
            for i in range(4):
                m = nc.tensor.matmul(p.bank[b][:, i * P:(i + 1) * P], q["xt"][:, i, :], q["w"][:, i, :], start=True, stop=True)
            m1 = counted(m)
        for i in range(4):
            m = nc.tensor.matmul(p.bank[b + 1][:, i * P:(i + 1) * P], q["w"][:, i, :], q["xt"][:, i, :], start=True, stop=True)
        m2 = counted(m)
        if not last:
            q["x_t"] = V(nc.vector.tensor_tensor, q["x"][:, :, :], p.bank[b][:, :].rearrange("p (k t) -> p k t", k=4),
                         q["x"][:, :, :], ALU.add, after=(m1,))
            p.bank_free[b] = q["x_t"]
        q["xt_t"] = V(nc.vector.tensor_tensor, q["xt"][:, :, :], p.bank[b + 1][:, :].rearrange("p (k t) -> p k t", k=4),
                      q["xt"][:, :, :], ALU.add, after=(m2,))
        p.bank_free[b + 1] = q["xt_t"]

    def by_parity(tile_, par, n=2):
        return tile_[:, par::2, :]

    def solve(q, c, g):
        base = 4 * q["n"]
        R, U, lt = q["r"], q["u"], q["lt"]
        rt = []
        for par in range(2):
            b = base + par
            PE.wait(q["tri"], v_t, p.bank_free[b], state_t if c else None)
            for j in range(2):
                i, h, blk = 2 * j + par, 4 * g + 2 * j + par, 2 * g + j
                o = p.bank[b][:, j * 64:j * 64 + 64]
                m = nc.tensor.matmul(o, lt[:, i, 2, :], v_rows[:, c, 64 * h:64 * h + 64], start=True, stop=c == 0)
                if c:
                    m = nc.tensor.matmul(o, ar[64 * par:64 * par + 64, blk, c, 0, :], state[64 * par:64 * par + 64, blk, :],
                                         start=False, stop=True)
            m = counted(m)
            r_ = A(nc.scalar.activation, by_parity(R, par), p.bank[b][:, 0:P].rearrange("p (k t) -> p k t", k=2), ACT.Copy,
                   after=(m, q["free"]))
            p.bank_free[b] = r_
            rt.append(r_)
        b = base + 2
        PE.wait(rt, q["xt_t"], p.bank_free[b])
        for i in range(4):
            m = nc.tensor.matmul(p.bank[b][:, i * 64:i * 64 + 64], q["xt"][:, i, :], R[:, i, :], start=True, stop=True)
        m = counted(m)
        ut = A(nc.scalar.activation, U[:, :, :], p.bank[b][:, 0:256].rearrange("p (k t) -> p k t", k=4), ACT.Copy,
               after=(m, q["free"]))
        p.bank_free[b] = ut
        if c == 0:
            b = base + 3
            PE.wait(ut, bk_t, p.bank_free[b])
            for j in range(2):
                for par in range(2):
                    i, h = 2 * j + par, 4 * g + 2 * j + par
                    o = p.bank[b][64 * par:64 * par + 64, j * 64:j * 64 + 64]
                    nc.tensor.matmul(o, bt_rows[:, 64 * h:64 * h + 64], U[:, i, :], start=True, stop=False)
                    m = nc.tensor.matmul(o, kt_rows[:, 64 * h:64 * h + 64], v_rows[:, 0, 64 * h:64 * h + 64], start=False,
                                         stop=True)
            m = counted(m)
            s_ = V(nc.vector.tensor_tensor, state[:, 2 * g:2 * g + 2, :], p.bank[b][:, 0:P].rearrange("p (k t) -> p k t", k=2),
                   p.state_factor[:, 2 * g:2 * g + 2].unsqueeze(2).to_broadcast((P, 2, 64)), ALU.mult, after=(m, dead))
            p.bank_free[b] = s_
            state_t[2 * g] = state_t[2 * g + 1] = s_
        yt = []
        for par in range(2):
            b = base + par
            PE.wait(ut, p.bank_free[b])
            for j in range(2):
                i, h, blk = 2 * j + par, 4 * g + 2 * j + par, 2 * g + j
                o = p.bank[b][:, j * 64:j * 64 + 64]
                nc.tensor.matmul(o, lt[:, i, 1, :], U[:, i, :], start=True, stop=False)
                m = nc.tensor.matmul(o, lt[:, i, 3, :], v_rows[:, c, 64 * h:64 * h + 64], start=False, stop=c == 0)
                if c:
                    m = nc.tensor.matmul(o, ar[64 * par:64 * par + 64, blk, c, 1, :], state[64 * par:64 * par + 64, blk, :],
                                         start=False, stop=True)
            m = counted(m)
            dst = y[:, c, :].rearrange("p (h d) -> p h d", d=64)[:, 4 * g + par:4 * g + 4:2, :]
            y_ = A(nc.scalar.activation, dst, p.bank[b][:, 0:P].rearrange("p (k t) -> p k t", k=2), ACT.Copy, after=(m, dead))
            p.bank_free[b] = y_
            yt.append(y_)
        q["free"] = [PE.last(), V.last()]
        return yt

    lg_, lg_ready, lg_b = gain_lnx_g
    lb_, lb_ready, lb_b = gain_lnx_b

    def finish_rows(c, yt):
        yc = y[:, c, :].rearrange("p (h d) -> p h d", d=64)
        y2v = p.xn[:, c, 0:RW].rearrange("p (h d) -> p h d", d=64)
        st_ = p.gn[:, :]

        def wide(a):
            return a.unsqueeze(2).to_broadcast((P, RW_HEADS, 64))
        a = V(nc.vector.tensor_reduce, out=st_[:, 0:12], in_=yc, axis=AX.X, op=ALU.add, after=(yt, p.gn_free))
        a = V(nc.vector.tensor_scalar, st_[:, 12:24], st_[:, 0:12], 1.0 / 64, None, ALU.mult, after=(a,))
        a = V(nc.vector.tensor_tensor, yc, yc, wide(st_[:, 12:24]), ALU.subtract, after=(a,))
        s_ = A(nc.scalar.activation, y2v, yc, ACT.Square, scale=0.125, after=(a, p.gn_free, p.xn_free))
        s_ = V(nc.vector.tensor_reduce, out=st_[:, 24:36], in_=y2v, axis=AX.X, op=ALU.add, after=(s_,))
        s_ = p.power(st_[:, 24:36], LNX_EPS, s_)
        a = V(nc.vector.tensor_tensor, yc, yc, wide(st_[:, 24:36]), ALU.mult, after=(s_,))
        b_ = V(nc.vector.tensor_tensor, y2v, v_rows[:, c, :].rearrange("p (h d) -> p h d", d=64), wide(p.rk_rows[:, c, :]),
               ALU.mult, after=(s_, rk_t, v_t))
        a = V(nc.vector.tensor_tensor, y[:, c, :], y[:, c, :], lg_, ALU.mult, after=(a, lg_ready))
        b_ = V(nc.vector.tensor_tensor, p.xn[:, c, 0:RW], p.xn[:, c, 0:RW], lb_, ALU.add, after=(b_, lb_ready))
        a = V(nc.vector.tensor_tensor, y[:, c, :], y[:, c, :], p.xn[:, c, 0:RW], ALU.add, after=(a, b_))
        a = V(nc.vector.tensor_tensor, p.xn[:, c, 0:RW], y[:, c, :], gate[:, c, :], ALU.mult, after=(a, gate_t, p.xn_free))
        p.gn_free = a
        return a

    work_list = [(c, g) for c in range(NT) for g in range(3)]
    yts = {0: [], 1: []}
    rows_done = []
    for n in range(0, 6, 2):
        two = [(sets[0],) + work_list[n], (sets[1],) + work_list[n + 1]]
        for q, c, g in two:
            triangles(q, c, g)
        for level in range(1, 7):
            for q, c, g in two:
                double_first(q, level)
            for q, c, g in two:
                double_second(q, level)
        for q, c, g in two:
            yts[c] += solve(q, c, g)
        if n == 2:
            rows_done.append(finish_rows(0, yts[0]))
    rows_done.append(finish_rows(1, yts[1]))
    p.gain_free[lg_b] = p.gain_free[lb_b] = rows_done
    gain_n2 = p.load_gain("a_norm2_g_2")
    xt = p.to_channels(lambda tok, k: p.xn[:, tok, k * P:(k + 1) * P], KT, p.XH, p.XL, (rows_done, ma), p.xt_free)
    p.xn_free = xt
    x_done = p.project_residual("a_w_out_2", X, xt)
    x_done = p.feed_forward(("a_ffn_gu_2",), "a_ffn_down_2", gain_n2, x_done)

    gain_kv, gain_b1 = p.load_gain("kv_norm_g_2"), p.load_gain("b_norm1_g_2")
    KH, KL = p.work("kv_channels_hi", 8, [P, KT, S], F32R), p.work("kv_channels_lo", 16, [P, KT, S], F32R)
    r = p.inv_rms(lambda tok: p.x[:, tok, :], D, EPS, x_done, p.rstd)
    kv_n = p.normalize(lambda tok: p.x[:, tok, :], lambda tok: p.xn[:, tok, :], D, gain_kv, p.rstd, r)
    kv_x = p.to_channels(lambda tok, k: p.xn[:, tok, k * P:(k + 1) * P], KT, KH, KL, kv_n)
    b_n = p.normalize(lambda tok: p.x[:, tok, :], lambda tok: p.xn[:, tok, :], D, gain_b1, p.rstd, r, kv_x)
    b_x = p.to_channels(lambda tok, k: p.xn[:, tok, k * P:(k + 1) * P], KT, p.XH, p.XL, b_n, p.xt_free)
    p.xn_free = b_x
    gain_lat, gain_q = p.load_gain("kv_latent_g_2", 256), p.load_gain("b_q_norm_g_2", 512)

    rope = p.work("rope", 80, [P, 8, NT, 16])
    cosr, sinr = p.cosr, p.sinr
    angle, turns_, red = rope[:, 0, :, :], rope[:, 1, :, :], rope[:, 2, :, :]
    posf = V(nc.vector.tensor_copy, p.posf[:, :], p.posi[:, :], after=(pos_ready,))
    a = V(nc.vector.tensor_tensor, angle, p.posf[:, :].unsqueeze(2).to_broadcast((P, NT, 16)),
          p.freq[:, :].unsqueeze(1).to_broadcast((P, NT, 16)), ALU.mult, after=(posf, x_done))
    magic = 12582912.0
    b_ = V(nc.vector.tensor_scalar, turns_, angle, 1.0 / (2 * math.pi), magic, ALU.mult, ALU.add, after=(a,))
    b_ = V(nc.vector.tensor_scalar, turns_, turns_, magic, None, ALU.subtract, after=(b_,))
    parts = (6.28125, 0.0019350051879882812, 2 * math.pi - 6.28125 - 0.0019350051879882812)
    src = angle
    for part in parts:
        a = V(nc.vector.scalar_tensor_tensor, out=red, in0=turns_, scalar=-part, in1=src, op0=ALU.mult, op1=ALU.add, after=(a, b_))
        src = red
    pi = 3.1415925
    a = V(nc.vector.tensor_scalar, red, red, pi, -pi, ALU.min, ALU.max, after=(a,))
    sin_t = A(nc.scalar.activation, sinr[:, :, :], red, ACT.Sin, after=(a,))
    c_ = A(nc.scalar.activation, rope[:, 3, :, :], red, ACT.Abs, after=(a,))
    c_ = V(nc.vector.tensor_scalar, rope[:, 3, :, :], rope[:, 3, :, :], -1.0, math.pi / 2, ALU.mult, ALU.add, after=(c_,))
    cos_t = A(nc.scalar.activation, cosr[:, :, :], rope[:, 3, :, :], ACT.Sin, after=(c_,))

    ckr = p.work("latent_rows", 24, [P, NT, 288])
    bproj = p.work("b_proj", 27, [P, NT, 768])
    ckr_t, cq_t, qm_t = [], [], []
    p.run(p.job("kv_w_down_2", (KH, KL), kv_x, KT, 0, 288, (0, 1), p.rows_of(at_tok(ckr), (0, 1), 288, ckr_t)),
          p.job("b_w_in_2", X, b_x, KT, 0, 512, (2, 3), p.rows_of(at_tok(bproj, (0, 512)), (2, 3), 512, cq_t)),
          p.job("b_w_in_2", X, b_x, KT, 512, 256, (0, 1), p.rows_of(at_tok(bproj, (512, 768)), (0, 1), 256, qm_t)))
    LH, LL = p.work("latent_hi", 33, [P, 2, S], F32R), p.work("latent_lo", 35, [P, 2, S], F32R)
    QH, QL = p.work("q_latent_hi", 37, [P, 4, S], F32R), p.work("q_latent_lo", 41, [P, 4, S], F32R)
    lat = p.norm_to_channels(ckr, 256, gain_lat, EPS, LH, LL, [ckr_t] * NT)
    qlat = p.norm_to_channels(bproj, 512, gain_q, EPS, QH, QL, [cq_t] * NT)
    kv = p.work("kv", 8, [P, NT, 2 * RW])
    q = p.work("q", 45, [P, NT, MLA_HEADS * QK])
    kv_t, q_t = [], []
    kv_dead = p.used_token(len(p.units) - 1)

    def kv_rows(done, c0, bank_ids, width):
        A.wait(kv_dead)
        V.wait(kv_dead)
        p.rows_of(at_tok(kv, (c0, c0 + width)), bank_ids, width, kv_t)(done)
    p.run(p.job("kv_w_up_2", (LH, LL), lat, 2, 0, 1024, (0, 1, 2, 3), lambda d: kv_rows(d, 0, (0, 1, 2, 3), 1024)),
          p.job("kv_w_up_2", (LH, LL), lat, 2, 1024, 512, (0, 1), lambda d: kv_rows(d, 1024, (0, 1), 512)))
    for c0, w, banks in ((0, 512, (2, 3)), (512, 512, (0, 1)), (1024, 128, (2, 3))):
        p.run(p.job("b_q_up_2", (QH, QL), qlat, 4, c0, w, banks, p.rows_of(at_tok(q, (c0, c0 + w)), banks, w, q_t)))

    qmT1 = p.work("memory_queries_1", 54.5, [P, 2, S])
    qm1 = heads_to_channels(512, qmT1, qm_t, n_blocks=2, src=bproj)
    mb = memory_attention(1, qmT1, qm1, "m1")

    tmp = p.work("rotate", 57, [P, 4, MLA_HEADS, 16])

    def rotate(src, dst, tok, heads, ready, free):
        cb, sb_ = (x[:, tok, :].unsqueeze(1).to_broadcast((P, heads, 16)) for x in (cosr, sinr))
        t1, t2 = src[:, :, 0:16], src[:, :, 16:32]
        m = [V(nc.vector.tensor_tensor, tmp[:, i, 0:heads, :], x, w, ALU.mult, after=(ready, cos_t, sin_t, free))
             for i, (x, w) in enumerate(((t1, cb), (t2, sb_), (t2, cb), (t1, sb_)))]
        d1 = V(nc.vector.tensor_tensor, dst[:, :, 0:16], tmp[:, 0, 0:heads, :], tmp[:, 1, 0:heads, :], ALU.subtract, after=m)
        d2 = V(nc.vector.tensor_tensor, dst[:, :, 16:32], tmp[:, 2, 0:heads, :], tmp[:, 3, 0:heads, :], ALU.add, after=m)
        return [d1, d2]

    kcat = p.work("k_cat", 60, [P, NT, MLA_HEADS * QK])
    free = None
    q_rot, k_rot = [], []
    for tok in range(NT):
        qh = q[:, tok, :].rearrange("p (h d) -> p h d", d=QK)[:, :, 64:96]
        free = rotate(qh, qh, tok, MLA_HEADS, q_t, free)
        q_rot += free
        kr = ckr[:, tok, 256:288].unsqueeze(1)
        free = rotate(kr, kr, tok, 1, ckr_t, free)
        kc = kcat[:, tok, :].rearrange("p (h d) -> p h d", d=QK)
        k_rot.append(V(nc.vector.tensor_copy, kc[:, :, 64:96], kr.to_broadcast((P, MLA_HEADS, 32)), after=(free,)))
        k_rot.append(A(nc.scalar.activation, kc[:, :, 0:64], kv[:, tok, :].rearrange("p (h d) -> p h d", d=P)[:, :, 0:64],
                       ACT.Copy, after=(kv_t,)))
    q96, k96 = p.work("q_channels", 20, [QK, MLA_HEADS, S]), p.work("k_channels", 69.5, [QK, MLA_HEADS, S])

    def to_heads(src, dst, ready, free):
        blocks = [(src[:, tok, QK * h:QK * (h + 1)], QK) for h in range(MLA_HEADS) for tok in range(NT)]
        return p.transposes(blocks, ready, lambda n, bank, done: p.copy(
            n, dst[:, 2 * n:2 * n + 2, :], bank[0:QK, :].rearrange("p (k t) -> p k t", k=2), (done, free)))
    heads_t = to_heads(q, q96, q_rot, [k_rot, PE.last(), V.last(), A.last()])
    heads_t += to_heads(kcat, k96, k_rot, None)

    def qk_latent(h, bank, spans, off):
        for tok in range(NT):
            m = nc.tensor.matmul(bank[:, off[tok]:off[tok] + spans[tok]], q96[:, h, tok * P:(tok + 1) * P],
                                 k96[:, h, 0:spans[tok]], start=True, stop=True)
        return counted(m)

    causal = p.work("causal", 57, [P, 384])
    cz = G(nc.gpsimd.memset, causal[:, :], 0.0, after=(V.last(),))
    for c0, w, base_ in ((0, P, 0), (P, S, P)):
        cz = G(nc.gpsimd.affine_select, out=causal[:, c0:c0 + w], in_=causal[:, c0:c0 + w], compare_op=ALU.is_ge, fill=NEG,
               base=base_, pattern=[[-1, w]], channel_multiplier=1, after=(cz,))
    p.bias_ready = cz
    ol = p.attention(list(range(MLA_HEADS)), qk_latent, (P, S), float(QK) ** -0.5, lambda h: causal[:, :],
                     lambda h, j: kv[:, j, P * h + 64:P * h + 128], 64, lambda i: p.xn[:, :, 64 * i:64 * i + 64],
                     [heads_t], "l", out_free=p.xn_free)
    gain_n3 = p.load_gain("b_norm2_g_2")
    xt = p.to_channels(lambda tok, k: p.xn[:, tok, k * P:(k + 1) * P], KT, p.XH, p.XL, (ol, mb),
                       p.used_token(len(p.units) - 1))
    p.xn_free = xt
    x_done = p.project_residual("b_w_out_2", X, xt)
    x_done = p.feed_forward(("b_ffn_gu_2",), "b_ffn_down_2", gain_n3, x_done)
    gain_last = p.load_gain("final_norm_g_2")
    r = p.inv_rms(lambda tok: p.x[:, tok, :], D, EPS, x_done, p.rstd)
    x_done = p.normalize(lambda tok: p.x[:, tok, :], lambda tok: p.x[:, tok, :], D, gain_last, p.rstd, r)
    SP.wait(x_done)
    nc.sync.dma_start(out_dram.rearrange("(t p) d -> p t d", p=P), p.x[:, :, :]).then_inc(io[0], 16)
    nc.sync.wait_ge(io[0], 32)
    return p.units


STREAMED = ("w_in", "w_ck", "w_cv", "w_out", "w_cq", "a_mem_kv_2", "b_mem_kv_2", "w_co", "w_gate", "w_up", "w_down",
            "a_w_in_2", "a_w_out_2", "a_ffn_gu_2", "a_ffn_down_2", "kv_w_down_2", "kv_w_up_2", "b_w_in_2", "b_q_up_2",
            "b_w_out_2", "b_ffn_gu_2", "b_ffn_down_2")
VECTORS = ("mix_norm_g", "moba_out_g", "diff_lambda", "diff_subln_g", "cross_norm_g", "mem_norm_g", "ffn_norm_g",
           "final_norm_g", "mem_norm_g_2", "a_norm1_g_2", "a_lnx_g_2", "a_lnx_b_2", "a_norm2_g_2", "kv_norm_g_2",
           "kv_latent_g_2", "b_norm1_g_2", "b_q_norm_g_2", "b_norm2_g_2", "final_norm_g_2")
PLAIN = ("x", "mem", "mem_2", "positions_2", "rel_bias_table", "a_shift_mu_2", "a_decay_bias_2", "a_aaa_bias_2",
         "a_k_k_2", "a_k_a_2", "a_r_k_2", "a_decay_up_2", "a_aaa_up_2", "a_gate_up_2")


def bucket_one_hot():
    dist = 255 - np.arange(384)
    n = np.maximum(dist, 0)
    ratio = np.log(np.maximum(n, 16).astype(np.float32) / np.float32(16)) / np.float32(math.log(8))
    large = np.minimum(16 + (ratio * np.float32(16)).astype(np.int32), 31)
    bucket = np.where(n < 16, n, large)
    hot = (bucket[None, :] == np.arange(33)[:, None]) & (dist >= 0)[None, :]
    hot[32] = dist < 0
    return hot.astype(np.float32)


def triangle_masks():
    r, c = np.arange(P)[:, None], np.arange(P)[None, :]
    masks = [r < c, r <= c, r < c, r <= c, r > c]
    for level in range(7):
        size = 1 << level
        masks.append((r // (2 * size) == c // (2 * size)) & (r // size > c // size))
    masks.append(masks[5].T)
    return np.stack(masks, axis=1).astype(np.float32)


def constants():
    half = 16
    inv_freq = np.power(10000.0, -np.arange(half, dtype=np.float64) / half).astype(np.float32)
    head_of = (np.arange(RW)[:, None] // 64 == np.arange(RW_HEADS)[None, :]).astype(np.float32)
    return {"bucket_one_hot": bucket_one_hot(), "triangle_masks": triangle_masks(), "inv_freq": inv_freq[None, :],
            "head_of": np.ascontiguousarray(head_of.reshape(RWB, P, RW_HEADS).transpose(1, 0, 2)),
            "head_of_t": np.ascontiguousarray(head_of.T)}


def place_unit(unit, spec, arrays):
    if spec[0] == "pair":
        _, names, pair, k0 = spec
        if len(names) == 2:
            gate, up = arrays[names[0]][0], arrays[names[1]][0]
        else:
            gate, up = arrays[names[0]][0][:, :FF], arrays[names[0]][0][:, FF:]
        v = unit.reshape(P, 4, 2, 256)
        for j, w in enumerate((gate, up)):
            v[:, :, j, :] = w[k0 * P:(k0 + 4) * P, 256 * pair:256 * pair + 256].reshape(4, P, 256).transpose(1, 0, 2)
        return
    _, name, k0, nk, c0, width, pitch = spec
    w = arrays[name].reshape(-1, arrays[name].shape[-1])
    v = unit[:, 0:nk * pitch].reshape(P, nk, pitch)
    v[:, :, 0:width] = w[k0 * P:(k0 + nk) * P, c0:c0 + width].reshape(nk, P, width).transpose(1, 0, 2)


FEED_FORWARD_UNITS = 2 * NPAIR + NPAIR
FIRST_UNITS = 2 * (6 + 2) + 2 * (2 + 2 + 2 + 2) + FEED_FORWARD_UNITS
LAYER_A_UNITS = 2 + (2 * 5 + 1) + 4 + FEED_FORWARD_UNITS
LAYER_B_UNITS = 2 + 2 + (2 + 1) + (1 + 1) + 3 + 4 + FEED_FORWARD_UNITS
TOTAL_UNITS = FIRST_UNITS + LAYER_A_UNITS + LAYER_B_UNITS


def kernel(**inputs):
    import concourse.bacc as bacc
    from concourse.bass_utils import run_bass_kernel_spmd

    nc = bacc.Bacc("TRN2", target_bir_lowering=False, num_devices=1)
    host = {n: np.ascontiguousarray(inputs[n]) for n in PLAIN}
    host.update({n: np.ascontiguousarray(inputs[n]).reshape(1, -1) for n in VECTORS})
    host.update(constants())
    for n in ("x", "mem", "mem_2"):
        host[n] = host[n].reshape(S, D)
    for n in ("a_decay_up_2", "a_aaa_up_2", "a_gate_up_2"):
        host[n] = host[n].reshape(host[n].shape[-2:])
    host["a_r_k_2"] = host["a_r_k_2"].reshape(1, RW)
    host["weights"] = np.zeros((TOTAL_UNITS, P, UNIT), np.float32)
    t = {n: nc.dram_tensor("in_" + n, a.shape, mybir.dt.from_np(a.dtype), kind="ExternalInput").ap()
         for n, a in host.items()}
    out = nc.dram_tensor("out", (S, D), F32, kind="ExternalOutput").ap()
    units = build(nc, t, out, TOTAL_UNITS)
    assert len(units) == TOTAL_UNITS, len(units)
    arrays = {n: np.asarray(inputs[n]) for n in STREAMED}
    for u, spec in enumerate(units):
        place_unit(host["weights"][u], spec, arrays)
    r = run_bass_kernel_spmd(nc, [{"in_" + n: a for n, a in host.items()}], core_ids=[0])
    return r.results[0]["out"].reshape(1, S, D)
```

```python
import math

import numpy as np

import concourse.bass as bass
from concourse import mybir

F32 = mybir.dt.float32
F32R = mybir.dt.float32r
I32 = mybir.dt.int32
ACT = mybir.ActivationFunctionType
ALU = mybir.AluOpType
AX = mybir.AxisListType

P = 128
S = 256
NT = S // P
D = 1024
KT = D // P
FF = 2816
NPAIR = FF // 256
KB = 1024
NEG = -1e30
EPS = 1e-6
LNX_EPS = 64e-5
RING = 4
UNIT = 2048
AHEAD = 3
A_HEADS, B_HEADS, MEM_HEADS, RW_HEADS, MLA_HEADS = 8, 4, 4, 12, 12
RW = RW_HEADS * 64
RWB = RW // P
SHB = 20
QK = 96
KAPPA = math.exp(-0.5)
LAMBDA_INIT = 0.8 - 0.6 * math.exp(0.0)


class Token:

    def __init__(self, sem, value, rate=0):
        self.sem, self.value, self.rate = sem, value, rate


class Lane:

    def __init__(self, nc, engine, name):
        self.engine, self.sem = engine, nc.alloc_semaphore(name)
        self.count, self.rate, self.round = 0, 0, None
        self.waited = {}

    def wait(self, *tokens):
        for t in tokens:
            if t is None:
                continue
            if isinstance(t, (list, tuple)):
                self.wait(*t)
                continue
            key = (t.sem.name, t.rate)
            if self.waited.get(key, 0) >= t.value:
                continue
            self.waited[key] = t.value
            self.engine.wait_ge(t.sem, t.value if not t.rate else self.round * t.rate + t.value)

    def last(self):
        return Token(self.sem, self.count, self.rate)

    def quiet(self, instruction, *args, after=(), **kw):
        self.wait(after)
        return instruction(*args, **kw)

    def __call__(self, instruction, *args, after=(), **kw):
        self.wait(after)
        instruction(*args, **kw).then_inc(self.sem, 1)
        self.count += 1
        return Token(self.sem, self.count, self.rate)


class Program:
    def __init__(self, nc, t):
        self.nc, self.t = nc, t
        self.PE = Lane(nc, nc.tensor, "pe_done")
        self.V = Lane(nc, nc.vector, "dve_done")
        self.A = Lane(nc, nc.scalar, "act_done")
        self.G = Lane(nc, nc.gpsimd, "pool_done")
        self.SP = Lane(nc, nc.sync, "sp_done")
        self.lanes = (self.PE, self.V, self.A, self.G, self.SP)
        self.loaded = [nc.alloc_semaphore(f"weights_loaded_{s}") for s in range(RING)]
        self.split_done = nc.alloc_semaphore("weights_split")
        self.used = nc.alloc_semaphore("weights_used")
        self.units = []
        self.looping = False
        self.n_split = 0
        self.bank_free = [None] * 8
        self.arena_tensors = 0
        self.gain_free = [None, None]
        self.gain_turn = 0
        self.pending = []

    def sb(self, name, shape, dtype=F32):
        return self.nc.alloc_sbuf_tensor(name, shape, dtype)

    def work(self, name, kb, shape, dtype=F32):
        size = 4 * int(np.prod(shape[1:]))
        assert kb * KB + size <= self.arena_size, (name, kb * KB + size, self.arena_size)
        return self.nc.alloc_sbuf_tensor_at(name, shape, dtype, offset=int(self.arena + kb * KB))

    def ring_token(self, sem, value, rate):
        return Token(sem, value, rate if self.looping else 0)

    def used_token(self, u):
        return self.ring_token(self.used, u + 1, RING)

    def split(self, u):
        s = u % RING
        hi = self.A(self.nc.scalar.activation, self.w_hi[:, s, :], self.w_raw[:, s, :], ACT.Copy,
                    after=(self.ring_token(self.loaded[s], 16 * (u // RING + 1), 16),
                           self.used_token(u - RING) if u >= RING else None))
        self.V.quiet(self.nc.vector.tensor_tensor, self.w_lo[:, s, :], self.w_raw[:, s, :],
                     self.w_hi[:, s, :].bitcast(F32), ALU.subtract, after=(hi,)).then_inc(self.split_done, 1)

    def unit_product(self, spec, k0, nk, nc_, width, first, last, lhs, banks, after=()):
        u = len(self.units)
        self.units.append(spec)
        s = u % RING
        while self.n_split < u + AHEAD and (self.looping or self.n_split < self.total_units):
            self.split(self.n_split)
            self.n_split += 1
        pe, mm = self.PE, self.nc.tensor.matmul
        pe.wait(self.ring_token(self.split_done, u + 1, RING), after)
        segs = [(c, min(512, width - c)) for c in range(0, width, 512)]
        passes = [(k, n) for k in range(nk) for n in range(3)]
        order = ([(k, n, tok) for tok in range(NT) for k, n in passes] if last
                 else [(k, n, tok) for k, n in passes for tok in range(NT)])
        first_tok = None
        for k, n, tok in order:
            x, w = ((0, self.w_hi), (1, self.w_hi), (0, self.w_lo))[n]
            for c, cw in segs:
                o = banks[tok * len(segs) + c // 512]
                m = mm(o[:, 0:cw], lhs[x][:, k0 + k, tok * P:(tok + 1) * P],
                       w[:, s, k * nc_ + c:k * nc_ + c + cw],
                       start=first and k == 0 and n == 0, stop=last and k == nk - 1 and n == 2)
            if last and (k, n, tok) == (nk - 1, 2, 0):
                m.then_inc(pe.sem, 1)
                pe.count += 1
                first_tok = pe.last()
        m.then_inc(self.used, 1)
        return [first_tok, self.used_token(u)]

    def job(self, name, lhs, ready, nk, c0, width, bank_ids, evacuate):
        banks = [self.bank[b] for b in bank_ids]
        pitch = 256 if (width <= 256 and nk == KT) else 512 if width <= 512 else width
        per = min(nk, UNIT // pitch)
        for k in range(0, nk, per):
            n = min(per, nk - k)
            after = ([self.bank_free[b] for b in bank_ids], ready) if k == 0 else ()
            done = self.unit_product(("part", name, k, n, c0, width, pitch), k, n, pitch, width, k == 0, k + n == nk,
                                     lhs, banks, after=after)
            if k + n == nk:
                evacuate(done)
            yield

    def run(self, *jobs):
        for j in jobs:
            for _ in j:
                pass

    def fill(self, units):
        while units > 0 and self.pending:
            try:
                next(self.pending[0])
                units -= 1
            except StopIteration:
                self.pending.pop(0)

    def fill_rest(self):
        self.run(*self.pending)
        self.pending = []

    def rows_of(self, dst, bank_ids, width, into=None):
        def evacuate(done):
            out = []
            for tok in range(NT):
                segs = [(c, min(512, width - c)) for c in range(0, width, 512)]
                for j, (c, w) in enumerate(segs):
                    b = bank_ids[tok * len(segs) + j]
                    t = self.copy(tok, dst(tok)[:, c:c + w], self.bank[b][:, 0:w], (done[tok],))
                    self.bank_free[b] = t
                    out.append(t)
            if into is not None:
                into.extend(out)
        return evacuate

    def loop(self, rounds, body, state):
        before = [lane.count for lane in self.lanes]
        body(0, state)
        grown = [lane.count - b for lane, b in zip(self.lanes, before)]
        rate_of = {lane.sem.name: (lane, g, b) for lane, g, b in zip(self.lanes, grown, before)}
        rate_of[self.used.name] = (None, RING, 0)

        def moved(t, turns):
            if t is None:
                return None
            if isinstance(t, (list, tuple)):
                return [moved(x, turns) for x in t]
            lane, g, b = rate_of[t.sem.name]
            if turns is None:
                return Token(t.sem, t.value, g) if lane is None or t.value > b else t
            return Token(t.sem, t.value + turns * g if t.rate else t.value)

        units, splits = len(self.units), self.n_split
        counts = [lane.count for lane in self.lanes]
        for k in state:
            state[k] = moved(state[k], None)
        self.bank_free = moved(self.bank_free, None)
        self.looping = True
        kept = [dict(lane.waited) for lane in self.lanes]
        with self.nc.Fori(0, rounds - 1) as i:
            for lane, g in zip(self.lanes, grown):
                lane.rate, lane.round = g, i
            body(i + 1, state)
        self.looping = False
        turns = rounds - 2
        for lane, g, c, w in zip(self.lanes, grown, counts, kept):
            assert lane.count - c == g
            lane.count = c + (rounds - 1) * g
            lane.rate, lane.round = 0, None
            lane.waited = w
        for k in state:
            state[k] = moved(state[k], turns)
        self.bank_free = moved(self.bank_free, turns)
        round_units = self.units[units:]
        del self.units[units:]
        for n in range(rounds - 1):
            self.units += [spec[:2] + (spec[2] + 2 * n,) + spec[3:] for spec in round_units]
        self.n_split = splits + (rounds - 1) * RING

    def load_gain(self, name, width=D, parts=1):
        b = self.gain_turn % 2
        self.gain_turn += 1
        sem = self.nc.alloc_semaphore(f"gain_{self.gain_turn}")
        out = self.gains[b][:, 0:width]
        self.G.wait(self.gain_free[b])
        self.nc.gpsimd.dma_start(out, self.t[name].to_broadcast((P, width))).then_inc(sem, 16)
        return out, Token(sem, 16), b

    def inv_rms(self, src, width, eps, ready, out, junk=None):
        if junk is None:
            junk = self.xn
        result = []
        for tok in range(NT):
            a = self.A(self.nc.scalar.activation, junk[:, tok, 0:width], src(tok), ACT.Square,
                       scale=float(width) ** -0.5, accum_out=out[:, tok:tok + 1],
                       after=(ready[tok], self.xn_free, self.rstd_free))
            result.append(self.power(out[:, tok:tok + 1], eps, (a,)))
        return result

    def power(self, ms, eps, ready):
        t = self.G(self.nc.gpsimd.tensor_scalar, ms, ms, eps, None, ALU.add, after=(ready,))
        n = ms.shape[-1]
        return self.G(self.nc.gpsimd.tensor_tensor, ms, ms, self.minus_half[0:ms.shape[0], 0:n], ALU.pow, after=(t,))

    def normalize(self, src, dst, width, gain, rstd, ready, dst_free=None):
        g, g_ready, b = gain
        step = min(width, 512)
        out = []
        for tok in range(NT):
            out.append([self.V(self.nc.vector.scalar_tensor_tensor, out=dst(tok)[:, c:c + step], in0=src(tok)[:, c:c + step],
                               scalar=rstd[:, tok:tok + 1], in1=g[:, c:c + step], op0=ALU.mult, op1=ALU.mult,
                               after=(ready[tok], g_ready, dst_free)) for c in range(0, width, step)])
        self.gain_free[b] = out
        self.rstd_free = out
        return out

    def transposes(self, blocks, ready, evacuate, banks=(4, 5, 6, 7), per=4):
        tokens, n = [], 0
        while n < len(blocks):
            now = blocks[n:n + per]
            b = banks[(n // per) % len(banks)]
            for j, (src, rows) in enumerate(now):
                self.PE.wait(ready, self.bank_free[b])
                m = self.nc.tensor.transpose(self.bank[b][0:rows, j * P:(j + 1) * P], src, self.ident[:, :])
            m.then_inc(self.PE.sem, 1)
            self.PE.count += 1
            done = Token(self.PE.sem, self.PE.count, self.PE.rate)
            read = evacuate(n // per, self.bank[b], done)
            self.bank_free[b] = read
            tokens.append(read)
            n += per
        return tokens

    def copy(self, n, out, in_, after):
        if n % 2:
            return self.A(self.nc.scalar.activation, out, in_, ACT.Copy, after=after)
        return self.V(self.nc.vector.tensor_copy, out, in_, after=after)

    def to_channels(self, src, nk, hi, lo, ready, free=None, banks=(4, 5, 6, 7), before=None):
        out = []
        groups = [(tok, k) for tok in range(NT) for k in range(0, nk, 4)]
        made = {}
        for n, (tok, k0) in enumerate(groups):
            if before is not None:
                for g in groups[n:n + 2]:
                    if g not in made:
                        made[g] = before(g[0], g[1] // 4)
            b, m = banks[n % len(banks)], min(4, nk - k0)
            self.PE.wait(ready, made.get((tok, k0)), self.bank_free[b])
            for j in range(m):
                t = self.nc.tensor.transpose(self.bank[b][:, j * P:(j + 1) * P], src(tok, k0 + j), self.ident[:, :])
            t.then_inc(self.PE.sem, 1)
            self.PE.count += 1
            done = self.PE.last()
            view = self.bank[b][:, 0:m * P].rearrange("p (k t) -> p k t", k=m)
            cols = (slice(None), slice(k0, k0 + m), slice(tok * P, (tok + 1) * P))
            h = self.A(self.nc.scalar.activation, hi[cols], view, ACT.Copy, after=(done, free))
            l = self.V(self.nc.vector.tensor_tensor, lo[cols], view, hi[cols].bitcast(F32), ALU.subtract,
                       after=(h, done, free))
            self.bank_free[b] = [h, l]
            out += [h, l]
        return out

    def norm_to_channels(self, x, width, gain, eps, hi, lo, ready, free=None, rstd_ready=None, rows=None, junk=None):
        if len(ready) != NT:
            ready = [ready] * NT
        r = rstd_ready or self.inv_rms(lambda tok: x[:, tok, 0:width], width, eps, ready, self.rstd, junk)
        g, g_ready, b = gain
        step = min(width, 512)
        norms = []
        xn_free = self.xn_free if rows is None else None
        xn = self.xn if rows is None else rows

        def before(tok, n):
            c = slice(n * step, (n + 1) * step)
            norms.append(self.V(self.nc.vector.scalar_tensor_tensor, out=xn[:, tok, c], in0=x[:, tok, c],
                                scalar=self.rstd[:, tok:tok + 1], in1=g[:, c], op0=ALU.mult, op1=ALU.mult,
                                after=(r[tok], g_ready, xn_free)))
            return norms[-1]
        t = self.to_channels(lambda tok, k: xn[:, tok, k * P:(k + 1) * P], width // P, hi, lo, None, free,
                             before=before)
        self.gain_free[b] = self.rstd_free = norms
        if rows is None:
            self.xn_free = t
        return t

    def attention(self, heads, stage_qk, spans, scale, bias, v_of, dv, out_of, ready, tag, out_free=None, between=None,
                  combine=None):
        nc, PE, V, A = self.nc, self.PE, self.V, self.A
        off = [0, spans[0]]
        total = sum(spans)
        step = 1 if combine is None else 2
        n = len(heads) // step
        st = {}
        e_size = 384 if total == 384 else 512
        self.e_free = [list(self.e_free)] * 4
        e_free, pt_free, l_free = self.e_free, self.pt_free, self.l_free
        outs = []
        ne = 4 if step == 2 else 2

        def logits_and_exp(i):
            st[i] = {"e": [], "exp": []}
            for j in range(step):
                hh = heads[i * step + j]
                b = 4 + hh % 2
                PE.wait(ready, self.bank_free[b])
                q = stage_qk(hh, self.bank[b], spans, off)
                stat = self.stats[:, (i * step + j) % 4, :]
                sf = self.stat_free[(i * step + j) % 4]
                lb = hh % 2
                if bias is not None:
                    L = self.lbuf[:, lb, 0:total]
                    l = V(nc.vector.scalar_tensor_tensor, out=L, in0=self.bank[b][:, 0:total], scalar=scale,
                          in1=bias(hh), op0=ALU.mult, op1=ALU.add, after=(q, l_free[lb], self.bias_ready))
                    self.bank_free[b] = l
                    k = 1.0
                else:
                    L, l, k = self.bank[b][:, 0:total], q, scale
                mx = [V(nc.vector.tensor_reduce, out=stat[:, tok:tok + 1], in_=L[:, off[tok]:off[tok] + spans[tok]],
                        axis=AX.X, op=ALU.max, negate=True, after=(l, sf)) for tok in range(NT)]
                if k != 1.0:
                    mx = V(nc.vector.tensor_scalar, stat[:, 0:2], stat[:, 0:2], k, None, ALU.mult, after=mx)
                slot = (i * step + j) % ne
                E = self.ebuf[:, slot * e_size:slot * e_size + total]
                ex = [A(nc.scalar.activation, E[:, off[tok]:off[tok] + spans[tok]], L[:, off[tok]:off[tok] + spans[tok]],
                        ACT.Exp, bias=stat[:, tok:tok + 1], scale=k, accum_out=stat[:, 2 + tok:3 + tok],
                        after=(mx, l, e_free[slot])) for tok in range(NT)]
                if bias is None:
                    self.bank_free[b] = ex
                else:
                    l_free[lb] = ex
                st[i]["e"].append((E, slot, stat, (i * step + j) % 4))
                st[i]["exp"].append(ex)

        def weights_transposed(i):
            E, slot, stat, sn = st[i]["e"][0]
            rc = [V(nc.vector.reciprocal, s_[:, 4:6], s_[:, 2:4], after=(x, self.stat_free[m]))
                  for (_, _, s_, m), x in zip(st[i]["e"], st[i]["exp"])]
            if step == 2:
                E1, slot1, stat1, sn1 = st[i]["e"][1]
                m = V(nc.vector.tensor_scalar, stat1[:, 6:8], stat1[:, 4:6], combine[0], None, ALU.mult,
                      after=(rc, combine[1]))
                rc = []
                for tok in range(NT):
                    a, z = off[tok], off[tok] + spans[tok]
                    f = V(nc.vector.tensor_scalar, E1[:, a:z], E1[:, a:z], stat1[:, 6 + tok:7 + tok], None, ALU.mult,
                          after=(m,))
                    rc.append(V(nc.vector.scalar_tensor_tensor, out=E[:, a:z], in0=E[:, a:z],
                                scalar=stat[:, 4 + tok:5 + tok], in1=E1[:, a:z], op0=ALU.mult, op1=ALU.add, after=(f,)))
                e_free[slot1] = rc
                self.stat_free[sn1] = rc
                self.stat_free[sn] = rc
            blocks = [E[:, c:c + P] for c in range(0, total, P)]
            b = 6 + i % 2
            PE.wait(rc if step == 2 else st[i]["exp"], self.bank_free[b])
            for j, blk in enumerate(blocks):
                m = nc.tensor.transpose(self.bank[b][:, j * P:(j + 1) * P], blk, self.ident[:, :])
            m.then_inc(PE.sem, 1)
            PE.count += 1
            done = Token(PE.sem, PE.count)
            e_free[slot] = done
            pt = self.ptbuf[:, (i % 2) * 512:(i % 2) * 512 + total]
            c = A(nc.scalar.activation, pt, self.bank[b][:, 0:total], ACT.Copy, after=(done, pt_free[i % 2]))
            self.bank_free[b] = c
            st[i].update(pt=pt, copied=c, rc=rc, stat=stat, sn=sn)

        def values(i):
            b = 2 + i % 2
            pt = st[i]["pt"]
            PE.wait(st[i]["copied"], self.bank_free[b])
            for tok in range(NT):
                nb = spans[tok] // P
                for j in range(nb):
                    c = off[tok] + j * P
                    m = nc.tensor.matmul(self.bank[b][:, tok * dv:(tok + 1) * dv], pt[:, c:c + P], v_of(heads[i * step], j),
                                         start=j == 0, stop=j == nb - 1)
            m.then_inc(PE.sem, 1)
            PE.count += 1
            done = Token(PE.sem, PE.count)
            pt_free[i % 2] = done
            view = self.bank[b][:, 0:NT * dv].rearrange("p (t d) -> p t d", t=NT)
            if step == 2:
                o = self.A(nc.scalar.activation, out_of(i), view, ACT.Copy, after=(done, out_free))
            else:
                o = V(nc.vector.tensor_tensor, out_of(i), view,
                      st[i]["stat"][:, 4:6].unsqueeze(2).to_broadcast((P, NT, dv)), ALU.mult,
                      after=(done, st[i]["rc"], out_free))
                self.stat_free[st[i]["sn"]] = o
            self.bank_free[b] = o
            outs.append(o)

        for i in range(n + 2):
            if i < n:
                logits_and_exp(i)
            if 1 <= i <= n:
                weights_transposed(i - 1)
            if i >= 2:
                values(i - 2)
            if between is not None and i < n:
                between(i)
        return outs

    def qk_pairs(self, qT, kT, scale_rows=64):
        def stage(h, bank, spans, off):
            p, blk = 64 * (h % 2), h // 2
            for tok in range(NT):
                m = self.nc.tensor.matmul(bank[:, off[tok]:off[tok] + spans[tok]],
                                          qT[p:p + 64, blk, tok * P:(tok + 1) * P],
                                          kT[p:p + 64, blk, 0:spans[tok]], start=True, stop=True)
            m.then_inc(self.PE.sem, 1)
            self.PE.count += 1
            return Token(self.PE.sem, self.PE.count)
        return stage

    def add_residual(self, done, bank_ids, cols):
        out = []
        for tok, b in enumerate(bank_ids):
            o = self.x[:, tok, cols:cols + 512]
            t = self.V(self.nc.vector.tensor_tensor, o, self.bank[b][:, :], o, ALU.add, after=(done[tok], self.x_free))
            self.bank_free[b] = t
            out.append(t)
        return out

    def project_residual(self, name, lhs, ready, between=None):
        out = []
        for g in range(2):
            if g and between is not None:
                between()
            banks = (2 * g, 2 * g + 1)
            self.run(self.job(name, lhs, ready, KT, 512 * g, 512, banks,
                              lambda done: out.append(self.add_residual(done, banks, 512 * g))))
        self.xt_free = self.used_token(len(self.units) - 1)
        return [[out[g][tok] for g in range(2)] for tok in range(NT)]

    def feed_forward(self, gate_up, down, gain, ready):
        nc, PE, V, A = self.nc, self.PE, self.V, self.A
        n = self.norm_to_channels(self.x, D, gain, EPS, self.XH, self.XL, ready, self.xt_free)
        tag = down
        HH = self.work("hidden_hi_" + tag, 24, [P, 2 * NPAIR, S], F32R)
        HL = self.work("hidden_lo_" + tag, 46, [P, 2 * NPAIR, S], F32R)
        act = self.work("silu_" + tag, 69, [P, 2, NT, 256])
        hid = self.work("hidden_" + tag, 73, [P, 2, NT, 256])
        hh = HH[:, :, :].rearrange("p k t -> p (k t)")
        hl = HL[:, :, :].rearrange("p k t -> p (k t)")
        state = {"act0": None, "act1": None, "hid0": None, "hid1": None, "mul0": None, "mul1": None}

        def gate_and_up(p, par):
            banks = (2 * par, 2 * par + 1)
            free = [self.bank_free[b] for b in banks]
            first = self.unit_product(("pair",) + (gate_up, p, 0), 0, 4, 512, 512, True, False, (self.XH, self.XL),
                                      [self.bank[b] for b in banks], after=(free, n if not self.looping else None))
            done = self.unit_product(("pair",) + (gate_up, p, 4), 4, 4, 512, 512, False, True, (self.XH, self.XL),
                                     [self.bank[b] for b in banks])
            mul = []
            for tok in range(NT):
                b = banks[tok]
                a = A(nc.scalar.activation, act[:, par, tok, :], self.bank[b][:, 0:256], ACT.Silu,
                      after=(done[tok], state[f"mul{par}"]))
                m = V(nc.vector.tensor_tensor, hid[:, par, tok, :], act[:, par, tok, :], self.bank[b][:, 256:512],
                      ALU.mult, after=(a, done[tok], state[f"hid{par}"]))
                self.bank_free[b] = [a, m]
                mul.append(m)
            state[f"mul{par}"] = mul
            return done

        def hidden_to_channels(at, par):
            b = 4 + par
            PE.wait(state[f"mul{par}"], self.bank_free[b])
            for c in range(2):
                for tok in range(NT):
                    m = nc.tensor.transpose(self.bank[b][:, (2 * c + tok) * P:(2 * c + tok + 1) * P],
                                            hid[:, par, tok, c * P:(c + 1) * P], self.ident[:, :])
            m.then_inc(PE.sem, 1)
            PE.count += 1
            done = Token(PE.sem, PE.count, PE.rate)
            state[f"hid{par}"] = done
            h = A(nc.scalar.activation, hh[:, at], self.bank[b][:, :], ACT.Copy, after=(done,))
            l = V(nc.vector.tensor_tensor, hl[:, at], self.bank[b][:, :], hh[:, at].bitcast(F32), ALU.subtract,
                  after=(done, h))
            self.bank_free[b] = [h, l]
            return [h, l]

        def two_pairs(i, state):
            pair = 1 if self.looping else i
            gate_and_up(2 * pair + 1, 1)
            hidden_to_channels(bass.ds(i * 1024, 512), 0)
            gate_and_up(2 * pair + 2, 0)
            state["last"] = hidden_to_channels(bass.ds(i * 1024 + 512, 512), 1)

        gate_and_up(0, 0)
        self.loop((NPAIR - 1) // 2, two_pairs, state)
        last = hidden_to_channels(bass.ds((NPAIR - 1) * 512, 512), 0)
        self.xt_free = self.used_token(len(self.units) - 1)
        banks = (0, 1, 2, 3)
        free = [self.bank_free[b] for b in banks]
        for u in range(NPAIR):
            done = self.unit_product(("part", down, 2 * u, 2, 0, D, D), 2 * u, 2, D, D, u == 0, u == NPAIR - 1,
                                     (HH, HL), [self.bank[b] for b in banks],
                                     after=(free, state["last"] if u < NPAIR - 1 else last))
        out = []
        for tok in range(NT):
            out.append([])
            for half in range(2):
                b, o = 2 * tok + half, self.x[:, tok, 512 * half:512 * half + 512]
                self.bank_free[b] = self.V(nc.vector.tensor_tensor, o, self.bank[b][:, :], o, ALU.add, after=(done[tok],))
                out[tok].append(self.bank_free[b])
        return out


def build(nc, t, out_dram, total_units):
    p = Program(nc, t)
    PE, V, A, G, SP = p.PE, p.V, p.A, p.G, p.SP
    p.total_units = total_units
    weights = t["weights"]

    ring_at = nc.sbuf_base + (-nc.sbuf_base) % 64
    place = p.sb("ring_place", [P, RING * UNIT + 16])
    p.w_raw = nc.alloc_sbuf_tensor_at("w_raw", [P, RING, UNIT], F32, offset=ring_at)
    p.w_lo = nc.alloc_sbuf_tensor_at("w_lo", [P, RING, UNIT], F32R, offset=ring_at)
    p.w_hi = p.sb("w_hi", [P, RING, UNIT], F32R)
    p.x = p.sb("x", [P, NT, D])
    p.xn = p.sb("xn", [P, NT, D])
    channels_at = nc.sbuf_base + (-nc.sbuf_base) % 64
    p.sb("channels_place", [P, 2 * KT * S + 16])
    p.XH = nc.alloc_sbuf_tensor_at("x_channels_hi", [P, KT, S], F32R, offset=channels_at)
    p.XL = nc.alloc_sbuf_tensor_at("x_channels_lo", [P, KT, S], F32R, offset=channels_at + 4 * KT * S)

    def in_channels_place(name, kb, shape):
        return nc.alloc_sbuf_tensor_at(name, shape, F32, offset=int(channels_at + kb * KB))
    p.gains = [p.sb(f"gain_{b}", [P, D]) for b in range(2)]
    p.ident = p.sb("ident", [P, P])
    p.minus_half = p.sb("minus_half", [P, 16])
    p.cols = p.sb("cols", [P, 64])
    p.rstd = p.sb("rstd", [P, 2])
    p.rstd2 = p.sb("rstd2", [P, 16])
    p.stats = p.sb("stats", [P, 4, 8])
    p.lamb = p.sb("lambda_", [P, 8])
    p.sb_masks = p.sb("triangle_masks", [P, 13, P], mybir.dt.bfloat16)
    p.head_of = p.sb("head_of", [P, RWB, RW_HEADS])
    p.head_rk = p.sb("head_r_k", [P, RWB, RW_HEADS])
    p.mid, p.omk, p.state_factor = p.sb("mid", [P, RWB * NT]), p.sb("one_less_k_a", [P, RWB]), p.sb("state_factor", [P, RWB])
    p.rk_rows, p.gn = p.sb("r_k_rows", [P, NT, RW_HEADS]), p.sb("group_norm", [P, 36])
    p.posi, p.posf, p.freq = p.sb("pos_int", [P, NT], I32), p.sb("pos", [P, NT]), p.sb("freq", [P, 16])
    p.cosr, p.sinr = p.sb("cos", [P, NT, 16]), p.sb("sin", [P, NT, 16])
    arena = nc.sbuf_base + (-nc.sbuf_base) % 64
    p.arena, p.arena_size = arena, nc.sbuf_usable_end - arena
    p.lbuf = p.work("logits", 88, [P, 2, 512])
    p.ebuf = p.work("exps", 92, [P, 3 * 512])[:, :]
    p.ptbuf = p.work("weights_t", 84, [P, 2 * 512])[:, :]
    p.bank = [nc.alloc_psum_tensor(f"bank{b}", [P, 512], F32)[:, :] for b in range(8)]
    p.xn_free = p.xt_free = p.x_free = p.bias_ready = None
    p.e_free, p.pt_free, p.l_free, p.stat_free = [None] * 4, [None] * 2, [None] * 2, [None] * 4
    p.rstd_free = p.gn_free = None

    def load_unit(u, slot, round_=None):
        if round_ is None:
            if u >= RING:
                nc.sync.wait_ge(p.used, u - RING + 1)
            src = weights[u]
        else:
            nc.sync.wait_ge(p.used, round_ * RING + slot + 1)
            src = weights[bass.ds((round_ + 1) * RING + slot, 1)].rearrange("a p n -> (a p) n")
        nc.sync.dma_start(p.w_raw[:, slot, :], src).then_inc(p.loaded[slot], 16)

    io = [nc.alloc_semaphore(f"input_{n}") for n in range(8)]

    def row_major(name):
        return t[name].rearrange("(t p) d -> p t d", p=P)

    nc.sync.dma_start(p.x[:, :, :], row_major("x")).then_inc(io[0], 16)
    x_ready = Token(io[0], 16)
    for u in range(RING):
        load_unit(u, u)
    gain_mix = p.load_gain("mix_norm_g")

    def identity(m, rows):
        z = G(nc.gpsimd.memset, m, 0.0)
        return G(nc.gpsimd.affine_select, out=m, in_=m, compare_op=ALU.not_equal, fill=1.0, base=0,
                 pattern=[[-1, P]], channel_multiplier=1, after=(z,))

    ident_ready = identity(p.ident[:, :], P)
    half_ready = G(nc.gpsimd.memset, p.minus_half[:, :], -0.5)
    PE.wait(ident_ready)

    NB, RL, NH = 33, 384, A_HEADS + B_HEADS
    tab = p.work("bias_table", 34, [NB, NH])
    hot = p.work("bias_one_hot", 35, [NB, RL])
    tneg = V(nc.vector.memset, tab[:, :], NEG)
    A.wait(tneg)
    nc.scalar.dma_start(tab[0:NB - 1, :], t["rel_bias_table"]).then_inc(io[3], 16)
    nc.scalar.dma_start(hot[:, :], t["bucket_one_hot"]).then_inc(io[3], 16)
    toep = nc.dram_tensor("bias_rows", (NH, P, RL), F32, kind="Internal").ap()
    line = p.work("bias_lines", 16, [P, NH, RL])
    for h in range(NH):
        b = h % 8
        m = PE(nc.tensor.matmul, p.bank[b][:, 0:RL], tab[:, h:h + 1].to_broadcast((NB, P)), hot[:, :], start=True,
               stop=True, after=(Token(io[3], 32), p.bank_free[b]))
        p.bank_free[b] = p.copy(h, line[:, h, :], p.bank[b][:, 0:RL], (m,))
        SP.wait(p.bank_free[b])
        nc.sync.dma_start(toep[h, :, :], line[:, h, :]).then_inc(io[4], 16)
    lines_written = Token(io[4], 16 * NH)
    bias = p.work("bias", 64, [P, NH, 384])

    def read_bias():
        A.wait(lines_written)
        for tile, (lo, n) in enumerate(((P, P), (0, S))):
            skew = bass.AP(toep.tensor, P - 1 + lo, [[RL - 1, P], [P * RL, NH], [1, n]])
            nc.scalar.dma_start(bias[:, :, tile * P:tile * P + n], skew).then_inc(io[5], 16)
        p.bias_ready = Token(io[5], 32)

    with nc.sync.Fori(0, total_units // RING - 1) as i:
        for slot in range(RING):
            load_unit(None, slot, i)
    for u in range(total_units // RING * RING, total_units):
        load_unit(u, u % RING)

    def at_tok(tile_, w=None):
        return lambda tok: tile_[:, tok, :] if w is None else tile_[:, tok, w[0]:w[1]]

    xt = p.norm_to_channels(p.x, D, gain_mix, EPS, p.XH, p.XL, [[x_ready, half_ready]] * NT)
    proj = p.work("proj", 40, [P, NT, 6 * 512])
    X = (p.XH, p.XL)

    def in_pair(g, banks, into):
        return p.job("w_in", X, xt, KT, 512 * g, 512, banks,
                     p.rows_of(at_tok(proj, (512 * g, 512 * g + 512)), banks, 512, into))

    def heads_to_channels(src_cols, dst, ready, banks=(4, 5, 6, 7), n_blocks=4, src=None, free=None):
        src = proj if src is None else src
        blocks = [(src[:, tok, src_cols + k * P:src_cols + (k + 1) * P], P) for k in range(n_blocks) for tok in range(NT)]
        turn = [0]

        def evacuate(g, bank, done):
            m = min(2, n_blocks - 2 * g)
            turn[0] += 1
            return p.copy(turn[0], dst[:, 2 * g:2 * g + m, :], bank[:, 0:m * S].rearrange("p (k t) -> p k t", k=m), (done, free))
        return p.transposes(blocks, ready, evacuate, banks)

    qa_rows, va_rows, b_rows = [], [], []
    p.run(in_pair(0, (0, 1), qa_rows))
    read_bias()
    gain_lambda = p.load_gain("diff_lambda", 256)
    mem1 = p.work("mem_rows", 16, [P, NT, D])
    G.wait(lines_written)
    nc.gpsimd.dma_start(mem1[:, :, :], row_major("mem")).then_inc(io[1], 16)
    mem1_ready = Token(io[1], 16)
    p.run(in_pair(1, (2, 3), qa_rows))

    wide_masks = p.work("wide_masks", 0, [P, 13, P])
    for dst, name in ((wide_masks[:, :, :], "triangle_masks"), (p.head_of[:, :, :], "head_of")):
        nc.gpsimd.dma_start(dst, t[name]).then_inc(io[7], 16)
    nc.gpsimd.dma_start(p.freq[:, :], t["inv_freq"].to_broadcast((P, 16))).then_inc(io[7], 16)
    nc.gpsimd.dma_start(p.posi[:, :], t["positions_2"].rearrange("a (t p) -> p (a t)", p=P),
                        allow_slow_non_contiguous=True).then_inc(io[7], 16)
    const_ready = pos_ready = Token(io[7], 64)
    masks_ready = V(nc.vector.tensor_copy, p.sb_masks[:, :, :], wide_masks[:, :, :], after=(const_ready,))

    rows = p.work("vector_rows", 7, [P, P])
    col_of, n_rows, loads = {}, 0, 0
    for name, width in (("a_shift_mu_2", SHB * P), ("a_decay_bias_2", RW), ("a_aaa_bias_2", RW), ("a_k_k_2", RW),
                        ("a_k_a_2", RW), ("a_r_k_2", RW)):
        n = width // P
        nc.gpsimd.dma_start(rows[n_rows:n_rows + n, :], t[name].rearrange("a (n p) -> (a n) p", p=P)).then_inc(io[2], 16)
        col_of[name] = n_rows
        n_rows += n
        loads += 16
    PE.wait(Token(io[2], loads))
    cols_t = PE(nc.tensor.transpose, p.bank[7][:, 0:n_rows], rows[0:n_rows, :], p.ident[0:n_rows, 0:n_rows])
    cols_ready = V(nc.vector.tensor_copy, p.cols[:, 0:n_rows], p.bank[7][:, 0:n_rows], after=(cols_t,))
    p.bank_free[7] = cols_ready

    def col(name, b):
        return p.cols[:, col_of[name] + b:col_of[name] + b + 1]


    lg, lg_ready, lgb = gain_lambda
    lv = lg.rearrange("p (a b d) -> p a b d", a=2, b=2)
    lprod = p.work("lambda_product", 7.5, [P, 2, 64])
    a1 = V(nc.vector.tensor_tensor, lprod[:, :, :], lv[:, :, 0, :], lv[:, :, 1, :], ALU.mult, after=(lg_ready,))
    p.gain_free[lgb] = a1
    a2 = V(nc.vector.tensor_reduce, out=p.lamb[:, 0:2], in_=lprod[:, :, :], axis=AX.X, op=ALU.add, after=(a1,))
    a3 = A(nc.scalar.activation, p.lamb[:, 2:4], p.lamb[:, 0:2], ACT.Exp, after=(a2,))
    a4 = V(nc.vector.tensor_tensor, p.lamb[:, 4:5], p.lamb[:, 3:4], p.lamb[:, 2:3], ALU.subtract, after=(a3,))
    lam_ready = V(nc.vector.tensor_scalar, p.lamb[:, 5:6], p.lamb[:, 4:5], -LAMBDA_INIT, None, ALU.add, after=(a4,))

    gain_moba = p.load_gain("moba_out_g", 512)
    p.run(in_pair(2, (0, 1), va_rows))
    qT, kT = p.work("qT", 8, [P, 4, S]), p.work("kT", 12, [P, 4, S])
    qk = heads_to_channels(0, qT, qa_rows) + heads_to_channels(512, kT, qa_rows)
    p.pending = [in_pair(3, (0, 1), b_rows), in_pair(4, (0, 1), b_rows), in_pair(5, (0, 1), b_rows)]
    oa = p.attention(list(range(A_HEADS)), p.qk_pairs(qT, kT), (P, S), 0.125, lambda h: bias[:, h, :],
                     lambda h, j: proj[:, j, 1024 + 64 * h:1088 + 64 * h], 64, lambda i: p.xn[:, :, 64 * i:64 * i + 64],
                     [qk, va_rows], "a", out_free=p.xn_free, between=lambda i: p.fill(1))
    p.fill_rest()
    p.xt_free = p.used_token(len(p.units) - 1)

    qk = heads_to_channels(1536, qT, b_rows) + heads_to_channels(2048, kT, b_rows)
    gain_mem = p.load_gain("mem_norm_g")
    MH, ML = p.work("mem_channels_hi", 24, [P, KT, S], F32R), p.work("mem_channels_lo", 32, [P, KT, S], F32R)
    mem_squares = p.work("mem_squares", 0, [P, NT, D])
    mt = p.norm_to_channels(mem1, D, gain_mem, EPS, MH, ML, [[mem1_ready, masks_ready, cols_ready, lam_ready, PE.last()]] * NT,
                            rows=mem1, junk=mem_squares)

    r = p.inv_rms(lambda tok: p.xn[:, tok, 0:512], 512, EPS, [oa] * NT, p.rstd, junk=p.lbuf)
    p.l_free = [[V.last(), A.last()]] * 2
    oa = p.normalize(lambda tok: p.xn[:, tok, 0:512], lambda tok: p.xn[:, tok, 0:512], 512, gain_moba, p.rstd,
                     [(r[tok], oa) for tok in range(NT)])
    gain_sub = p.load_gain("diff_subln_g", P)
    gain_cross = p.load_gain("cross_norm_g")
    cross_v = p.work("cross_v", 16, [P, NT, D])
    ck_rows, cv_rows = [], []
    M = (MH, ML)
    p.pending = [p.job("w_ck", M, mt, KT, 512 * g, 512, (0, 1),
                       p.rows_of(at_tok(proj, (512 * g, 512 * g + 512)), (0, 1), 512, ck_rows)) for g in range(2)]
    p.pending += [p.job("w_cv", M, mt, KT, 512 * g, 512, (0, 1),
                        p.rows_of(at_tok(cross_v, (512 * g, 512 * g + 512)), (0, 1), 512, cv_rows)) for g in range(2)]
    ob = p.attention(list(range(2 * B_HEADS)), p.qk_pairs(qT, kT), (P, S), 0.125, lambda h: bias[:, A_HEADS + h // 2, :],
                     lambda h, j: proj[:, j, 2560 + 64 * h:2688 + 64 * h], P,
                     lambda i: p.xn[:, :, 512 + P * i:640 + P * i], [qk], "b", between=lambda i: p.fill(2),
                     combine=(p.lamb[:, 5:6], lam_ready))
    p.fill_rest()
    sq = p.lbuf[:, :, :]
    o4 = p.xn[:, :, 512:1024]
    b1 = A(nc.scalar.activation, sq, o4, ACT.Square, scale=float(P) ** -0.5, after=(ob, p.l_free))
    p.l_free = [b1, b1]
    b2 = V(nc.vector.tensor_reduce, out=p.rstd2[:, 0:8], in_=sq.rearrange("p t (h d) -> p (t h) d", h=B_HEADS), axis=AX.X,
           op=ALU.add, after=(b1,))
    p.l_free = [b2, b2]
    b3 = p.power(p.rstd2[:, 0:8], EPS, b2)
    b4 = V(nc.vector.tensor_scalar, p.rstd2[:, 8:16], p.rstd2[:, 0:8], 1.0 - LAMBDA_INIT, None, ALU.mult, after=(b3,))
    g, g_ready, gb = gain_sub
    for tok in range(NT):
        o = o4[:, tok, :].rearrange("p (h d) -> p h d", h=B_HEADS)
        b5 = V(nc.vector.tensor_tensor, o, o, p.rstd2[:, 8 + 4 * tok:12 + 4 * tok].unsqueeze(2).to_broadcast((P, B_HEADS, P)),
               ALU.mult, after=(b4,))
        b5 = V(nc.vector.tensor_tensor, o, o, g.unsqueeze(1).to_broadcast((P, B_HEADS, P)), ALU.mult, after=(b5, g_ready))
    p.gain_free[gb] = b5
    gain_mem2 = p.load_gain("mem_norm_g_2")
    mem2, mem2_squares = p.work("mem2_rows", 56, [P, NT, D]), p.work("mem2_squares", 44, [P, NT, D])
    G.wait(PE.last(), V.last(), A.last())
    nc.gpsimd.dma_start(mem2[:, :, :], row_major("mem_2")).then_inc(io[6], 16)
    m2 = []
    mixed = p.to_channels(lambda tok, k: p.xn[:, tok, k * P:(k + 1) * P], KT, p.XH, p.XL, (oa, b5), p.xt_free)
    p.xn_free = mixed
    x_done = p.project_residual("w_out", X, mixed, between=lambda: m2.extend(p.norm_to_channels(
        mem2, D, gain_mem2, EPS, MH, ML, [[Token(io[6], 16)]] * NT, rows=mem2, junk=mem2_squares)))

    cross_kT = p.work("cross_kT", 8, [P, KT, S])
    ckT = heads_to_channels(0, cross_kT, ck_rows, n_blocks=8, free=PE.last())
    xt = p.norm_to_channels(p.x, D, gain_cross, EPS, p.XH, p.XL, x_done, p.xt_free)
    gain_ffn = p.load_gain("ffn_norm_g")
    cq, cqT = p.work("cross_q", 40, [P, NT, D]), p.work("cross_qT", 48, [P, KT, S])
    cq_rows = []
    for g in range(2):
        p.run(p.job("w_cq", X, [xt, ckT], KT, 512 * g, 512, (2 * g, 2 * g + 1),
                    p.rows_of(at_tok(cq, (512 * g, 512 * g + 512)), (2 * g, 2 * g + 1), 512, cq_rows)))
    p.xt_free = p.used_token(len(p.units) - 1)
    qT2 = heads_to_channels(0, cqT, cq_rows, n_blocks=8, src=cq)

    mem_kT = [p.work(f"mem_kT_{n}", 4 * n, [P, 2, S]) for n in range(2)]
    mem_v = [p.work(f"mem_v_{n}", 4 * n + 2, [P, NT, S]) for n in range(2)]
    mk_rows = [p.work(f"mem_k_rows_{n}", 64 + 2 * n, [P, NT, S]) for n in range(2)]
    mem_ready = [[], []]

    def mem_kv(n, name):
        def evacuate(done):
            for tok in range(NT):
                a = A(nc.scalar.activation, mk_rows[n][:, tok, :], p.bank[tok][:, 0:256], ACT.Copy, after=(done[tok],))
                v = V(nc.vector.tensor_copy, mem_v[n][:, tok, :], p.bank[tok][:, 256:512], after=(done[tok], a))
                p.bank_free[tok] = [a, v]
                mem_ready[n] += [a, v]
        return p.job(name, M, m2, KT, 0, 512, (0, 1), evacuate)

    p.pending = [mem_kv(0, "a_mem_kv_2"), mem_kv(1, "b_mem_kv_2")]

    def qk_cross(h, bank, spans, off):
        for tok in range(NT):
            for k in range(2):
                m = nc.tensor.matmul(bank[:, off[tok]:off[tok] + S], cqT[:, 2 * h + k, tok * P:(tok + 1) * P],
                                     cross_kT[:, 2 * h + k, :], start=k == 0, stop=k == 1)
        m.then_inc(PE.sem, 1)
        PE.count += 1
        return Token(PE.sem, PE.count)

    oc = p.attention(list(range(MEM_HEADS)), qk_cross, (S, S), 0.0625, None,
                     lambda h, j: cross_v[:, j, 256 * h:256 * h + 256], 256, lambda i: p.xn[:, :, 256 * i:256 * i + 256],
                     [qT2, ckT, cv_rows], "c", out_free=p.xn_free, between=lambda i: p.fill(1))
    p.fill_rest()
    xt = p.to_channels(lambda tok, k: p.xn[:, tok, k * P:(k + 1) * P], KT, p.XH, p.XL, oc, p.xt_free)
    p.xn_free = xt
    for n in range(2):
        mem_ready[n] += heads_to_channels(0, mem_kT[n], mem_ready[n], n_blocks=2, src=mk_rows[n])
    x_done = p.project_residual("w_co", X, xt)

    x_done = p.feed_forward(("w_gate", "w_up"), "w_down", gain_ffn, x_done)
    gain_final, gain_n1 = p.load_gain("final_norm_g"), p.load_gain("a_norm1_g_2")
    r = p.inv_rms(lambda tok: p.x[:, tok, :], D, EPS, x_done, p.rstd)
    x_done = p.normalize(lambda tok: p.x[:, tok, :], lambda tok: p.x[:, tok, :], D, gain_final, p.rstd, r)

    n1 = p.norm_to_channels(p.x, D, gain_n1, EPS, p.XH, p.XL, x_done, p.xt_free)
    gain_lnx_g, gain_lnx_b = p.load_gain("a_lnx_g_2", RW), p.load_gain("a_lnx_b_2", RW)
    decay_up = p.work("decay_up", 76.625, [64, RW])
    aaa_up = p.work("aaa_up", 76.625, [P, RW])
    gate_up = p.work("gate_up", 79.625, [P, RW])
    head_of_t = p.work("head_of_t", 94.5, [RW_HEADS, RW])
    lora = nc.alloc_semaphore("lora_weights")
    G.wait(PE.last(), V.last(), A.last())
    for dst, name in ((decay_up[:, :], "a_decay_up_2"), (aaa_up[64:P, :], "a_aaa_up_2"), (gate_up[:, :], "a_gate_up_2"),
                      (head_of_t[:, :], "head_of_t")):
        nc.gpsimd.dma_start(dst, t[name]).then_inc(lora, 16)
    lora_ready = Token(lora, 64)
    proj2 = p.work("proj2", 8, [P, NT, 2816])
    raw = p.work("raw_channels", 30, [P, SHB, S + 1])
    sh = p.work("shifted", 50.25, [P, SHB, S])
    qmT = p.work("memory_queries", 23, [P, 2, S])
    raw0 = G(nc.gpsimd.memset, raw[:, :, 0:1], 0.0, after=(PE.last(), V.last(), A.last()))
    shifted = [None] * SHB
    qm_ready = []

    def shift_columns(g, rows):
        blocks = list(range(4 * g, min(4 * g + 4, 22)))

        def evacuate(n, bank, done):
            b0 = blocks[2 * n]
            view = bank[:, :].rearrange("p (k t) -> p k t", k=2)
            if b0 >= SHB:
                t = A(nc.scalar.activation, qmT[:, :, :], view, ACT.Copy, after=(done,))
                qm_ready.append(t)
                return t
            t = A(nc.scalar.activation, raw[:, b0:b0 + 2, 1:S + 1], view, ACT.Copy, after=(done,))
            d = V(nc.vector.tensor_tensor, sh[:, b0:b0 + 2, :], raw[:, b0:b0 + 2, 0:S], raw[:, b0:b0 + 2, 1:S + 1],
                  ALU.subtract, after=(t, raw0))
            for b in (b0, b0 + 1):
                shifted[b] = V(nc.vector.scalar_tensor_tensor, out=sh[:, b, :], in0=sh[:, b, :], scalar=col("a_shift_mu_2", b),
                               in1=raw[:, b, 1:S + 1], op0=ALU.mult, op1=ALU.add, after=(d, cols_ready))
            return t
        p.transposes([(proj2[:, tok, b * P:(b + 1) * P], P) for b in blocks for tok in range(NT)], rows, evacuate)

    last_rows = None
    for g in range(6):
        rows, width = [], 512 if g < 5 else 256
        banks = (2 * (g % 2), 2 * (g % 2) + 1)
        p.run(p.job("a_w_in_2", X, n1, KT, 512 * g, width, banks,
                    p.rows_of(at_tok(proj2, (512 * g, 512 * g + width)), banks, width, rows)))
        if g:
            shift_columns(g - 1, last_rows)
        last_rows = rows
    shift_columns(5, last_rows)
    p.xt_free = p.used_token(len(p.units) - 1)

    def memory_attention(n, qT_, ready, tag, between=None):
        return p.attention(list(range(MEM_HEADS)), p.qk_pairs(qT_, mem_kT[n]), (S, S), 0.125, None,
                           lambda h, j: mem_v[n][:, j, 64 * h:64 * h + 64], 64,
                           lambda i: p.xn[:, :, RW + 64 * i:RW + 64 * i + 64], [ready, mem_ready[n]], tag, out_free=p.xn_free,
                           between=between)

    masks = p.sb_masks
    rB, kB, vB = (sh[:, RWB * n:RWB * (n + 1), :] for n in range(3))
    sig = p.work("decay_sigmoid", 44, [P, RWB, S])
    lr = p.work("learning_rate", 38, [P, RWB, S])
    kk = p.work("removal_key", 32, [P, RWB, S])
    sqk = in_channels_place("removal_key_squares", 0, [P, RWB, S])
    cs = p.work("cumulated", 70.5, [P, RWB, NT, P + 1])
    down_ = p.work("decay_down", 76.625, [P, RWB, NT, P + 1])
    up_ = in_channels_place("decay_up_exp", 6, [P, RWB, NT, P + 1])
    ones_c = in_channels_place("ones_row", 12.25, [P, P])
    nrm = in_channels_place("inverse_norms", 13, [RW_HEADS, S])
    mid = p.mid
    raw_dead = list(shifted)
    channels_free = [p.xt_free]

    def per_channel(name):
        return p.cols[:, col_of[name]:col_of[name] + RWB].unsqueeze(2).to_broadcast((P, RWB, S))

    def by_chunk(a):
        return a.rearrange("p b (c t) -> p (b c) t", c=NT)

    td = A(nc.scalar.activation, sh[0:64, 18, :], sh[0:64, 18, :], ACT.Tanh, after=(shifted[18],))
    sg = A(nc.scalar.activation, sh[:, 19, :], sh[:, 19, :], ACT.Sigmoid, after=(shifted[19],))
    k1 = V(nc.vector.tensor_tensor, kk[:, :, :], kB, per_channel("a_k_k_2"), ALU.mult, after=(shifted,))
    cs0 = G(nc.gpsimd.memset, cs[:, :, :, 0:1], 0.0)
    on = G(nc.gpsimd.memset, ones_c[:, :], 1.0, after=channels_free)

    def upward(rows0, w, out, bias_name, bank, b):
        m = PE(nc.tensor.matmul, p.bank[bank][:, 0:S], w[rows0:rows0 + 64, b * P:(b + 1) * P], sh[rows0:rows0 + 64, 18, :],
               start=True, stop=True, after=(lora_ready, td, shifted[18], p.bank_free[bank]))
        p.bank_free[bank] = A(nc.scalar.activation, out[:, b, :], p.bank[bank][:, 0:S], ACT.Sigmoid,
                              bias=col(bias_name, b), after=(m, raw_dead, cols_ready))
        return p.bank_free[bank]

    sig_t = [upward(0, decay_up, sig, "a_decay_bias_2", 4 + b % 2, b) for b in range(RWB)]
    scans = [V(nc.vector.tensor_tensor_scan, out=cs[:, b, c, 1:P + 1], data0=ones_c[:, :], data1=sig[:, b, c * P:(c + 1) * P],
               initial=0.0, op0=ALU.mult, op1=ALU.add, after=(sig_t[b], on)) for b in range(RWB) for c in range(NT)]
    k2 = A(nc.scalar.activation, sqk[:, :, :], kk[:, :, :], ACT.Square, after=(k1, channels_free))
    lr_t = [upward(64, aaa_up, lr, "a_aaa_bias_2", 6 + b % 2, b) for b in range(RWB)]
    for b in range(RWB):
        PE.wait(k2, p.bank_free[0], const_ready)
        m = nc.tensor.matmul(p.bank[0][0:RW_HEADS, 0:S], p.head_of[:, b, :], sqk[:, b, :], start=b == 0, stop=b == RWB - 1)
    m.then_inc(PE.sem, 1)
    PE.count += 1
    squares_summed = PE.last()
    k3 = V(nc.vector.tensor_scalar, nrm[:, :], p.bank[0][0:RW_HEADS, 0:S], 1e-24, None, ALU.max, after=(PE.last(), channels_free))
    p.bank_free[0] = k3
    k4 = A(nc.scalar.activation, nrm[:, :], nrm[:, :], ACT.Sqrt, after=(k3,))
    csf = cs[:, :, :, :].rearrange("p b c t -> p (b c) t")
    md = V(nc.vector.tensor_copy, mid[:, :], csf[:, :, 64:65].rearrange("p n o -> p (n o)"), after=(scans,))
    k4 = V(nc.vector.reciprocal, nrm[:, :], nrm[:, :], after=(k4,))
    cm = V(nc.vector.tensor_tensor, csf, csf, mid[:, :].unsqueeze(2).to_broadcast((P, RWB * NT, P + 1)), ALU.subtract,
           after=(md, cs0))

    gate = p.work("gate", 17, [P, NT, RW])
    gate_t = []
    for tok in range(NT):
        for j, (c, w) in enumerate(((0, 512), (512, 256))):
            b = 2 * tok + j
            m = PE(nc.tensor.matmul, p.bank[b][:, 0:w], sh[:, 19, tok * P:(tok + 1) * P], gate_up[:, c:c + w], start=True,
                   stop=True, after=(lora_ready, sg, p.bank_free[b]))
            a = A(nc.scalar.activation, gate[:, tok, c:c + w], p.bank[b][:, 0:w], ACT.Copy, after=(m,))
            p.bank_free[b] = a
            gate_t.append(a)
    td_used = PE.last()
    e1 = A(nc.scalar.activation, down_[:, :, :, :], cs[:, :, :, :], ACT.Exp, scale=-KAPPA, after=(cm, td_used))
    e2 = A(nc.scalar.activation, up_[:, :, :, :], cs[:, :, :, :], ACT.Exp, scale=KAPPA, after=(cm, channels_free))

    kkn = []
    for n in range(3):
        b = 1 + n
        PE.wait(k4, p.bank_free[b])
        for j in range(2):
            m = nc.tensor.matmul(p.bank[b][:, j * S:(j + 1) * S], head_of_t[:, (2 * n + j) * P:(2 * n + j + 1) * P], nrm[:, :],
                                 start=True, stop=True)
        m.then_inc(PE.sem, 1)
        PE.count += 1
        k = kk[:, 2 * n:2 * n + 2, :].rearrange("p k t -> p (k t)")
        o = V(nc.vector.scalar_tensor_tensor, out=k, in0=k, scalar=-1.0, in1=p.bank[b][:, :], op0=ALU.mult, op1=ALU.mult,
              after=(PE.last(), k2))
        p.bank_free[b] = o
        kkn.append(o)

    v_rows = p.work("v_rows", 23, [P, NT, RW])

    def rows_back(dst, blocks_of, ready, free=None, banks=(4, 5, 6, 7)):
        def evacuate(n, bank, done):
            w = min(4, RWB - 4 * n) * P
            return p.copy(n, dst[:, 512 * n:512 * n + w], bank[:, 0:w], (done, free))
        return p.transposes([(blocks_of(b), P) for b in range(RWB)], ready, evacuate, banks)

    ar = p.work("a_and_r", 62.5, [P, RWB, NT, 2, P])
    fac = in_channels_place("key_factor", 0, [P, RWB, S])
    rk = in_channels_place("r_k", 0, [P, RWB, S])
    bt, kt = kk, lr
    tok_ = {}

    def key_factor():
        omk = V(nc.vector.tensor_scalar, p.omk[:, :], p.cols[:, col_of["a_k_a_2"]:col_of["a_k_a_2"] + RWB], -1.0, 1.0,
                ALU.mult, ALU.add, after=(cols_ready,))
        kf = [V(nc.vector.tensor_scalar, fac[:, b, :], lr[:, b, :], col("a_k_a_2", b), p.omk[:, b:b + 1], ALU.mult, ALU.add,
                after=(lr_t[b], omk, squares_summed)) for b in range(RWB)]
        tok_["b1"] = G(nc.gpsimd.tensor_tensor, lr[:, :, :], kk[:, :, :], lr[:, :, :], ALU.mult, after=(kf, kkn))
        tok_["kn"] = V(nc.vector.tensor_tensor, kB, kB, fac[:, :, :], ALU.mult, after=(kf, k1))

    def r_times_k():
        tok_["rcol"] = V(nc.vector.tensor_tensor, p.head_rk[:, :, :], p.head_of[:, :, :],
                         p.cols[:, col_of["a_r_k_2"]:col_of["a_r_k_2"] + RWB].unsqueeze(2).to_broadcast((P, RWB, RW_HEADS)),
                         ALU.mult, after=(cols_ready, const_ready))
        tok_["r1"] = V(nc.vector.tensor_tensor, rk[:, :, :], rB, kB, ALU.mult, after=(tok_["kn"], shifted[0:6]))

    pieces = [key_factor, r_times_k]
    ma = memory_attention(0, qmT, qm_ready, "m0", between=lambda i: pieces[i]() if i < len(pieces) else None)
    after_ma = [PE.last(), V.last(), A.last()]
    kn, r1, rcol = tok_["kn"], tok_["r1"], tok_["rcol"]
    v_t = []
    for tok in range(NT):
        v_t += rows_back(v_rows[:, tok, :], lambda b: vB[:, b, tok * P:(tok + 1) * P], shifted[12:18], after_ma)

    def each(a, q):
        return a[:, :, :, q, :].rearrange("p b c t -> p (b c) t")

    downf, upf = (z[:, :, :, :].rearrange("p b c t -> p (b c) t") for z in (down_, up_))
    o1 = V(nc.vector.tensor_tensor, each(ar, 0), by_chunk(kk[:, :, :]), downf[:, :, 0:P], ALU.mult,
           after=(e1, e2, kkn, v_t, td_used))
    o3 = V(nc.vector.scalar_tensor_tensor, out=by_chunk(bt[:, :, :]), in0=by_chunk(lr[:, :, :]), scalar=-1.0,
           in1=upf[:, :, 1:P + 1], op0=ALU.mult, op1=ALU.mult, after=(e2, tok_["b1"], o1))
    o4_ = V(nc.vector.tensor_tensor, by_chunk(kt[:, :, :]), by_chunk(kB), upf[:, :, 1:P + 1], ALU.mult, after=(e2, o3, r1))
    for c in range(NT):
        PE.wait(r1, rcol, p.bank_free[0])
        for b in range(RWB):
            m = nc.tensor.matmul(p.bank[0][:, c * 16:c * 16 + RW_HEADS], rk[:, b, c * P:(c + 1) * P], p.head_rk[:, b, :],
                                 start=b == 0, stop=b == RWB - 1)
    m.then_inc(PE.sem, 1)
    PE.count += 1
    rk_t = A(nc.scalar.activation, p.rk_rows[:, :, :],
             p.bank[0][:, 0:32].rearrange("p (c h) -> p c h", c=2)[:, :, 0:RW_HEADS], ACT.Copy, after=(PE.last(),))
    p.bank_free[0] = rk_t
    bt_rows, kt_rows = p.work("b_rows", 8, [P, RW]), p.work("k_rows", 11, [P, RW])
    o2 = V(nc.vector.tensor_tensor, each(ar, 1), by_chunk(rB), downf[:, :, 1:P + 1], ALU.mult,
           after=(e1, e2, r1, v_t, td_used, o4_))
    sf = V(nc.vector.tensor_tensor, p.state_factor[:, :], down_[:, :, 0, P:P + 1].rearrange("p b o -> p (b o)"),
           up_[:, :, 1, 0:1].rearrange("p b o -> p (b o)"), ALU.mult, after=(e1, e2))
    bk_t = rows_back(bt_rows[:, :], lambda b: bt[:, b, 0:P], o3, free=td_used)
    bk_t += rows_back(kt_rows[:, :], lambda b: kt[:, b, 0:P], o4_, free=td_used)

    y = p.work("y", 76.625, [P, NT, RW])
    state = p.work("state", 82.75, [P, RWB, 64])
    dead = [o1, o2, o3, o4_, sf, bk_t, after_ma]
    sets = []
    for n in range(2):
        at = ((44, 52, 54, 56, 58), (89, 60, 14, 29.5, 74.5))[n]
        sets.append(dict(
            lt=p.work(f"upper_{n}", at[0], [P, 4, 4, P]), lab=p.work(f"lab_{n}", at[1], [P, 4, P]),
            x=p.work(f"inverse_{n}", at[2], [P, 4, P]), xt=p.work(f"inverse_t_{n}", at[3], [P, 4, P]),
            w=p.work(f"step_{n}", at[4], [P, 4, P]),
            r=p.work(f"rhs_{n}", 84.5 + 2 * n, [P, 4, 64]), u=p.work(f"u_{n}", 85.5 + 2 * n, [P, 4, 64]), n=n, free=dead))
    state_t = [None] * RWB

    def mask(i):
        return masks[:, i, :].unsqueeze(1).to_broadcast((P, 4, P))

    def counted(m):
        m.then_inc(PE.sem, 1)
        PE.count += 1
        return PE.last()

    def triangles(q, c, g):
        base = 4 * q["n"]
        done = []
        for i in range(4):
            h = 4 * g + i
            par, blk, b = 64 * (h % 2), h // 2, base + h % 2
            rhs = ar[par:par + 64, blk, c, :, :].rearrange("p a t -> p (a t)")
            PE.wait(dead, p.bank_free[b])
            for j, lhs in enumerate((bt, kt)):
                m = nc.tensor.matmul(p.bank[b][:, 256 * j:256 * j + 256], lhs[par:par + 64, blk, c * P:(c + 1) * P], rhs,
                                     start=True, stop=True)
            m = counted(m)
            v = V(nc.vector.tensor_tensor, q["lt"][:, i, :, :], p.bank[b][:, :].rearrange("p (k t) -> p k t", k=4),
                  masks[:, 0:4, :], ALU.mult, after=(m, q["free"], masks_ready))
            p.bank_free[b] = v
            done.append(v)
        for par in range(2):
            b = base + 2 + par
            PE.wait(p.bank_free[b])
            for j in range(2):
                blk, r0 = 2 * g + j, 64 * par
                m = nc.tensor.matmul(p.bank[b][:, j * P:(j + 1) * P], ar[r0:r0 + 64, blk, c, 0, :],
                                     bt[r0:r0 + 64, blk, c * P:(c + 1) * P], start=True, stop=True)
            m = counted(m)
            v = V(nc.vector.tensor_tensor, q["lab"][:, par::2, :], p.bank[b][:, 0:256].rearrange("p (k t) -> p k t", k=2),
                  masks[:, 4:5, :].to_broadcast((P, 2, P)), ALU.mult, after=(m, q["free"]))
            p.bank_free[b] = v
            done.append(v)
        q["tri"] = done
        ib = p.ident[:, :].unsqueeze(1).to_broadcast((P, 4, P))
        a = V(nc.vector.tensor_tensor, q["x"][:, :, :], q["lab"][:, :, :], mask(5), ALU.mult, after=done)
        b_ = V(nc.vector.tensor_tensor, q["xt"][:, :, :], q["lt"][:, :, 0, :], mask(12), ALU.mult, after=done)
        a = V(nc.vector.tensor_tensor, q["x"][:, :, :], q["x"][:, :, :], ib, ALU.add, after=(a,))
        b_ = V(nc.vector.tensor_tensor, q["xt"][:, :, :], q["xt"][:, :, :], ib, ALU.add, after=(b_,))
        q["x_t"], q["xt_t"] = a, b_

    def double_first(q, level):
        b = 4 * q["n"]
        PE.wait(q["x_t"], q["tri"], p.bank_free[b])
        for i in range(4):
            m = nc.tensor.matmul(p.bank[b][:, i * P:(i + 1) * P], q["lt"][:, i, 0, :], q["x"][:, i, :], start=True, stop=True)
        m = counted(m)
        q["w_t"] = V(nc.vector.tensor_tensor, q["w"][:, :, :], p.bank[b][:, :].rearrange("p (k t) -> p k t", k=4),
                     mask(5 + level), ALU.mult, after=(m, q["x_t"], q["xt_t"]))
        p.bank_free[b] = q["w_t"]

    def double_second(q, level):
        b = 4 * q["n"] + 1
        last = level == 6
        PE.wait(q["w_t"], q["xt_t"], p.bank_free[b], p.bank_free[b + 1])
        if not last:
            for i in range(4):
                m = nc.tensor.matmul(p.bank[b][:, i * P:(i + 1) * P], q["xt"][:, i, :], q["w"][:, i, :], start=True, stop=True)
            m1 = counted(m)
        for i in range(4):
            m = nc.tensor.matmul(p.bank[b + 1][:, i * P:(i + 1) * P], q["w"][:, i, :], q["xt"][:, i, :], start=True, stop=True)
        m2 = counted(m)
        if not last:
            q["x_t"] = V(nc.vector.tensor_tensor, q["x"][:, :, :], p.bank[b][:, :].rearrange("p (k t) -> p k t", k=4),
                         q["x"][:, :, :], ALU.add, after=(m1,))
            p.bank_free[b] = q["x_t"]
        q["xt_t"] = V(nc.vector.tensor_tensor, q["xt"][:, :, :], p.bank[b + 1][:, :].rearrange("p (k t) -> p k t", k=4),
                      q["xt"][:, :, :], ALU.add, after=(m2,))
        p.bank_free[b + 1] = q["xt_t"]

    def by_parity(tile_, par, n=2):
        return tile_[:, par::2, :]

    def solve(q, c, g):
        base = 4 * q["n"]
        R, U, lt = q["r"], q["u"], q["lt"]
        rt = []
        for par in range(2):
            b = base + par
            PE.wait(q["tri"], v_t, p.bank_free[b], state_t if c else None)
            for j in range(2):
                i, h, blk = 2 * j + par, 4 * g + 2 * j + par, 2 * g + j
                o = p.bank[b][:, j * 64:j * 64 + 64]
                m = nc.tensor.matmul(o, lt[:, i, 2, :], v_rows[:, c, 64 * h:64 * h + 64], start=True, stop=c == 0)
                if c:
                    m = nc.tensor.matmul(o, ar[64 * par:64 * par + 64, blk, c, 0, :], state[64 * par:64 * par + 64, blk, :],
                                         start=False, stop=True)
            m = counted(m)
            r_ = A(nc.scalar.activation, by_parity(R, par), p.bank[b][:, 0:P].rearrange("p (k t) -> p k t", k=2), ACT.Copy,
                   after=(m, q["free"]))
            p.bank_free[b] = r_
            rt.append(r_)
        yield
        b = base + 2
        PE.wait(rt, q["xt_t"], p.bank_free[b])
        for i in range(4):
            m = nc.tensor.matmul(p.bank[b][:, i * 64:i * 64 + 64], q["xt"][:, i, :], R[:, i, :], start=True, stop=True)
        m = counted(m)
        ut = A(nc.scalar.activation, U[:, :, :], p.bank[b][:, 0:256].rearrange("p (k t) -> p k t", k=4), ACT.Copy,
               after=(m, q["free"]))
        p.bank_free[b] = ut
        yield
        if c == 0:
            b = base + 3
            PE.wait(ut, bk_t, p.bank_free[b])
            for j in range(2):
                for par in range(2):
                    i, h = 2 * j + par, 4 * g + 2 * j + par
                    o = p.bank[b][64 * par:64 * par + 64, j * 64:j * 64 + 64]
                    nc.tensor.matmul(o, bt_rows[:, 64 * h:64 * h + 64], U[:, i, :], start=True, stop=False)
                    m = nc.tensor.matmul(o, kt_rows[:, 64 * h:64 * h + 64], v_rows[:, 0, 64 * h:64 * h + 64], start=False,
                                         stop=True)
            m = counted(m)
            s_ = V(nc.vector.tensor_tensor, state[:, 2 * g:2 * g + 2, :], p.bank[b][:, 0:P].rearrange("p (k t) -> p k t", k=2),
                   p.state_factor[:, 2 * g:2 * g + 2].unsqueeze(2).to_broadcast((P, 2, 64)), ALU.mult, after=(m, dead))
            p.bank_free[b] = s_
            state_t[2 * g] = state_t[2 * g + 1] = s_
            yield
        yt = q["y_t"] = []
        for par in range(2):
            b = base + par
            PE.wait(ut, p.bank_free[b])
            for j in range(2):
                i, h, blk = 2 * j + par, 4 * g + 2 * j + par, 2 * g + j
                o = p.bank[b][:, j * 64:j * 64 + 64]
                nc.tensor.matmul(o, lt[:, i, 1, :], U[:, i, :], start=True, stop=False)
                m = nc.tensor.matmul(o, lt[:, i, 3, :], v_rows[:, c, 64 * h:64 * h + 64], start=False, stop=c == 0)
                if c:
                    m = nc.tensor.matmul(o, ar[64 * par:64 * par + 64, blk, c, 1, :], state[64 * par:64 * par + 64, blk, :],
                                         start=False, stop=True)
            m = counted(m)
            dst = y[:, c, :].rearrange("p (h d) -> p h d", d=64)[:, 4 * g + par:4 * g + 4:2, :]
            y_ = A(nc.scalar.activation, dst, p.bank[b][:, 0:P].rearrange("p (k t) -> p k t", k=2), ACT.Copy, after=(m, dead))
            p.bank_free[b] = y_
            yt.append(y_)
        q["free"] = [PE.last(), V.last()]

    lg_, lg_ready, lg_b = gain_lnx_g
    lb_, lb_ready, lb_b = gain_lnx_b

    def heads_of(a):
        return a.rearrange("p (h d) -> p h d", d=64)

    rest_t = []
    for c in range(NT):
        rest = p.xn[:, c, 0:RW]
        b_ = G(nc.gpsimd.tensor_tensor, heads_of(rest), heads_of(v_rows[:, c, :]),
               p.rk_rows[:, c, :].unsqueeze(2).to_broadcast((P, RW_HEADS, 64)), ALU.mult, after=(rk_t, v_t, p.xn_free))
        b_ = G(nc.gpsimd.tensor_tensor, rest, rest, lb_, ALU.add, after=(b_, lb_ready))
        b_ = G(nc.gpsimd.tensor_tensor, rest, rest, gate[:, c, :], ALU.mult, after=(b_, gate_t))
        rest_t.append(G(nc.gpsimd.tensor_tensor, gate[:, c, :], gate[:, c, :], lg_, ALU.mult, after=(b_, lg_ready)))
    p.gain_free[lg_b] = p.gain_free[lb_b] = rest_t
    y_squares = in_channels_place("y_squares", 0, [P, 2, 4, 64])
    p.gn_free = [dead] * 2

    def finish_heads(q, c, g, yt):
        yc = heads_of(y[:, c, 256 * g:256 * g + 256])
        st_, sq_ = p.gn[:, 12 * q["n"]:12 * q["n"] + 12], y_squares[:, q["n"], :, :]

        def wide(a):
            return a.unsqueeze(2).to_broadcast((P, 4, 64))
        out = p.xn[:, c, 256 * g:256 * g + 256]
        a = V(nc.vector.tensor_reduce, out=st_[:, 0:4], in_=yc, axis=AX.X, op=ALU.add, after=(yt, p.gn_free[q["n"]]))
        a = V(nc.vector.tensor_scalar, st_[:, 4:8], st_[:, 0:4], 1.0 / 64, None, ALU.mult, after=(a,))
        a = V(nc.vector.tensor_tensor, yc, yc, wide(st_[:, 4:8]), ALU.subtract, after=(a,))
        s_ = A(nc.scalar.activation, sq_, yc, ACT.Square, scale=0.125, after=(a, p.gn_free[q["n"]]))
        yield
        s_ = V(nc.vector.tensor_reduce, out=st_[:, 8:12], in_=sq_, axis=AX.X, op=ALU.add, after=(s_,))
        s_ = p.power(st_[:, 8:12], LNX_EPS, s_)
        yield
        a = V(nc.vector.tensor_tensor, yc, yc, wide(st_[:, 8:12]), ALU.mult, after=(s_,))
        p.gn_free[q["n"]] = a
        a = V(nc.vector.tensor_tensor, y[:, c, 256 * g:256 * g + 256], y[:, c, 256 * g:256 * g + 256],
              gate[:, c, 256 * g:256 * g + 256], ALU.mult, after=(a, rest_t[c]))
        yield
        rows_done.append(V(nc.vector.tensor_tensor, out, out, y[:, c, 256 * g:256 * g + 256], ALU.add, after=(a, rest_t[c])))

    work_list = [(c, g) for c in range(NT) for g in range(3)]
    rows_done, unfinished = [], []

    def step(steps):
        for piece in list(steps):
            if next(piece, "end") == "end":
                steps.remove(piece)

    for n in range(0, 6, 2):
        two = [(sets[0],) + work_list[n], (sets[1],) + work_list[n + 1]]
        for q, c, g in two:
            triangles(q, c, g)
        for level in range(1, 7):
            for q, c, g in two:
                double_first(q, level)
            for q, c, g in two:
                double_second(q, level)
            step(unfinished)
        solving = [solve(q, c, g) for q, c, g in two]
        while solving:
            step(solving)
        unfinished = [finish_heads(q, c, g, q["y_t"]) for q, c, g in two]
    while unfinished:
        step(unfinished)
    gain_n2 = p.load_gain("a_norm2_g_2")
    xt = p.to_channels(lambda tok, k: p.xn[:, tok, k * P:(k + 1) * P], KT, p.XH, p.XL, (rows_done, ma), p.xt_free)
    p.xn_free = xt
    x_done = p.project_residual("a_w_out_2", X, xt)
    x_done = p.feed_forward(("a_ffn_gu_2",), "a_ffn_down_2", gain_n2, x_done)

    gain_kv, gain_b1 = p.load_gain("kv_norm_g_2"), p.load_gain("b_norm1_g_2")
    KH, KL = p.work("kv_channels_hi", 8, [P, KT, S], F32R), p.work("kv_channels_lo", 16, [P, KT, S], F32R)
    r = p.inv_rms(lambda tok: p.x[:, tok, :], D, EPS, x_done, p.rstd)
    kv_n = p.normalize(lambda tok: p.x[:, tok, :], lambda tok: p.xn[:, tok, :], D, gain_kv, p.rstd, r)
    kv_x = p.to_channels(lambda tok, k: p.xn[:, tok, k * P:(k + 1) * P], KT, KH, KL, kv_n)
    b_n = p.normalize(lambda tok: p.x[:, tok, :], lambda tok: p.xn[:, tok, :], D, gain_b1, p.rstd, r, kv_x)
    b_x = p.to_channels(lambda tok, k: p.xn[:, tok, k * P:(k + 1) * P], KT, p.XH, p.XL, b_n, p.xt_free)
    p.xn_free = b_x
    gain_lat, gain_q = p.load_gain("kv_latent_g_2", 256), p.load_gain("b_q_norm_g_2", 512)

    rope = p.work("rope", 80, [P, 8, NT, 16])
    cosr, sinr = p.cosr, p.sinr
    angle, turns_, red = rope[:, 0, :, :], rope[:, 1, :, :], rope[:, 2, :, :]
    posf = V(nc.vector.tensor_copy, p.posf[:, :], p.posi[:, :], after=(pos_ready,))
    a = V(nc.vector.tensor_tensor, angle, p.posf[:, :].unsqueeze(2).to_broadcast((P, NT, 16)),
          p.freq[:, :].unsqueeze(1).to_broadcast((P, NT, 16)), ALU.mult, after=(posf, x_done))
    magic = 12582912.0
    b_ = V(nc.vector.tensor_scalar, turns_, angle, 1.0 / (2 * math.pi), magic, ALU.mult, ALU.add, after=(a,))
    b_ = V(nc.vector.tensor_scalar, turns_, turns_, magic, None, ALU.subtract, after=(b_,))
    parts = (6.28125, 0.0019350051879882812, 2 * math.pi - 6.28125 - 0.0019350051879882812)
    src = angle
    for part in parts:
        a = V(nc.vector.scalar_tensor_tensor, out=red, in0=turns_, scalar=-part, in1=src, op0=ALU.mult, op1=ALU.add, after=(a, b_))
        src = red
    pi = 3.1415925
    a = V(nc.vector.tensor_scalar, red, red, pi, -pi, ALU.min, ALU.max, after=(a,))
    sin_t = A(nc.scalar.activation, sinr[:, :, :], red, ACT.Sin, after=(a,))
    c_ = A(nc.scalar.activation, rope[:, 3, :, :], red, ACT.Abs, after=(a,))
    c_ = V(nc.vector.tensor_scalar, rope[:, 3, :, :], rope[:, 3, :, :], -1.0, math.pi / 2, ALU.mult, ALU.add, after=(c_,))
    cos_t = A(nc.scalar.activation, cosr[:, :, :], rope[:, 3, :, :], ACT.Sin, after=(c_,))

    ckr = p.work("latent_rows", 24, [P, NT, 288])
    bproj = p.work("b_proj", 27, [P, NT, 768])
    ckr_t, cq_t, qm_t = [], [], []
    p.run(p.job("kv_w_down_2", (KH, KL), kv_x, KT, 0, 288, (0, 1), p.rows_of(at_tok(ckr), (0, 1), 288, ckr_t)),
          p.job("b_w_in_2", X, b_x, KT, 0, 512, (2, 3), p.rows_of(at_tok(bproj, (0, 512)), (2, 3), 512, cq_t)),
          p.job("b_w_in_2", X, b_x, KT, 512, 256, (0, 1), p.rows_of(at_tok(bproj, (512, 768)), (0, 1), 256, qm_t)))
    LH, LL = p.work("latent_hi", 33, [P, 2, S], F32R), p.work("latent_lo", 35, [P, 2, S], F32R)
    QH, QL = p.work("q_latent_hi", 37, [P, 4, S], F32R), p.work("q_latent_lo", 41, [P, 4, S], F32R)
    lat = p.norm_to_channels(ckr, 256, gain_lat, EPS, LH, LL, [ckr_t] * NT)
    qlat = p.norm_to_channels(bproj, 512, gain_q, EPS, QH, QL, [cq_t] * NT)
    kv = p.work("kv", 8, [P, NT, 2 * RW])
    q = p.work("q", 45, [P, NT, MLA_HEADS * QK])
    kv_t, q_t = [], []
    kv_dead = p.used_token(len(p.units) - 1)

    def kv_rows(done, c0, bank_ids, width):
        A.wait(kv_dead)
        V.wait(kv_dead)
        p.rows_of(at_tok(kv, (c0, c0 + width)), bank_ids, width, kv_t)(done)
    p.run(p.job("kv_w_up_2", (LH, LL), lat, 2, 0, 1024, (0, 1, 2, 3), lambda d: kv_rows(d, 0, (0, 1, 2, 3), 1024)),
          p.job("kv_w_up_2", (LH, LL), lat, 2, 1024, 512, (0, 1), lambda d: kv_rows(d, 1024, (0, 1), 512)))
    for c0, w, banks in ((0, 512, (2, 3)), (512, 512, (0, 1)), (1024, 128, (2, 3))):
        p.run(p.job("b_q_up_2", (QH, QL), qlat, 4, c0, w, banks, p.rows_of(at_tok(q, (c0, c0 + w)), banks, w, q_t)))

    qmT1 = p.work("memory_queries_1", 54.5, [P, 2, S])
    qm1 = heads_to_channels(512, qmT1, qm_t, n_blocks=2, src=bproj)
    mb = memory_attention(1, qmT1, qm1, "m1")

    tmp = p.work("rotate", 57, [P, 4, MLA_HEADS, 16])

    def rotate(src, dst, tok, heads, ready, free):
        cb, sb_ = (x[:, tok, :].unsqueeze(1).to_broadcast((P, heads, 16)) for x in (cosr, sinr))
        t1, t2 = src[:, :, 0:16], src[:, :, 16:32]
        m = [V(nc.vector.tensor_tensor, tmp[:, i, 0:heads, :], x, w, ALU.mult, after=(ready, cos_t, sin_t, free))
             for i, (x, w) in enumerate(((t1, cb), (t2, sb_), (t2, cb), (t1, sb_)))]
        d1 = V(nc.vector.tensor_tensor, dst[:, :, 0:16], tmp[:, 0, 0:heads, :], tmp[:, 1, 0:heads, :], ALU.subtract, after=m)
        d2 = V(nc.vector.tensor_tensor, dst[:, :, 16:32], tmp[:, 2, 0:heads, :], tmp[:, 3, 0:heads, :], ALU.add, after=m)
        return [d1, d2]

    kcat = p.work("k_cat", 60, [P, NT, MLA_HEADS * QK])
    free = None
    q_rot, k_rot = [], []
    for tok in range(NT):
        qh = q[:, tok, :].rearrange("p (h d) -> p h d", d=QK)[:, :, 64:96]
        free = rotate(qh, qh, tok, MLA_HEADS, q_t, free)
        q_rot += free
        kr = ckr[:, tok, 256:288].unsqueeze(1)
        free = rotate(kr, kr, tok, 1, ckr_t, free)
        kc = kcat[:, tok, :].rearrange("p (h d) -> p h d", d=QK)
        k_rot.append(V(nc.vector.tensor_copy, kc[:, :, 64:96], kr.to_broadcast((P, MLA_HEADS, 32)), after=(free,)))
        k_rot.append(A(nc.scalar.activation, kc[:, :, 0:64], kv[:, tok, :].rearrange("p (h d) -> p h d", d=P)[:, :, 0:64],
                       ACT.Copy, after=(kv_t,)))
    q96, k96 = p.work("q_channels", 20, [QK, MLA_HEADS, S]), p.work("k_channels", 69.5, [QK, MLA_HEADS, S])

    def to_heads(src, dst, ready, free):
        blocks = [(src[:, tok, QK * h:QK * (h + 1)], QK) for h in range(MLA_HEADS) for tok in range(NT)]
        return p.transposes(blocks, ready, lambda n, bank, done: p.copy(
            n, dst[:, 2 * n:2 * n + 2, :], bank[0:QK, :].rearrange("p (k t) -> p k t", k=2), (done, free)))
    heads_t = to_heads(q, q96, q_rot, [k_rot, PE.last(), V.last(), A.last()])
    heads_t += to_heads(kcat, k96, k_rot, None)

    def qk_latent(h, bank, spans, off):
        for tok in range(NT):
            m = nc.tensor.matmul(bank[:, off[tok]:off[tok] + spans[tok]], q96[:, h, tok * P:(tok + 1) * P],
                                 k96[:, h, 0:spans[tok]], start=True, stop=True)
        return counted(m)

    causal = p.work("causal", 57, [P, 384])
    cz = G(nc.gpsimd.memset, causal[:, :], 0.0, after=(V.last(),))
    for c0, w, base_ in ((0, P, 0), (P, S, P)):
        cz = G(nc.gpsimd.affine_select, out=causal[:, c0:c0 + w], in_=causal[:, c0:c0 + w], compare_op=ALU.is_ge, fill=NEG,
               base=base_, pattern=[[-1, w]], channel_multiplier=1, after=(cz,))
    p.bias_ready = cz
    ol = p.attention(list(range(MLA_HEADS)), qk_latent, (P, S), float(QK) ** -0.5, lambda h: causal[:, :],
                     lambda h, j: kv[:, j, P * h + 64:P * h + 128], 64, lambda i: p.xn[:, :, 64 * i:64 * i + 64],
                     [heads_t], "l", out_free=p.xn_free)
    gain_n3 = p.load_gain("b_norm2_g_2")
    xt = p.to_channels(lambda tok, k: p.xn[:, tok, k * P:(k + 1) * P], KT, p.XH, p.XL, (ol, mb),
                       p.used_token(len(p.units) - 1))
    p.xn_free = xt
    x_done = p.project_residual("b_w_out_2", X, xt)
    x_done = p.feed_forward(("b_ffn_gu_2",), "b_ffn_down_2", gain_n3, x_done)
    gain_last = p.load_gain("final_norm_g_2")
    r = p.inv_rms(lambda tok: p.x[:, tok, :], D, EPS, x_done, p.rstd)
    x_done = p.normalize(lambda tok: p.x[:, tok, :], lambda tok: p.x[:, tok, :], D, gain_last, p.rstd, r)
    SP.wait(x_done)
    nc.sync.dma_start(out_dram.rearrange("(t p) d -> p t d", p=P), p.x[:, :, :]).then_inc(io[0], 16)
    nc.sync.wait_ge(io[0], 32)
    return p.units


STREAMED = ("w_in", "w_ck", "w_cv", "w_out", "w_cq", "a_mem_kv_2", "b_mem_kv_2", "w_co", "w_gate", "w_up", "w_down",
            "a_w_in_2", "a_w_out_2", "a_ffn_gu_2", "a_ffn_down_2", "kv_w_down_2", "kv_w_up_2", "b_w_in_2", "b_q_up_2",
            "b_w_out_2", "b_ffn_gu_2", "b_ffn_down_2")
VECTORS = ("mix_norm_g", "moba_out_g", "diff_lambda", "diff_subln_g", "cross_norm_g", "mem_norm_g", "ffn_norm_g",
           "final_norm_g", "mem_norm_g_2", "a_norm1_g_2", "a_lnx_g_2", "a_lnx_b_2", "a_norm2_g_2", "kv_norm_g_2",
           "kv_latent_g_2", "b_norm1_g_2", "b_q_norm_g_2", "b_norm2_g_2", "final_norm_g_2")
PLAIN = ("x", "mem", "mem_2", "positions_2", "rel_bias_table", "a_shift_mu_2", "a_decay_bias_2", "a_aaa_bias_2",
         "a_k_k_2", "a_k_a_2", "a_r_k_2", "a_decay_up_2", "a_aaa_up_2", "a_gate_up_2")


def bucket_one_hot():
    dist = 255 - np.arange(384)
    n = np.maximum(dist, 0)
    ratio = np.log(np.maximum(n, 16).astype(np.float32) / np.float32(16)) / np.float32(math.log(8))
    large = np.minimum(16 + (ratio * np.float32(16)).astype(np.int32), 31)
    bucket = np.where(n < 16, n, large)
    hot = (bucket[None, :] == np.arange(33)[:, None]) & (dist >= 0)[None, :]
    hot[32] = dist < 0
    return hot.astype(np.float32)


def triangle_masks():
    r, c = np.arange(P)[:, None], np.arange(P)[None, :]
    masks = [r < c, r <= c, r < c, r <= c, r > c]
    for level in range(7):
        size = 1 << level
        masks.append((r // (2 * size) == c // (2 * size)) & (r // size > c // size))
    masks.append(masks[5].T)
    return np.stack(masks, axis=1).astype(np.float32)


def constants():
    half = 16
    inv_freq = np.power(10000.0, -np.arange(half, dtype=np.float64) / half).astype(np.float32)
    head_of = (np.arange(RW)[:, None] // 64 == np.arange(RW_HEADS)[None, :]).astype(np.float32)
    return {"bucket_one_hot": bucket_one_hot(), "triangle_masks": triangle_masks(), "inv_freq": inv_freq[None, :],
            "head_of": np.ascontiguousarray(head_of.reshape(RWB, P, RW_HEADS).transpose(1, 0, 2)),
            "head_of_t": np.ascontiguousarray(head_of.T)}


def place_unit(unit, spec, arrays):
    if spec[0] == "pair":
        _, names, pair, k0 = spec
        if len(names) == 2:
            gate, up = arrays[names[0]][0], arrays[names[1]][0]
        else:
            gate, up = arrays[names[0]][0][:, :FF], arrays[names[0]][0][:, FF:]
        v = unit.reshape(P, 4, 2, 256)
        for j, w in enumerate((gate, up)):
            v[:, :, j, :] = w[k0 * P:(k0 + 4) * P, 256 * pair:256 * pair + 256].reshape(4, P, 256).transpose(1, 0, 2)
        return
    _, name, k0, nk, c0, width, pitch = spec
    w = arrays[name].reshape(-1, arrays[name].shape[-1])
    v = unit[:, 0:nk * pitch].reshape(P, nk, pitch)
    v[:, :, 0:width] = w[k0 * P:(k0 + nk) * P, c0:c0 + width].reshape(nk, P, width).transpose(1, 0, 2)


FEED_FORWARD_UNITS = 2 * NPAIR + NPAIR
FIRST_UNITS = 2 * (6 + 2) + 2 * (2 + 2 + 2 + 2) + FEED_FORWARD_UNITS
LAYER_A_UNITS = 2 + (2 * 5 + 1) + 4 + FEED_FORWARD_UNITS
LAYER_B_UNITS = 2 + 2 + (2 + 1) + (1 + 1) + 3 + 4 + FEED_FORWARD_UNITS
TOTAL_UNITS = FIRST_UNITS + LAYER_A_UNITS + LAYER_B_UNITS


def kernel(**inputs):
    import concourse.bacc as bacc
    from concourse.bass_utils import run_bass_kernel_spmd

    nc = bacc.Bacc("TRN2", target_bir_lowering=False, num_devices=1)
    host = {n: np.ascontiguousarray(inputs[n]) for n in PLAIN}
    host.update({n: np.ascontiguousarray(inputs[n]).reshape(1, -1) for n in VECTORS})
    host.update(constants())
    for n in ("x", "mem", "mem_2"):
        host[n] = host[n].reshape(S, D)
    for n in ("a_decay_up_2", "a_aaa_up_2", "a_gate_up_2"):
        host[n] = host[n].reshape(host[n].shape[-2:])
    host["a_r_k_2"] = host["a_r_k_2"].reshape(1, RW)
    host["weights"] = np.zeros((TOTAL_UNITS, P, UNIT), np.float32)
    t = {n: nc.dram_tensor("in_" + n, a.shape, mybir.dt.from_np(a.dtype), kind="ExternalInput").ap()
         for n, a in host.items()}
    out = nc.dram_tensor("out", (S, D), F32, kind="ExternalOutput").ap()
    units = build(nc, t, out, TOTAL_UNITS)
    assert len(units) == TOTAL_UNITS, len(units)
    arrays = {n: np.asarray(inputs[n]) for n in STREAMED}
    for u, spec in enumerate(units):
        place_unit(host["weights"][u], spec, arrays)
    r = run_bass_kernel_spmd(nc, [{"in_" + n: a for n, a in host.items()}], core_ids=[0])
    return r.results[0]["out"].reshape(1, S, D)
```

```python
import math

import numpy as np

import concourse.bass as bass
from concourse import mybir

F32 = mybir.dt.float32
F32R = mybir.dt.float32r
I32 = mybir.dt.int32
ACT = mybir.ActivationFunctionType
ALU = mybir.AluOpType
AX = mybir.AxisListType

P = 128
S = 256
NT = S // P
D = 1024
KT = D // P
FF = 2816
NPAIR = FF // 256
KB = 1024
NEG = -1e30
EPS = 1e-6
LNX_EPS = 64e-5
RING = 4
UNIT = 2048
AHEAD = 3
A_HEADS, B_HEADS, MEM_HEADS, RW_HEADS, MLA_HEADS = 8, 4, 4, 12, 12
RW = RW_HEADS * 64
RWB = RW // P
OFFSET = 9
SHB = 20
QK = 96
KAPPA = math.exp(-0.5)
LAMBDA_INIT = 0.8 - 0.6 * math.exp(0.0)


class Token:

    def __init__(self, sem, value, rate=0):
        self.sem, self.value, self.rate = sem, value, rate


class Channels(list):

    def __init__(self):
        super().__init__()
        self.parts, self.rest = {}, None


class Lane:

    def __init__(self, nc, engine, name):
        self.engine, self.sem = engine, nc.alloc_semaphore(name)
        self.count, self.rate, self.round = 0, 0, None
        self.waited = {}

    def wait(self, *tokens):
        for t in tokens:
            if t is None:
                continue
            if isinstance(t, (list, tuple)):
                self.wait(*t)
                continue
            key = (t.sem.name, t.rate)
            if self.waited.get(key, 0) >= t.value:
                continue
            self.waited[key] = t.value
            self.engine.wait_ge(t.sem, t.value if not t.rate else self.round * t.rate + t.value)

    def last(self):
        return Token(self.sem, self.count, self.rate)

    def quiet(self, instruction, *args, after=(), **kw):
        self.wait(after)
        return instruction(*args, **kw)

    def __call__(self, instruction, *args, after=(), **kw):
        self.wait(after)
        instruction(*args, **kw).then_inc(self.sem, 1)
        self.count += 1
        return Token(self.sem, self.count, self.rate)


class Program:
    def __init__(self, nc, t):
        self.nc, self.t = nc, t
        self.PE = Lane(nc, nc.tensor, "pe_done")
        self.V = Lane(nc, nc.vector, "dve_done")
        self.A = Lane(nc, nc.scalar, "act_done")
        self.G = Lane(nc, nc.gpsimd, "pool_done")
        self.SP = Lane(nc, nc.sync, "sp_done")
        self.lanes = (self.PE, self.V, self.A, self.G, self.SP)
        self.loaded = [nc.alloc_semaphore(f"weights_loaded_{s}") for s in range(RING)]
        self.split_done = nc.alloc_semaphore("weights_split")
        self.used = nc.alloc_semaphore("weights_used")
        self.units = []
        self.looping = False
        self.n_split = 0
        self.bank_free = [None] * 8
        self.arena_tensors = 0
        self.gain_free = [None, None]
        self.gain_turn = 0
        self.pending = []

    def sb(self, name, shape, dtype=F32):
        return self.nc.alloc_sbuf_tensor(name, shape, dtype)

    def work(self, name, kb, shape, dtype=F32):
        size = 4 * int(np.prod(shape[1:]))
        assert kb * KB + size <= self.arena_size, (name, kb * KB + size, self.arena_size)
        return self.nc.alloc_sbuf_tensor_at(name, shape, dtype, offset=int(self.arena + kb * KB))

    def ring_token(self, sem, value, rate):
        return Token(sem, value, rate if self.looping else 0)

    def used_token(self, u):
        return self.ring_token(self.used, u + 1, RING)

    def split(self, u):
        s = u % RING
        hi = self.A(self.nc.scalar.activation, self.w_hi[:, s, :], self.w_raw[:, s, :], ACT.Copy,
                    after=(self.ring_token(self.loaded[s], 16 * (u // RING + 1), 16),
                           self.used_token(u - RING) if u >= RING else None))
        self.V.quiet(self.nc.vector.tensor_tensor, self.w_lo[:, s, :], self.w_raw[:, s, :],
                     self.w_hi[:, s, :].bitcast(F32), ALU.subtract, after=(hi,)).then_inc(self.split_done, 1)

    def unit_product(self, spec, k0, nk, nc_, width, first, last, lhs, banks, after=(), channels=()):
        u = len(self.units)
        self.units.append(spec)
        s = u % RING
        def split_up_to(n):
            while self.n_split < n and (self.looping or self.n_split < self.total_units):
                self.split(self.n_split)
                self.n_split += 1
        split_up_to(u + 1)
        pe, mm = self.PE, self.nc.tensor.matmul
        pe.wait(self.ring_token(self.split_done, u + 1, RING), after)
        segs = [(c, min(512, width - c)) for c in range(0, width, 512)]
        tok_done = None
        for tok in range(NT):
            for ch in channels:
                if tok and ch.rest:
                    ch.rest()
                    ch.rest = None
            if tok or not any(ch.rest for ch in channels):
                split_up_to(u + AHEAD)
            steps = [(x, w, k) for x, w in ((0, self.w_hi), (0, self.w_lo), (1, self.w_hi)) for k in range(nk)]
            for n, (x, w, k) in enumerate(steps):
                for ch in channels:
                    pe.wait(ch.parts[tok, (k0 + k) // 4][x])
                for c, cw in segs:
                    o = banks[tok * len(segs) + c // 512]
                    m = mm(o[:, 0:cw], lhs[x][:, k0 + k, tok * P:(tok + 1) * P],
                           w[:, s, k * nc_ + c:k * nc_ + c + cw],
                           start=first and n == 0, stop=last and n == len(steps) - 1)
            if last and tok == 0:
                m.then_inc(pe.sem, 1)
                pe.count += 1
                tok_done = pe.last()
        m.then_inc(self.used, 1)
        return [tok_done, self.used_token(u)]

    def job(self, name, lhs, ready, nk, c0, width, bank_ids, evacuate):
        banks = [self.bank[b] for b in bank_ids]
        pitch = 256 if (width <= 256 and nk == KT) else 512 if width <= 512 else width
        per = min(nk, UNIT // pitch)
        ready = ready if isinstance(ready, (list, tuple)) and not isinstance(ready, Channels) else [ready]
        channels = [r for r in ready if isinstance(r, Channels)]
        for k in range(0, nk, per):
            n = min(per, nk - k)
            after = ([self.bank_free[b] for b in bank_ids],
                     [r for r in ready if not isinstance(r, Channels)]) if k == 0 else ()
            done = self.unit_product(("part", name, k, n, c0, width, pitch), k, n, pitch, width, k == 0, k + n == nk,
                                     lhs, banks, after=after, channels=channels)
            if k + n == nk:
                evacuate(done)
            yield

    def run(self, *jobs):
        for j in jobs:
            for _ in j:
                pass

    def fill(self, units):
        while units > 0 and self.pending:
            try:
                next(self.pending[0])
                units -= 1
            except StopIteration:
                self.pending.pop(0)

    def fill_rest(self):
        self.run(*self.pending)
        self.pending = []

    def rows_of(self, dst, bank_ids, width, into=None):
        def evacuate(done):
            out = []
            for tok in range(NT):
                segs = [(c, min(512, width - c)) for c in range(0, width, 512)]
                for j, (c, w) in enumerate(segs):
                    b = bank_ids[tok * len(segs) + j]
                    t = self.copy(tok, dst(tok)[:, c:c + w], self.bank[b][:, 0:w], (done[tok],))
                    self.bank_free[b] = t
                    out.append(t)
            if into is not None:
                into.extend(out)
        return evacuate

    def loop(self, rounds, body, state):
        before = [lane.count for lane in self.lanes]
        body(0, state)
        grown = [lane.count - b for lane, b in zip(self.lanes, before)]
        rate_of = {lane.sem.name: (lane, g, b) for lane, g, b in zip(self.lanes, grown, before)}
        rate_of[self.used.name] = (None, RING, 0)

        def moved(t, turns):
            if t is None:
                return None
            if isinstance(t, (list, tuple)):
                return [moved(x, turns) for x in t]
            lane, g, b = rate_of[t.sem.name]
            if turns is None:
                return Token(t.sem, t.value, g) if lane is None or t.value > b else t
            return Token(t.sem, t.value + turns * g if t.rate else t.value)

        units, splits = len(self.units), self.n_split
        counts = [lane.count for lane in self.lanes]
        for k in state:
            state[k] = moved(state[k], None)
        self.bank_free = moved(self.bank_free, None)
        self.looping = True
        kept = [dict(lane.waited) for lane in self.lanes]
        with self.nc.Fori(0, rounds - 1) as i:
            for lane, g in zip(self.lanes, grown):
                lane.rate, lane.round = g, i
            body(i + 1, state)
        self.looping = False
        turns = rounds - 2
        for lane, g, c, w in zip(self.lanes, grown, counts, kept):
            assert lane.count - c == g
            lane.count = c + (rounds - 1) * g
            lane.rate, lane.round = 0, None
            lane.waited = w
        for k in state:
            state[k] = moved(state[k], turns)
        self.bank_free = moved(self.bank_free, turns)
        round_units = self.units[units:]
        del self.units[units:]
        for n in range(rounds - 1):
            self.units += [spec[:2] + (spec[2] + 2 * n,) + spec[3:] for spec in round_units]
        self.n_split = splits + (rounds - 1) * RING

    def load_gain(self, name, width=D, parts=1):
        b = self.gain_turn % 2
        self.gain_turn += 1
        sem = self.nc.alloc_semaphore(f"gain_{self.gain_turn}")
        out = self.gains[b][:, 0:width]
        self.G.wait(self.gain_free[b])
        self.nc.gpsimd.dma_start(out, self.t[name].to_broadcast((P, width))).then_inc(sem, 16)
        return out, Token(sem, 16), b

    def inv_rms(self, src, width, eps, ready, out, junk=None):
        if junk is None:
            junk = self.xn
        result = []
        for tok in range(NT):
            a = self.A(self.nc.scalar.activation, junk[:, tok, 0:width], src(tok), ACT.Square,
                       scale=float(width) ** -0.5, accum_out=out[:, tok:tok + 1],
                       after=(ready[tok], self.xn_free, self.rstd_free))
            result.append(self.power(out[:, tok:tok + 1], eps, (a,)))
        return result

    def power(self, ms, eps, ready):
        t = self.G(self.nc.gpsimd.tensor_scalar, ms, ms, eps, None, ALU.add, after=(ready,))
        n = ms.shape[-1]
        return self.G(self.nc.gpsimd.tensor_tensor, ms, ms, self.minus_half[0:ms.shape[0], 0:n], ALU.pow, after=(t,))

    def normalize(self, src, dst, width, gain, rstd, ready, dst_free=None):
        g, g_ready, b = gain
        step = min(width, 512)
        out = []
        for tok in range(NT):
            out.append([self.V(self.nc.vector.scalar_tensor_tensor, out=dst(tok)[:, c:c + step], in0=src(tok)[:, c:c + step],
                               scalar=rstd[:, tok:tok + 1], in1=g[:, c:c + step], op0=ALU.mult, op1=ALU.mult,
                               after=(ready[tok], g_ready, dst_free)) for c in range(0, width, step)])
        self.gain_free[b] = out
        self.rstd_free = out
        return out

    def transposes(self, blocks, ready, evacuate, banks=(4, 5, 6, 7), per=4):
        tokens, n = [], 0
        while n < len(blocks):
            now = blocks[n:n + per]
            b = banks[(n // per) % len(banks)]
            for j, (src, rows) in enumerate(now):
                self.PE.wait(ready, self.bank_free[b])
                m = self.nc.tensor.transpose(self.bank[b][0:rows, j * P:(j + 1) * P], src, self.ident[:, :])
            m.then_inc(self.PE.sem, 1)
            self.PE.count += 1
            done = Token(self.PE.sem, self.PE.count, self.PE.rate)
            read = evacuate(n // per, self.bank[b], done)
            self.bank_free[b] = read
            tokens.append(read)
            n += per
        return tokens

    def copy(self, n, out, in_, after):
        if n % 2:
            return self.A(self.nc.scalar.activation, out, in_, ACT.Copy, after=after)
        return self.V(self.nc.vector.tensor_copy, out, in_, after=after)

    def keep_warm(self, n, bank):
        self.PE.wait(self.bank_free[bank])
        for _ in range(n):
            self.nc.tensor.transpose(self.bank[bank][:, 0:P], self.ident[:, :], self.ident[:, :])

    def to_channels(self, src, nk, hi, lo, ready, free=None, banks=(4, 5, 6, 7), before=None, defer=False):
        out = Channels()
        groups = [(tok, k) for tok in range(NT) for k in range(0, nk, 4)]
        made = {}

        def turn(n, tok, k0):
            if before is not None:
                for g in groups[n:n + 2] if not (defer and n) else groups[n:]:
                    if g not in made:
                        made[g] = before(g[0], g[1] // 4)
            b, m = banks[n % len(banks)], min(4, nk - k0)
            self.PE.wait(ready, made.get((tok, k0)), self.bank_free[b])
            for j in range(m):
                t = self.nc.tensor.transpose(self.bank[b][:, j * P:(j + 1) * P], src(tok, k0 + j), self.ident[:, :])
            t.then_inc(self.PE.sem, 1)
            self.PE.count += 1
            done = self.PE.last()
            view = self.bank[b][:, 0:m * P].rearrange("p (k t) -> p k t", k=m)
            cols = (slice(None), slice(k0, k0 + m), slice(tok * P, (tok + 1) * P))
            h = self.A(self.nc.scalar.activation, hi[cols], view, ACT.Copy, after=(done, free))
            l = self.V(self.nc.vector.tensor_tensor, lo[cols], view, hi[cols].bitcast(F32), ALU.subtract,
                       after=(h, done, free))
            self.bank_free[b] = [h, l]
            out.extend([h, l])
            out.parts[tok, k0 // 4] = (h, l)

        def turn_tiles(of):
            for n, (tok, k0) in enumerate(groups):
                if tok in of:
                    turn(n, tok, k0)
        turn_tiles((0,) if defer else range(NT))
        if defer:
            out.rest = lambda: turn_tiles(range(1, NT))
        return out

    def norm_to_channels(self, x, width, gain, eps, hi, lo, ready, free=None, rstd_ready=None, rows=None, junk=None,
                         banks=(4, 5, 6, 7), defer=False, warm=18):
        if len(ready) != NT:
            ready = [ready] * NT
        r = rstd_ready or self.inv_rms(lambda tok: x[:, tok, 0:width], width, eps, ready, self.rstd, junk)
        self.keep_warm(warm, banks[0])
        g, g_ready, b = gain
        step = min(width, 512)
        norms = []
        xn_free = self.xn_free if rows is None else None
        xn = self.xn if rows is None else rows

        def before(tok, n):
            c = slice(n * step, (n + 1) * step)
            norms.append(self.V(self.nc.vector.scalar_tensor_tensor, out=xn[:, tok, c], in0=x[:, tok, c],
                                scalar=self.rstd[:, tok:tok + 1], in1=g[:, c], op0=ALU.mult, op1=ALU.mult,
                                after=(r[tok], g_ready, xn_free)))
            return norms[-1]
        t = self.to_channels(lambda tok, k: xn[:, tok, k * P:(k + 1) * P], width // P, hi, lo, None, free,
                             banks, before, defer)
        self.gain_free[b] = self.rstd_free = norms
        if rows is None:
            self.xn_free = t
        return t

    def attention(self, heads, stage_qk, spans, scale, bias, v_of, dv, out_of, ready, tag, out_free=None, between=None,
                  combine=None, finish=None):
        nc, PE, V, A = self.nc, self.PE, self.V, self.A
        off = [0, spans[0]]
        total = sum(spans)
        step = 1 if combine is None else 2
        n = len(heads) // step
        st = {}
        e_size = 384 if total == 384 else 512
        self.e_free = [list(self.e_free)] * 4
        e_free, pt_free, l_free = self.e_free, self.pt_free, self.l_free
        outs = []
        ne = 4 if step == 2 else 2

        def logits_and_exp(i):
            st[i] = {"e": [], "exp": []}
            for j in range(step):
                hh = heads[i * step + j]
                b = 4 + hh % 2
                PE.wait(ready, self.bank_free[b])
                q = stage_qk(hh, self.bank[b], spans, off)
                stat = self.stats[:, (i * step + j) % 4, :]
                sf = self.stat_free[(i * step + j) % 4]
                lb = hh % 2
                if bias is not None:
                    L = self.lbuf[:, lb, 0:total]
                    l = V(nc.vector.scalar_tensor_tensor, out=L, in0=self.bank[b][:, 0:total], scalar=scale,
                          in1=bias(hh), op0=ALU.mult, op1=ALU.add, after=(q, l_free[lb], self.bias_ready))
                    self.bank_free[b] = l
                    k = 1.0
                else:
                    L, l, k = self.bank[b][:, 0:total], q, scale
                mx = [V(nc.vector.tensor_reduce, out=stat[:, tok:tok + 1], in_=L[:, off[tok]:off[tok] + spans[tok]],
                        axis=AX.X, op=ALU.max, negate=True, after=(l, sf)) for tok in range(NT)]
                if k != 1.0:
                    mx = V(nc.vector.tensor_scalar, stat[:, 0:2], stat[:, 0:2], k, None, ALU.mult, after=mx)
                slot = (i * step + j) % ne
                E = self.ebuf[:, slot * e_size:slot * e_size + total]
                ex = [A(nc.scalar.activation, E[:, off[tok]:off[tok] + spans[tok]], L[:, off[tok]:off[tok] + spans[tok]],
                        ACT.Exp, bias=stat[:, tok:tok + 1], scale=k, accum_out=stat[:, 2 + tok:3 + tok],
                        after=(mx, l, e_free[slot])) for tok in range(NT)]
                if bias is None:
                    self.bank_free[b] = ex
                else:
                    l_free[lb] = ex
                st[i]["e"].append((E, slot, stat, (i * step + j) % 4))
                st[i]["exp"].append(ex)
            if step == 2:
                scale_weights(i)

        def scale_weights(i):
            E, slot, stat, sn = st[i]["e"][0]
            rc = [V(nc.vector.reciprocal, s_[:, 4:6], s_[:, 2:4], after=(x, self.stat_free[m]))
                  for (_, _, s_, m), x in zip(st[i]["e"], st[i]["exp"])]
            if step == 2:
                E1, slot1, stat1, sn1 = st[i]["e"][1]
                m = V(nc.vector.tensor_scalar, stat1[:, 6:8], stat1[:, 4:6], combine[0], None, ALU.mult,
                      after=(rc, combine[1]))
                rc = []
                for tok in range(NT):
                    a, z = off[tok], off[tok] + spans[tok]
                    f = V(nc.vector.tensor_scalar, E1[:, a:z], E1[:, a:z], stat1[:, 6 + tok:7 + tok], None, ALU.mult,
                          after=(m,))
                    rc.append(V(nc.vector.scalar_tensor_tensor, out=E[:, a:z], in0=E[:, a:z],
                                scalar=stat[:, 4 + tok:5 + tok], in1=E1[:, a:z], op0=ALU.mult, op1=ALU.add, after=(f,)))
                e_free[slot1] = rc
                self.stat_free[sn1] = rc
                self.stat_free[sn] = rc
            st[i]["rc"] = rc

        def weights_transposed(i):
            E, slot, stat, sn = st[i]["e"][0]
            if step == 1:
                scale_weights(i)
            rc = st[i]["rc"]
            blocks = [E[:, c:c + P] for c in range(0, total, P)]
            b = 6 + i % 2
            PE.wait(rc if step == 2 else st[i]["exp"], self.bank_free[b])
            for j, blk in enumerate(blocks):
                m = nc.tensor.transpose(self.bank[b][:, j * P:(j + 1) * P], blk, self.ident[:, :])
            m.then_inc(PE.sem, 1)
            PE.count += 1
            done = Token(PE.sem, PE.count)
            e_free[slot] = done
            pt = self.ptbuf[:, (i % 2) * 512:(i % 2) * 512 + total]
            c = A(nc.scalar.activation, pt, self.bank[b][:, 0:total], ACT.Copy, after=(done, pt_free[i % 2]))
            self.bank_free[b] = c
            st[i].update(pt=pt, copied=c, rc=rc, stat=stat, sn=sn)

        def values(i):
            b = 2 + i % 2
            pt = st[i]["pt"]
            PE.wait(st[i]["copied"], self.bank_free[b])
            for tok in range(NT):
                nb = spans[tok] // P
                for j in range(nb):
                    c = off[tok] + j * P
                    m = nc.tensor.matmul(self.bank[b][:, tok * dv:(tok + 1) * dv], pt[:, c:c + P], v_of(heads[i * step], j),
                                         start=j == 0, stop=j == nb - 1)
            m.then_inc(PE.sem, 1)
            PE.count += 1
            done = Token(PE.sem, PE.count)
            pt_free[i % 2] = done
            view = self.bank[b][:, 0:NT * dv].rearrange("p (t d) -> p t d", t=NT)
            if step == 2:
                o = self.A(nc.scalar.activation, out_of(i), view, ACT.Copy, after=(done, out_free))
            else:
                o = V(nc.vector.tensor_tensor, out_of(i), view,
                      st[i]["stat"][:, 4:6].unsqueeze(2).to_broadcast((P, NT, dv)), ALU.mult,
                      after=(done, st[i]["rc"], out_free))
                self.stat_free[st[i]["sn"]] = o
            self.bank_free[b] = o
            outs.append(o)

        for i in range(n + 2 + (finish is not None)):
            if i < n:
                logits_and_exp(i)
            if 1 <= i <= n:
                weights_transposed(i - 1)
            if 2 <= i < n + 2:
                values(i - 2)
            if finish is not None and i >= 3:
                outs[i - 3] = finish(i - 3, outs[i - 3])
            if between is not None and i < n + 2:
                between(i)
        return outs

    def qk_pairs(self, qT, kT, scale_rows=64):
        def stage(h, bank, spans, off):
            p, blk = 64 * (h % 2), h // 2
            for tok in range(NT):
                m = self.nc.tensor.matmul(bank[:, off[tok]:off[tok] + spans[tok]],
                                          qT[p:p + 64, blk, tok * P:(tok + 1) * P],
                                          kT[p:p + 64, blk, 0:spans[tok]], start=True, stop=True)
            m.then_inc(self.PE.sem, 1)
            self.PE.count += 1
            return Token(self.PE.sem, self.PE.count)
        return stage

    def add_residual(self, done, bank_ids, cols):
        out = []
        for tok, b in enumerate(bank_ids):
            o = self.x[:, tok, cols:cols + 512]
            t = self.V(self.nc.vector.tensor_tensor, o, self.bank[b][:, :], o, ALU.add, after=(done[tok], self.x_free))
            self.bank_free[b] = t
            out.append(t)
        return out

    def project_residual(self, name, lhs, ready, between=None):
        out = []
        for g in range(2):
            if g and between is not None:
                between()
            banks = (2 * g, 2 * g + 1)
            self.run(self.job(name, lhs, ready, KT, 512 * g, 512, banks,
                              lambda done: out.append(self.add_residual(done, banks, 512 * g))))
        self.xt_free = self.used_token(len(self.units) - 1)
        return [[out[g][tok] for g in range(2)] for tok in range(NT)]

    def feed_forward(self, gate_up, down, gain, ready):
        nc, PE, V, A = self.nc, self.PE, self.V, self.A
        n = self.norm_to_channels(self.x, D, gain, EPS, self.XH, self.XL, ready, self.xt_free, defer=True)
        tag = down
        HH = self.work("hidden_hi_" + tag, 24, [P, 2 * NPAIR, S], F32R)
        HL = self.work("hidden_lo_" + tag, 46, [P, 2 * NPAIR, S], F32R)
        act = self.work("silu_" + tag, 69, [P, 2, NT, 256])
        hid = self.work("hidden_" + tag, 73, [P, 2, NT, 256])
        hh = HH[:, :, :].rearrange("p k t -> p (k t)")
        hl = HL[:, :, :].rearrange("p k t -> p (k t)")
        state = {"act0": None, "act1": None, "hid0": None, "hid1": None, "mul0": None, "mul1": None}

        def gate_and_up(p, par):
            banks = (2 * par, 2 * par + 1)
            free = [self.bank_free[b] for b in banks]
            first = self.unit_product(("pair",) + (gate_up, p, 0), 0, 4, 512, 512, True, False, (self.XH, self.XL),
                                      [self.bank[b] for b in banks], after=(free,),
                                      channels=() if self.looping else (n,))
            done = self.unit_product(("pair",) + (gate_up, p, 4), 4, 4, 512, 512, False, True, (self.XH, self.XL),
                                     [self.bank[b] for b in banks], channels=() if self.looping else (n,))
            mul = []
            for tok in range(NT):
                b = banks[tok]
                a = A(nc.scalar.activation, act[:, par, tok, :], self.bank[b][:, 0:256], ACT.Silu,
                      after=(done[tok], state[f"mul{par}"]))
                m = V(nc.vector.tensor_tensor, hid[:, par, tok, :], act[:, par, tok, :], self.bank[b][:, 256:512],
                      ALU.mult, after=(a, done[tok], state[f"hid{par}"]))
                self.bank_free[b] = [a, m]
                mul.append(m)
            state[f"mul{par}"] = mul
            return done

        def hidden_to_channels(at, par):
            b = 4 + par
            PE.wait(state[f"mul{par}"], self.bank_free[b])
            for c in range(2):
                for tok in range(NT):
                    m = nc.tensor.transpose(self.bank[b][:, (2 * c + tok) * P:(2 * c + tok + 1) * P],
                                            hid[:, par, tok, c * P:(c + 1) * P], self.ident[:, :])
            m.then_inc(PE.sem, 1)
            PE.count += 1
            done = Token(PE.sem, PE.count, PE.rate)
            state[f"hid{par}"] = done
            h = A(nc.scalar.activation, hh[:, at], self.bank[b][:, :], ACT.Copy, after=(done,))
            l = V(nc.vector.tensor_tensor, hl[:, at], self.bank[b][:, :], hh[:, at].bitcast(F32), ALU.subtract,
                  after=(done, h))
            self.bank_free[b] = [h, l]
            return [h, l]

        def two_pairs(i, state):
            pair = 1 if self.looping else i
            gate_and_up(2 * pair + 1, 1)
            hidden_to_channels(bass.ds(i * 1024, 512), 0)
            gate_and_up(2 * pair + 2, 0)
            state["last"] = hidden_to_channels(bass.ds(i * 1024 + 512, 512), 1)

        gate_and_up(0, 0)
        self.loop((NPAIR - 1) // 2, two_pairs, state)
        last = hidden_to_channels(bass.ds((NPAIR - 1) * 512, 512), 0)
        self.xt_free = self.used_token(len(self.units) - 1)
        banks = (0, 1, 2, 3)
        free = [self.bank_free[b] for b in banks]
        for u in range(NPAIR):
            done = self.unit_product(("part", down, 2 * u, 2, 0, D, D), 2 * u, 2, D, D, u == 0, u == NPAIR - 1,
                                     (HH, HL), [self.bank[b] for b in banks],
                                     after=(free, state["last"] if u < NPAIR - 1 else last))
        out = []
        for tok in range(NT):
            out.append([])
            for half in range(2):
                b, o = 2 * tok + half, self.x[:, tok, 512 * half:512 * half + 512]
                self.bank_free[b] = self.V(nc.vector.tensor_tensor, o, self.bank[b][:, :], o, ALU.add, after=(done[tok],))
                out[tok].append(self.bank_free[b])
        return out


def build(nc, t, out_dram, total_units):
    p = Program(nc, t)
    PE, V, A, G, SP = p.PE, p.V, p.A, p.G, p.SP
    p.total_units = total_units
    weights = t["weights"]

    ring_at = nc.sbuf_base + (-nc.sbuf_base) % 64
    place = p.sb("ring_place", [P, RING * UNIT + 16])
    p.w_raw = nc.alloc_sbuf_tensor_at("w_raw", [P, RING, UNIT], F32, offset=ring_at)
    p.w_lo = nc.alloc_sbuf_tensor_at("w_lo", [P, RING, UNIT], F32R, offset=ring_at)
    p.w_hi = p.sb("w_hi", [P, RING, UNIT], F32R)
    p.x = p.sb("x", [P, NT, D])
    p.xn = p.sb("xn", [P, NT, D])
    channels_at = nc.sbuf_base + (-nc.sbuf_base) % 64
    p.sb("channels_place", [P, 2 * KT * S + 16])
    p.XH = nc.alloc_sbuf_tensor_at("x_channels_hi", [P, KT, S], F32R, offset=channels_at)
    p.XL = nc.alloc_sbuf_tensor_at("x_channels_lo", [P, KT, S], F32R, offset=channels_at + 4 * KT * S)

    def in_channels_place(name, kb, shape):
        return nc.alloc_sbuf_tensor_at(name, shape, F32, offset=int(channels_at + kb * KB))
    p.gains = [p.sb(f"gain_{b}", [P, D]) for b in range(2)]
    p.ident = p.sb("ident", [P, P])
    p.minus_half = p.sb("minus_half", [P, 16])
    p.cols = p.sb("cols", [P, 64])
    p.rstd = p.sb("rstd", [P, 2])
    p.rstd2 = p.sb("rstd2", [P, 16])
    p.stats = p.sb("stats", [P, 4, 8])
    p.lamb = p.sb("lambda_", [P, 8])
    p.sb_masks = p.sb("triangle_masks", [P, 13, P], mybir.dt.bfloat16)
    p.head_of = p.sb("head_of", [P, RWB, RW_HEADS])
    p.head_rk = p.sb("head_r_k", [P, RWB, RW_HEADS])
    p.mid, p.omk, p.state_factor = p.sb("mid", [P, RWB * NT]), p.sb("one_less_k_a", [P, RWB]), p.sb("state_factor", [P, RWB])
    p.rk_rows, p.gn = p.sb("r_k_rows", [P, NT, RW_HEADS]), p.sb("group_norm", [P, 36])
    p.posi, p.posf, p.freq = p.sb("pos_int", [P, NT], I32), p.sb("pos", [P, NT]), p.sb("freq", [P, 16])
    p.cosr, p.sinr = p.sb("cos", [P, NT, 16]), p.sb("sin", [P, NT, 16])
    arena = nc.sbuf_base + (-nc.sbuf_base) % 64
    p.arena, p.arena_size = arena, nc.sbuf_usable_end - arena
    p.lbuf = p.work("logits", 88, [P, 2, 512])
    p.ebuf = p.work("exps", 92, [P, 3 * 512])[:, :]
    p.ptbuf = p.work("weights_t", 84, [P, 2 * 512])[:, :]
    p.bank = [nc.alloc_psum_tensor(f"bank{b}", [P, 512], F32)[:, :] for b in range(8)]
    p.xn_free = p.xt_free = p.x_free = p.bias_ready = None
    p.e_free, p.pt_free, p.l_free, p.stat_free = [None] * 4, [None] * 2, [None] * 2, [None] * 4
    p.rstd_free = p.gn_free = None

    def load_unit(u, slot, round_=None):
        if round_ is None:
            if u >= RING:
                nc.sync.wait_ge(p.used, u - RING + 1)
            src = weights[u]
        else:
            nc.sync.wait_ge(p.used, round_ * RING + slot + 1)
            src = weights[bass.ds((round_ + 1) * RING + slot, 1)].rearrange("a p n -> (a p) n")
        nc.sync.dma_start(p.w_raw[:, slot, :], src).then_inc(p.loaded[slot], 16)

    io = [nc.alloc_semaphore(f"input_{n}") for n in range(8)]

    def row_major(name):
        return t[name].rearrange("(t p) d -> p t d", p=P)

    nc.sync.dma_start(p.x[:, :, :], row_major("x")).then_inc(io[0], 16)
    x_ready = Token(io[0], 16)
    for u in range(RING):
        load_unit(u, u)
    gain_mix = p.load_gain("mix_norm_g")
    gain_lambda = p.load_gain("diff_lambda", 256)

    def identity(m, rows):
        z = G(nc.gpsimd.memset, m, 0.0)
        return G(nc.gpsimd.affine_select, out=m, in_=m, compare_op=ALU.not_equal, fill=1.0, base=0,
                 pattern=[[-1, P]], channel_multiplier=1, after=(z,))

    ident_ready = identity(p.ident[:, :], P)
    half_ready = G(nc.gpsimd.memset, p.minus_half[:, :], -0.5)
    PE.wait(ident_ready)

    NB, RL, NH = 33, 384, A_HEADS + B_HEADS
    tab = p.work("bias_table", 34, [NB, NH])
    hot = p.work("bias_one_hot", 35, [NB, RL])
    tneg = V(nc.vector.memset, tab[:, :], NEG)
    A.wait(tneg)
    nc.scalar.dma_start(tab[0:NB - 1, :], t["rel_bias_table"]).then_inc(io[3], 16)
    nc.scalar.dma_start(hot[:, :], t["bucket_one_hot"]).then_inc(io[3], 16)
    tab_hi, tab_lo = p.work("bias_table_hi", 34.125, [NB, NH], F32R), p.work("bias_table_lo", 34.25, [NB, NH], F32R)
    hot_r = p.work("bias_one_hot_r", 37, [NB, RL], F32R)
    toep = nc.dram_tensor("bias_rows", (NH, P, RL), F32, kind="Internal").ap()
    line = p.work("bias_lines", 16, [P, NH, RL])
    bias = p.work("bias", 64, [P, NH, 384])

    def read_bias():
        A.wait(lines_written)
        for tile, (lo, n) in enumerate(((P, P), (0, S))):
            skew = bass.AP(toep.tensor, P - 1 + lo, [[RL - 1, P], [P * RL, NH], [1, n]])
            nc.scalar.dma_start(bias[:, :, tile * P:tile * P + n], skew).then_inc(io[5], 16)
        p.bias_ready = Token(io[5], 32)

    with nc.sync.Fori(0, total_units // RING - 1) as i:
        for slot in range(RING):
            load_unit(None, slot, i)
    for u in range(total_units // RING * RING, total_units):
        load_unit(u, u % RING)

    def at_tok(tile_, w=None):
        return lambda tok: tile_[:, tok, :] if w is None else tile_[:, tok, w[0]:w[1]]

    xt = p.norm_to_channels(p.x, D, gain_mix, EPS, p.XH, p.XL, [[x_ready, half_ready]] * NT, defer=True)
    proj = p.work("proj", 40, [P, NT, 6 * 512])
    X = (p.XH, p.XL)

    def in_pair(g, banks, into):
        return p.job("w_in", X, xt, KT, 512 * g, 512, banks,
                     p.rows_of(at_tok(proj, (512 * g, 512 * g + 512)), banks, 512, into))

    def heads_to_channels(src_cols, dst, ready, banks=(4, 5, 6, 7), n_blocks=4, src=None, free=None):
        src = proj if src is None else src
        blocks = [(src[:, tok, src_cols + k * P:src_cols + (k + 1) * P], P) for k in range(n_blocks) for tok in range(NT)]
        turn = [0]

        def evacuate(g, bank, done):
            m = min(2, n_blocks - 2 * g)
            turn[0] += 1
            return p.copy(turn[0], dst[:, 2 * g:2 * g + m, :], bank[:, 0:m * S].rearrange("p (k t) -> p k t", k=m), (done, free))
        return p.transposes(blocks, ready, evacuate, banks)

    qa_rows, va_rows, b_rows = [], [], []
    th = A(nc.scalar.activation, tab_hi[:, :], tab[:, :], ACT.Copy, after=(Token(io[3], 32),))
    A(nc.scalar.activation, hot_r[:, :], hot[:, :], ACT.Copy)
    tab_split = [A.last(), V(nc.vector.tensor_tensor, tab_lo[:, :], tab[:, :], tab_hi[:, :].bitcast(F32), ALU.subtract,
                             after=(th,))]
    pair_0, pair_1 = in_pair(0, (0, 1), qa_rows), in_pair(1, (2, 3), qa_rows)
    next(pair_0)
    line_t = []
    for h in range(NH):
        b = 2 + h % 6
        PE.wait(tab_split, p.bank_free[b])
        nc.tensor.matmul(p.bank[b][:, 0:RL], tab_hi[:, h:h + 1].to_broadcast((NB, P)), hot_r[:, :], start=True, stop=False)
        m = PE(nc.tensor.matmul, p.bank[b][:, 0:RL], tab_lo[:, h:h + 1].to_broadcast((NB, P)), hot_r[:, :], start=False,
               stop=True)
        p.bank_free[b] = p.copy(h, line[:, h, :], p.bank[b][:, 0:RL], (m,))
        line_t.append(p.bank_free[b])
        if h % 4 == 3:
            G.wait(line_t)
            nc.gpsimd.dma_start(toep[h - 3:h + 1, :, :].rearrange("h p r -> p h r"), line[:, h - 3:h + 1, :]).then_inc(io[4], 16)
    lines_written = Token(io[4], 16 * NH // 4)
    p.run(pair_0)
    next(pair_1)
    read_bias()
    p.run(pair_1)
    mem1 = p.work("mem_rows", 16, [P, NT, D])
    G.wait(lines_written)
    G.wait(p.bias_ready)
    nc.gpsimd.dma_start(mem1[:, :, :], row_major("mem")).then_inc(io[1], 16)
    mem1_ready = Token(io[1], 16)

    wide_masks = p.work("wide_masks", 0, [P, 13, P])
    for dst, name in ((wide_masks[:, :, :], "triangle_masks"), (p.head_of[:, :, :], "head_of")):
        nc.gpsimd.dma_start(dst, t[name]).then_inc(io[7], 16)
    nc.gpsimd.dma_start(p.freq[:, :], t["inv_freq"].to_broadcast((P, 16))).then_inc(io[7], 16)
    nc.gpsimd.dma_start(p.posi[:, :], t["positions_2"].rearrange("a (t p) -> p (a t)", p=P),
                        allow_slow_non_contiguous=True).then_inc(io[7], 16)
    const_ready = pos_ready = Token(io[7], 64)

    rows = p.work("vector_rows", 7, [P, P])
    col_of, n_rows, loads = {}, 0, 0
    for name, width in (("a_shift_mu_2", SHB * P), ("a_decay_bias_2", RW), ("a_aaa_bias_2", RW), ("a_k_k_2", RW),
                        ("a_k_a_2", RW), ("a_r_k_2", RW)):
        n = width // P
        nc.gpsimd.dma_start(rows[n_rows:n_rows + n, :], t[name].rearrange("a (n p) -> (a n) p", p=P)).then_inc(io[2], 16)
        col_of[name] = n_rows
        n_rows += n
        loads += 16
    masks_ready = cols_ready = None

    def turn_constants():
        nonlocal masks_ready, cols_ready
        masks_ready = V(nc.vector.tensor_copy, p.sb_masks[:, :, :], wide_masks[:, :, :], after=(const_ready,))
        cols_t = PE(nc.tensor.transpose, p.bank[7][:, 0:n_rows], rows[0:n_rows, :], p.ident[0:n_rows, 0:n_rows],
                    after=(Token(io[2], loads), p.bank_free[7]))
        cols_ready = V(nc.vector.tensor_copy, p.cols[:, 0:n_rows], p.bank[7][:, 0:n_rows], after=(cols_t,))
        p.bank_free[7] = cols_ready

    def col(name, b):
        return p.cols[:, col_of[name] + b:col_of[name] + b + 1]


    lg, lg_ready, lgb = gain_lambda
    lv = lg.rearrange("p (a b d) -> p a b d", a=2, b=2)
    lprod = p.work("lambda_product", 7.5, [P, 2, 64])
    a1 = V(nc.vector.tensor_tensor, lprod[:, :, :], lv[:, :, 0, :], lv[:, :, 1, :], ALU.mult, after=(lg_ready,))
    p.gain_free[lgb] = a1
    a2 = V(nc.vector.tensor_reduce, out=p.lamb[:, 0:2], in_=lprod[:, :, :], axis=AX.X, op=ALU.add, after=(a1,))
    a3 = A(nc.scalar.activation, p.lamb[:, 2:4], p.lamb[:, 0:2], ACT.Exp, after=(a2,))
    a4 = V(nc.vector.tensor_tensor, p.lamb[:, 4:5], p.lamb[:, 3:4], p.lamb[:, 2:3], ALU.subtract, after=(a3,))
    lam_ready = V(nc.vector.tensor_scalar, p.lamb[:, 5:6], p.lamb[:, 4:5], -LAMBDA_INIT, None, ALU.add, after=(a4,))

    gain_moba, gain_mem = p.load_gain("moba_out_g", 512), p.load_gain("mem_norm_g")
    p.run(in_pair(2, (0, 1), va_rows))
    qT, kT = p.work("qT", 8, [P, 4, S]), p.work("kT", 12, [P, 4, S])
    qk = heads_to_channels(0, qT, qa_rows) + heads_to_channels(512, kT, qa_rows)
    MH, ML = p.work("mem_channels_hi", 24, [P, KT, S], F32R), p.work("mem_channels_lo", 32, [P, KT, S], F32R)
    cross_v = p.work("cross_v", 16, [P, NT, D])
    mem_squares = p.work("mem_squares", 0, [P, NT, D])
    M, mt, ck_rows, cv_rows, mem_rstd, mem_rows = (MH, ML), Channels(), [], [], [], []
    p.pending = [in_pair(g, (0, 1), b_rows) for g in (3, 4, 5)]
    p.pending += [p.job("w_ck", M, mt, KT, 512 * g, 512, (0, 1),
                        p.rows_of(at_tok(proj, (512 * g, 512 * g + 512)), (0, 1), 512, ck_rows)) for g in range(2)]
    p.pending += [p.job("w_cv", M, mt, KT, 512 * g, 512, (0, 1),
                        p.rows_of(at_tok(cross_v, (512 * g, 512 * g + 512)), (0, 1), 512, cv_rows)) for g in range(2)]

    def beside_a(i):
        mem_in = [[mem1_ready, masks_ready, cols_ready, lam_ready]] * NT
        if i == 1:
            turn_constants()
        if i == 2:
            mem_rstd.extend(p.inv_rms(lambda tok: mem1[:, tok, :], D, EPS, mem_in, p.rstd, junk=mem_squares))
        if i == 4:
            made = p.to_channels(lambda tok, k: mem1[:, tok, k * P:(k + 1) * P], KT, MH, ML, mem_rows, banks=(0, 1))
            mt.extend(made)
            mt.parts.update(made.parts)
        if i < A_HEADS:
            p.fill(1)
        if i == 3:
            mem_rows.extend(p.normalize(lambda tok: mem1[:, tok, :], lambda tok: mem1[:, tok, :], D, gain_mem, p.rstd, mem_rstd))

    oa_rows = p.attention(list(range(A_HEADS)), p.qk_pairs(qT, kT), (P, S), 0.125, lambda h: bias[:, h, :],
                          lambda h, j: proj[:, j, 1024 + 64 * h:1088 + 64 * h], 64,
                          lambda i: p.xn[:, :, 64 * i:64 * i + 64], [qk, va_rows], "a", out_free=p.xn_free, between=beside_a)
    p.xt_free = p.used_token(len(p.units) - 1)

    qk = heads_to_channels(1536, qT, b_rows) + heads_to_channels(2048, kT, b_rows)
    later, oa = {}, []

    def beside_b(i):
        if i == 0:
            r = p.inv_rms(lambda tok: p.xn[:, tok, 0:512], 512, EPS, [oa_rows] * NT, p.rstd, junk=mem_squares)
            oa.extend(p.normalize(lambda tok: p.xn[:, tok, 0:512], lambda tok: p.xn[:, tok, 0:512], 512, gain_moba, p.rstd,
                                  [(r[tok], oa_rows) for tok in range(NT)]))
            later["sub"], later["cross"] = p.load_gain("diff_subln_g", P), p.load_gain("cross_norm_g")
        p.fill(1)

    def head_norm(i, o):
        g, g_ready, gb = later["sub"]
        out = []
        for tok in range(NT):
            rows, ms = p.xn[:, tok, 512 + P * i:640 + P * i], p.rstd2[:, 2 * i + tok:2 * i + tok + 1]
            b1 = A(nc.scalar.activation, mem_squares[:, tok, 512 + P * i:640 + P * i], rows, ACT.Square, scale=float(P) ** -0.5, accum_out=ms,
                   after=(o, mt))
            b2 = G(nc.gpsimd.tensor_scalar, ms, ms, EPS, (1.0 - LAMBDA_INIT) ** -2, ALU.add, ALU.mult, after=(b1,))
            b3 = G(nc.gpsimd.tensor_tensor, ms, ms, p.minus_half[:, 0:1], ALU.pow, after=(b2,))
            out.append(V(nc.vector.scalar_tensor_tensor, out=rows, in0=rows, scalar=ms, in1=g, op0=ALU.mult, op1=ALU.mult,
                         after=(b3, g_ready)))
        p.gain_free[gb] = out
        return out

    ob = p.attention(list(range(2 * B_HEADS)), p.qk_pairs(qT, kT), (P, S), 0.125, lambda h: bias[:, A_HEADS + h // 2, :],
                     lambda h, j: proj[:, j, 2560 + 64 * h:2688 + 64 * h], P,
                     lambda i: p.xn[:, :, 512 + P * i:640 + P * i], [qk], "b", between=beside_b,
                     combine=(p.lamb[:, 5:6], lam_ready), finish=head_norm)
    gain_cross = later["cross"]
    p.fill_rest()
    gain_mem2 = p.load_gain("mem_norm_g_2")
    mem2, mem2_squares = p.work("mem2_rows", 56, [P, NT, D]), p.work("mem2_squares", 44, [P, NT, D])
    G.wait(PE.last(), V.last(), A.last())
    nc.gpsimd.dma_start(mem2[:, :, :], row_major("mem_2")).then_inc(io[6], 16)
    m2 = Channels()

    def second_memory():
        made = p.norm_to_channels(mem2, D, gain_mem2, EPS, MH, ML, [[Token(io[6], 16)]] * NT, rows=mem2, junk=mem2_squares, warm=0)
        m2.extend(made)
        m2.parts.update(made.parts)

    mixed = p.to_channels(lambda tok, k: p.xn[:, tok, k * P:(k + 1) * P], KT, p.XH, p.XL, (oa, ob), p.xt_free,
                          defer=True)
    p.xn_free = mixed
    x_done = p.project_residual("w_out", X, mixed, between=second_memory)

    cross_kT = p.work("cross_kT", 8, [P, KT, S])
    ckT = heads_to_channels(0, cross_kT, ck_rows, n_blocks=8, free=PE.last())
    xt = p.norm_to_channels(p.x, D, gain_cross, EPS, p.XH, p.XL, x_done, p.xt_free, defer=True)
    gain_ffn = p.load_gain("ffn_norm_g")
    cq, cqT = p.work("cross_q", 40, [P, NT, D]), p.work("cross_qT", 48, [P, KT, S])
    cq_rows = []
    for g in range(2):
        p.run(p.job("w_cq", X, [xt, ckT], KT, 512 * g, 512, (2 * g, 2 * g + 1),
                    p.rows_of(at_tok(cq, (512 * g, 512 * g + 512)), (2 * g, 2 * g + 1), 512, cq_rows)))
    p.xt_free = p.used_token(len(p.units) - 1)
    qT2 = heads_to_channels(0, cqT, cq_rows, n_blocks=8, src=cq)

    mem_kT = [p.work(f"mem_kT_{n}", 4 * n, [P, 2, S]) for n in range(2)]
    mem_v = [p.work(f"mem_v_{n}", 4 * n + 2, [P, NT, S]) for n in range(2)]
    mk_rows = [p.work(f"mem_k_rows_{n}", 64 + 2 * n, [P, NT, S]) for n in range(2)]
    mem_ready = [[], []]

    def mem_kv(n, name):
        def evacuate(done):
            for tok in range(NT):
                a = A(nc.scalar.activation, mk_rows[n][:, tok, :], p.bank[tok][:, 0:256], ACT.Copy, after=(done[tok],))
                v = V(nc.vector.tensor_copy, mem_v[n][:, tok, :], p.bank[tok][:, 256:512], after=(done[tok], a))
                p.bank_free[tok] = [a, v]
                mem_ready[n] += [a, v]
        return p.job(name, M, m2, KT, 0, 512, (0, 1), evacuate)

    p.pending = [mem_kv(0, "a_mem_kv_2"), mem_kv(1, "b_mem_kv_2")]

    def qk_cross(h, bank, spans, off):
        for tok in range(NT):
            for k in range(2):
                m = nc.tensor.matmul(bank[:, off[tok]:off[tok] + S], cqT[:, 2 * h + k, tok * P:(tok + 1) * P],
                                     cross_kT[:, 2 * h + k, :], start=k == 0, stop=k == 1)
        m.then_inc(PE.sem, 1)
        PE.count += 1
        return Token(PE.sem, PE.count)

    oc = p.attention(list(range(MEM_HEADS)), qk_cross, (S, S), 0.0625, None,
                     lambda h, j: cross_v[:, j, 256 * h:256 * h + 256], 256, lambda i: p.xn[:, :, 256 * i:256 * i + 256],
                     [qT2, ckT, cv_rows], "c", out_free=p.xn_free, between=lambda i: p.fill(1))
    p.fill_rest()
    xt = p.to_channels(lambda tok, k: p.xn[:, tok, k * P:(k + 1) * P], KT, p.XH, p.XL, oc, p.xt_free, defer=True)
    p.xn_free = xt
    for n in range(2):
        mem_ready[n] += heads_to_channels(0, mem_kT[n], mem_ready[n], n_blocks=2, src=mk_rows[n])
    x_done = p.project_residual("w_co", X, xt)

    x_done = p.feed_forward(("w_gate", "w_up"), "w_down", gain_ffn, x_done)
    gain_final, gain_n1 = p.load_gain("final_norm_g"), p.load_gain("a_norm1_g_2")
    r = p.inv_rms(lambda tok: p.x[:, tok, :], D, EPS, x_done, p.rstd)
    x_done = p.normalize(lambda tok: p.x[:, tok, :], lambda tok: p.x[:, tok, :], D, gain_final, p.rstd, r)

    n1 = p.norm_to_channels(p.x, D, gain_n1, EPS, p.XH, p.XL, x_done, p.xt_free, defer=True, warm=40)
    gain_lnx_g, gain_lnx_b = p.load_gain("a_lnx_g_2", RW), p.load_gain("a_lnx_b_2", RW)
    decay_up = p.work("decay_up", 76.625, [64, RW])
    aaa_up = p.work("aaa_up", 76.625, [P, RW])
    gate_up = p.work("gate_up", 79.625, [P, RW])
    head_of_t = p.work("head_of_t", 94.5, [RW_HEADS, RW])
    lora = nc.alloc_semaphore("lora_weights")
    G.wait(PE.last(), V.last(), A.last())
    for dst, name in ((decay_up[:, :], "a_decay_up_2"), (aaa_up[64:P, :], "a_aaa_up_2"), (gate_up[:, :], "a_gate_up_2"),
                      (head_of_t[:, :], "head_of_t")):
        nc.gpsimd.dma_start(dst, t[name]).then_inc(lora, 16)
    lora_ready = Token(lora, 64)
    proj2 = p.work("proj2", 8, [P, NT, 2816])
    raw = p.work("raw_channels", 30, [P, SHB, S + 1])
    sh = p.work("shifted", 50.25, [P, SHB, S])
    qmT = p.work("memory_queries", 23, [P, 2, S])
    raw0 = G(nc.gpsimd.memset, raw[:, :, 0:1], 0.0, after=(PE.last(), V.last(), A.last()))
    shifted = [None] * SHB
    qm_ready = []

    def shift_columns(g, rows):
        blocks = list(range(4 * g, min(4 * g + 4, 22)))

        def evacuate(n, bank, done):
            b0 = blocks[2 * n]
            view = bank[:, :].rearrange("p (k t) -> p k t", k=2)
            if b0 >= SHB:
                t = A(nc.scalar.activation, qmT[:, :, :], view, ACT.Copy, after=(done,))
                qm_ready.append(t)
                return t
            t = A(nc.scalar.activation, raw[:, b0:b0 + 2, 1:S + 1], view, ACT.Copy, after=(done,))
            d = V(nc.vector.tensor_tensor, sh[:, b0:b0 + 2, :], raw[:, b0:b0 + 2, 0:S], raw[:, b0:b0 + 2, 1:S + 1],
                  ALU.subtract, after=(t, raw0))
            for b in (b0, b0 + 1):
                shifted[b] = V(nc.vector.scalar_tensor_tensor, out=sh[:, b, :], in0=sh[:, b, :], scalar=col("a_shift_mu_2", b),
                               in1=raw[:, b, 1:S + 1], op0=ALU.mult, op1=ALU.add, after=(d, cols_ready))
            return t
        p.transposes([(proj2[:, tok, b * P:(b + 1) * P], P) for b in blocks for tok in range(NT)], rows, evacuate)

    last_rows = None
    for g in range(6):
        rows, width = [], 512 if g < 5 else 256
        banks = (2 * (g % 2), 2 * (g % 2) + 1)
        p.run(p.job("a_w_in_2", X, n1, KT, 512 * g, width, banks,
                    p.rows_of(at_tok(proj2, (512 * g, 512 * g + width)), banks, width, rows)))
        if g:
            shift_columns(g - 1, last_rows)
        last_rows = rows
    shift_columns(5, last_rows)
    p.xt_free = p.used_token(len(p.units) - 1)

    def memory_attention(n, qT_, ready, tag, between=None):
        return p.attention(list(range(MEM_HEADS)), p.qk_pairs(qT_, mem_kT[n]), (S, S), 0.125, None,
                           lambda h, j: mem_v[n][:, j, 64 * h:64 * h + 64], 64,
                           lambda i: p.xn[:, :, RW + 64 * i:RW + 64 * i + 64], [ready, mem_ready[n]], tag, out_free=p.xn_free,
                           between=between)

    masks = p.sb_masks
    rB, kB, vB = (sh[:, RWB * n:RWB * (n + 1), :] for n in range(3))
    sig = p.work("decay_sigmoid", 44, [P, RWB, S])
    lr = p.work("learning_rate", 38, [P, RWB, S])
    kk = p.work("removal_key", 32, [P, RWB, S])
    sqk = in_channels_place("removal_key_squares", 0, [P, RWB, S])
    cs = p.work("cumulated", 70.5, [P, RWB, NT, P + 1])
    down_ = p.work("decay_down", 76.625, [P, RWB, NT, P + 1])
    up_ = in_channels_place("decay_up_exp", 6, [P, RWB, NT, P + 1])
    ones_c = in_channels_place("ones_row", 12.25, [P, P])
    nrm = in_channels_place("inverse_norms", 13, [RW_HEADS, S])
    mid = p.mid
    raw_dead = list(shifted)
    channels_free = [p.xt_free]

    def per_channel(name):
        return p.cols[:, col_of[name]:col_of[name] + RWB].unsqueeze(2).to_broadcast((P, RWB, S))

    def by_chunk(a):
        return a.rearrange("p b (c t) -> p (b c) t", c=NT)

    td = A(nc.scalar.activation, sh[0:64, 18, :], sh[0:64, 18, :], ACT.Tanh, after=(shifted[18],))
    sg = A(nc.scalar.activation, sh[:, 19, :], sh[:, 19, :], ACT.Sigmoid, after=(shifted[19],))
    k1 = V(nc.vector.tensor_tensor, kk[:, :, :], kB, per_channel("a_k_k_2"), ALU.mult, after=(shifted,))
    cs0 = G(nc.gpsimd.memset, cs[:, :, :, 0:1], 0.0)
    on = G(nc.gpsimd.memset, ones_c[:, :], 1.0, after=channels_free)

    def upward(rows0, w, out, bias_name, bank, b):
        m = PE(nc.tensor.matmul, p.bank[bank][:, 0:S], w[rows0:rows0 + 64, b * P:(b + 1) * P], sh[rows0:rows0 + 64, 18, :],
               start=True, stop=True, after=(lora_ready, td, shifted[18], p.bank_free[bank]))
        p.bank_free[bank] = A(nc.scalar.activation, out[:, b, :], p.bank[bank][:, 0:S], ACT.Sigmoid,
                              bias=col(bias_name, b), after=(m, raw_dead, cols_ready))
        return p.bank_free[bank]

    sig_t = [upward(0, decay_up, sig, "a_decay_bias_2", 4 + b % 2, b) for b in range(RWB)]
    scans = [V(nc.vector.tensor_tensor_scan, out=cs[:, b, c, 1:P + 1], data0=ones_c[:, :], data1=sig[:, b, c * P:(c + 1) * P],
               initial=0.0, op0=ALU.mult, op1=ALU.add, after=(sig_t[b], on)) for b in range(RWB) for c in range(NT)]
    k2 = A(nc.scalar.activation, sqk[:, :, :], kk[:, :, :], ACT.Square, after=(k1, channels_free))
    lr_t = [upward(64, aaa_up, lr, "a_aaa_bias_2", 6 + b % 2, b) for b in range(RWB)]
    for b in range(RWB):
        PE.wait(k2, p.bank_free[0], const_ready)
        m = nc.tensor.matmul(p.bank[0][0:RW_HEADS, 0:S], p.head_of[:, b, :], sqk[:, b, :], start=b == 0, stop=b == RWB - 1)
    m.then_inc(PE.sem, 1)
    PE.count += 1
    squares_summed = PE.last()
    k3 = V(nc.vector.tensor_scalar, nrm[:, :], p.bank[0][0:RW_HEADS, 0:S], 1e-24, None, ALU.max, after=(PE.last(), channels_free))
    p.bank_free[0] = k3
    k4 = A(nc.scalar.activation, nrm[:, :], nrm[:, :], ACT.Sqrt, after=(k3,))
    csf = cs[:, :, :, :].rearrange("p b c t -> p (b c) t")
    md = V(nc.vector.tensor_copy, mid[:, :], csf[:, :, 64:65].rearrange("p n o -> p (n o)"), after=(scans,))
    k4 = V(nc.vector.reciprocal, nrm[:, :], nrm[:, :], after=(k4,))
    cm = V(nc.vector.tensor_tensor, csf, csf, mid[:, :].unsqueeze(2).to_broadcast((P, RWB * NT, P + 1)), ALU.subtract,
           after=(md, cs0))

    gate = p.work("gate", 17, [P, NT, RW])
    gate_t = []
    for tok in range(NT):
        for j, (c, w) in enumerate(((0, 512), (512, 256))):
            b = 2 * tok + j
            m = PE(nc.tensor.matmul, p.bank[b][:, 0:w], sh[:, 19, tok * P:(tok + 1) * P], gate_up[:, c:c + w], start=True,
                   stop=True, after=(lora_ready, sg, p.bank_free[b]))
            a = A(nc.scalar.activation, gate[:, tok, c:c + w], p.bank[b][:, 0:w], ACT.Copy, after=(m,))
            p.bank_free[b] = a
            gate_t.append(a)
    td_used = PE.last()
    e1 = A(nc.scalar.activation, down_[:, :, :, :], cs[:, :, :, :], ACT.Exp, scale=-KAPPA, after=(cm, td_used))
    e2 = A(nc.scalar.activation, up_[:, :, :, :], cs[:, :, :, :], ACT.Exp, scale=KAPPA, after=(cm, channels_free))

    kkn = []
    for n in range(3):
        b = 1 + n
        PE.wait(k4, p.bank_free[b])
        for j in range(2):
            m = nc.tensor.matmul(p.bank[b][:, j * S:(j + 1) * S], head_of_t[:, (2 * n + j) * P:(2 * n + j + 1) * P], nrm[:, :],
                                 start=True, stop=True)
        m.then_inc(PE.sem, 1)
        PE.count += 1
        k = kk[:, 2 * n:2 * n + 2, :].rearrange("p k t -> p (k t)")
        o = V(nc.vector.scalar_tensor_tensor, out=k, in0=k, scalar=-1.0, in1=p.bank[b][:, :], op0=ALU.mult, op1=ALU.mult,
              after=(PE.last(), k2))
        p.bank_free[b] = o
        kkn.append(o)

    v_rows = p.work("v_rows", 23, [P, NT, RW])

    def rows_back(dst, blocks_of, ready, free=None, banks=(4, 5, 6, 7)):
        def evacuate(n, bank, done):
            w = min(4, RWB - 4 * n) * P
            return p.copy(n, dst[:, 512 * n:512 * n + w], bank[:, 0:w], (done, free))
        return p.transposes([(blocks_of(b), P) for b in range(RWB)], ready, evacuate, banks)

    ar = p.work("a_and_r", 62.5, [P, RWB, NT, 2, P])
    fac = in_channels_place("key_factor", 0, [P, RWB, S])
    rk = in_channels_place("r_k", 0, [P, RWB, S])
    bt, kt = kk, lr
    tok_ = {}

    def key_factor():
        omk = V(nc.vector.tensor_scalar, p.omk[:, :], p.cols[:, col_of["a_k_a_2"]:col_of["a_k_a_2"] + RWB], -1.0, 1.0,
                ALU.mult, ALU.add, after=(cols_ready,))
        kf = [V(nc.vector.tensor_scalar, fac[:, b, :], lr[:, b, :], col("a_k_a_2", b), p.omk[:, b:b + 1], ALU.mult, ALU.add,
                after=(lr_t[b], omk, squares_summed)) for b in range(RWB)]
        tok_["b1"] = G(nc.gpsimd.tensor_tensor, lr[:, :, :], kk[:, :, :], lr[:, :, :], ALU.mult, after=(kf, kkn))
        tok_["kn"] = V(nc.vector.tensor_tensor, kB, kB, fac[:, :, :], ALU.mult, after=(kf, k1))

    def r_times_k():
        tok_["rcol"] = V(nc.vector.tensor_tensor, p.head_rk[:, :, :], p.head_of[:, :, :],
                         p.cols[:, col_of["a_r_k_2"]:col_of["a_r_k_2"] + RWB].unsqueeze(2).to_broadcast((P, RWB, RW_HEADS)),
                         ALU.mult, after=(cols_ready, const_ready))
        tok_["r1"] = V(nc.vector.tensor_tensor, rk[:, :, :], rB, kB, ALU.mult, after=(tok_["kn"], shifted[0:6]))

    pieces = [key_factor, r_times_k]
    ma = memory_attention(0, qmT, qm_ready, "m0", between=lambda i: pieces[i]() if i < len(pieces) else None)
    after_ma = [PE.last(), V.last(), A.last()]
    kn, r1, rcol = tok_["kn"], tok_["r1"], tok_["rcol"]
    v_t = []
    for tok in range(NT):
        v_t += rows_back(v_rows[:, tok, :], lambda b: vB[:, b, tok * P:(tok + 1) * P], shifted[12:18], after_ma)

    def each(a, q):
        return a[:, :, :, q, :].rearrange("p b c t -> p (b c) t")

    downf, upf = (z[:, :, :, :].rearrange("p b c t -> p (b c) t") for z in (down_, up_))
    o1 = V(nc.vector.tensor_tensor, each(ar, 0), by_chunk(kk[:, :, :]), downf[:, :, 0:P], ALU.mult,
           after=(e1, e2, kkn, v_t, td_used))
    o3 = V(nc.vector.scalar_tensor_tensor, out=by_chunk(bt[:, :, :]), in0=by_chunk(lr[:, :, :]), scalar=-1.0,
           in1=upf[:, :, 1:P + 1], op0=ALU.mult, op1=ALU.mult, after=(e2, tok_["b1"], o1))
    o4_ = V(nc.vector.tensor_tensor, by_chunk(kt[:, :, :]), by_chunk(kB), upf[:, :, 1:P + 1], ALU.mult, after=(e2, o3, r1))
    for c in range(NT):
        PE.wait(r1, rcol, p.bank_free[0])
        for b in range(RWB):
            m = nc.tensor.matmul(p.bank[0][:, c * 16:c * 16 + RW_HEADS], rk[:, b, c * P:(c + 1) * P], p.head_rk[:, b, :],
                                 start=b == 0, stop=b == RWB - 1)
    m.then_inc(PE.sem, 1)
    PE.count += 1
    rk_t = A(nc.scalar.activation, p.rk_rows[:, :, :],
             p.bank[0][:, 0:32].rearrange("p (c h) -> p c h", c=2)[:, :, 0:RW_HEADS], ACT.Copy, after=(PE.last(),))
    p.bank_free[0] = rk_t
    bt_rows, kt_rows = p.work("b_rows", 8, [P, RW]), p.work("k_rows", 11, [P, RW])
    o2 = V(nc.vector.tensor_tensor, each(ar, 1), by_chunk(rB), downf[:, :, 1:P + 1], ALU.mult,
           after=(e1, e2, r1, v_t, td_used, o4_))
    sf = V(nc.vector.tensor_tensor, p.state_factor[:, :], down_[:, :, 0, P:P + 1].rearrange("p b o -> p (b o)"),
           up_[:, :, 1, 0:1].rearrange("p b o -> p (b o)"), ALU.mult, after=(e1, e2))
    bk_t = rows_back(bt_rows[:, :], lambda b: bt[:, b, 0:P], o3, free=td_used)
    bk_t += rows_back(kt_rows[:, :], lambda b: kt[:, b, 0:P], o4_, free=td_used)

    y = p.work("y", 76.625, [P, NT, RW])
    state = p.work("state", 82.75, [P, RWB, 64])
    dead = [o1, o2, o3, o4_, sf, bk_t, after_ma]
    sets = []
    for n in range(2):
        at = ((44, 52, 54, 56, 58), (89, 60, 14, 29.5, 74.5))[n]
        sets.append(dict(
            lt=p.work(f"upper_{n}", at[0], [P, 4, 4, P]), lab=p.work(f"lab_{n}", at[1], [P, 4, P]),
            x=p.work(f"inverse_{n}", at[2], [P, 4, P]), xt=p.work(f"inverse_t_{n}", at[3], [P, 4, P]),
            w=p.work(f"step_{n}", at[4], [P, 4, P]),
            r=p.work(f"rhs_{n}", 84.5 + 2 * n, [P, 4, 64]), u=p.work(f"u_{n}", 85.5 + 2 * n, [P, 4, 64]), n=n, free=dead))
    state_t = [None] * RWB

    def mask(i):
        return masks[:, i, :].unsqueeze(1).to_broadcast((P, 4, P))

    def counted(m):
        m.then_inc(PE.sem, 1)
        PE.count += 1
        return PE.last()

    def triangles(q, c, g):
        base = 4 * q["n"]
        done = []
        for i in range(4):
            h = 4 * g + i
            par, blk, b = 64 * (h % 2), h // 2, base + h % 2
            rhs = ar[par:par + 64, blk, c, :, :].rearrange("p a t -> p (a t)")
            PE.wait(dead, p.bank_free[b])
            for j, lhs in enumerate((bt, kt)):
                m = nc.tensor.matmul(p.bank[b][:, 256 * j:256 * j + 256], lhs[par:par + 64, blk, c * P:(c + 1) * P], rhs,
                                     start=True, stop=True)
            m = counted(m)
            v = V(nc.vector.tensor_tensor, q["lt"][:, i, :, :], p.bank[b][:, :].rearrange("p (k t) -> p k t", k=4),
                  masks[:, 0:4, :], ALU.mult, after=(m, q["free"], masks_ready))
            p.bank_free[b] = v
            done.append(v)
            if i == 1:
                yield
        yield
        for par in range(2):
            b = base + 2 + par
            PE.wait(p.bank_free[b])
            for j in range(2):
                blk, r0 = 2 * g + j, 64 * par
                m = nc.tensor.matmul(p.bank[b][:, j * P:(j + 1) * P], ar[r0:r0 + 64, blk, c, 0, :],
                                     bt[r0:r0 + 64, blk, c * P:(c + 1) * P], start=True, stop=True)
            m = counted(m)
            v = V(nc.vector.tensor_tensor, q["lab"][:, par::2, :], p.bank[b][:, 0:256].rearrange("p (k t) -> p k t", k=2),
                  masks[:, 4:5, :].to_broadcast((P, 2, P)), ALU.mult, after=(m, q["free"]))
            p.bank_free[b] = v
            done.append(v)
        q["tri"] = done
        ib = p.ident[:, :].unsqueeze(1).to_broadcast((P, 4, P))
        a = V(nc.vector.tensor_tensor, q["x"][:, :, :], q["lab"][:, :, :], mask(5), ALU.mult, after=done)
        b_ = G(nc.gpsimd.tensor_tensor, q["xt"][:, :, :], q["lt"][:, :, 0, :], mask(12), ALU.mult, after=done)
        a = V(nc.vector.tensor_tensor, q["x"][:, :, :], q["x"][:, :, :], ib, ALU.add, after=(a,))
        b_ = G(nc.gpsimd.tensor_tensor, q["xt"][:, :, :], q["xt"][:, :, :], ib, ALU.add, after=(b_,))
        q["x_t"], q["xt_t"] = a, b_

    def double_first(q, level):
        b = 4 * q["n"]
        PE.wait(q["x_t"], q["tri"], p.bank_free[b])
        for i in range(4):
            m = nc.tensor.matmul(p.bank[b][:, i * P:(i + 1) * P], q["lt"][:, i, 0, :], q["x"][:, i, :], start=True, stop=True)
        m = counted(m)
        q["w_t"] = V(nc.vector.tensor_tensor, q["w"][:, :, :], p.bank[b][:, :].rearrange("p (k t) -> p k t", k=4),
                     mask(5 + level), ALU.mult, after=(m, q["x_t"], q["xt_t"]))
        p.bank_free[b] = q["w_t"]

    def double_second(q, level):
        b = 4 * q["n"] + 1
        last = level == 6
        PE.wait(q["w_t"], q["xt_t"], p.bank_free[b], p.bank_free[b + 1])
        if not last:
            for i in range(4):
                m = nc.tensor.matmul(p.bank[b][:, i * P:(i + 1) * P], q["xt"][:, i, :], q["w"][:, i, :], start=True, stop=True)
            m1 = counted(m)
        for i in range(4):
            m = nc.tensor.matmul(p.bank[b + 1][:, i * P:(i + 1) * P], q["w"][:, i, :], q["xt"][:, i, :], start=True, stop=True)
        m2 = counted(m)
        if not last:
            q["x_t"] = V(nc.vector.tensor_tensor, q["x"][:, :, :], p.bank[b][:, :].rearrange("p (k t) -> p k t", k=4),
                         q["x"][:, :, :], ALU.add, after=(m1,))
            p.bank_free[b] = q["x_t"]
        q["xt_t"] = V(nc.vector.tensor_tensor, q["xt"][:, :, :], p.bank[b + 1][:, :].rearrange("p (k t) -> p k t", k=4),
                      q["xt"][:, :, :], ALU.add, after=(m2,))
        p.bank_free[b + 1] = q["xt_t"]

    def by_parity(tile_, par, n=2):
        return tile_[:, par::2, :]

    def solve(q, c, g):
        base = 4 * q["n"]
        R, U, lt = q["r"], q["u"], q["lt"]
        rt = []
        for par in range(2):
            b = base + par
            PE.wait(q["tri"], v_t, p.bank_free[b], state_t if c else None)
            for j in range(2):
                i, h, blk = 2 * j + par, 4 * g + 2 * j + par, 2 * g + j
                o = p.bank[b][:, j * 64:j * 64 + 64]
                m = nc.tensor.matmul(o, lt[:, i, 2, :], v_rows[:, c, 64 * h:64 * h + 64], start=True, stop=c == 0)
                if c:
                    m = nc.tensor.matmul(o, ar[64 * par:64 * par + 64, blk, c, 0, :], state[64 * par:64 * par + 64, blk, :],
                                         start=False, stop=True)
            m = counted(m)
            r_ = A(nc.scalar.activation, by_parity(R, par), p.bank[b][:, 0:P].rearrange("p (k t) -> p k t", k=2), ACT.Copy,
                   after=(m, q["free"]))
            p.bank_free[b] = r_
            rt.append(r_)
        yield
        b = base + 2
        PE.wait(rt, q["xt_t"], p.bank_free[b])
        for i in range(4):
            m = nc.tensor.matmul(p.bank[b][:, i * 64:i * 64 + 64], q["xt"][:, i, :], R[:, i, :], start=True, stop=True)
        m = counted(m)
        ut = A(nc.scalar.activation, U[:, :, :], p.bank[b][:, 0:256].rearrange("p (k t) -> p k t", k=4), ACT.Copy,
               after=(m, q["free"]))
        p.bank_free[b] = ut
        yield
        if c == 0:
            b = base + 3
            PE.wait(ut, bk_t, p.bank_free[b])
            for j in range(2):
                for par in range(2):
                    i, h = 2 * j + par, 4 * g + 2 * j + par
                    o = p.bank[b][64 * par:64 * par + 64, j * 64:j * 64 + 64]
                    nc.tensor.matmul(o, bt_rows[:, 64 * h:64 * h + 64], U[:, i, :], start=True, stop=False)
                    m = nc.tensor.matmul(o, kt_rows[:, 64 * h:64 * h + 64], v_rows[:, 0, 64 * h:64 * h + 64], start=False,
                                         stop=True)
            m = counted(m)
            s_ = V(nc.vector.tensor_tensor, state[:, 2 * g:2 * g + 2, :], p.bank[b][:, 0:P].rearrange("p (k t) -> p k t", k=2),
                   p.state_factor[:, 2 * g:2 * g + 2].unsqueeze(2).to_broadcast((P, 2, 64)), ALU.mult, after=(m, dead))
            p.bank_free[b] = s_
            state_t[2 * g] = state_t[2 * g + 1] = s_
            yield
        yt = q["y_t"] = []
        for par in range(2):
            b = base + par
            PE.wait(ut, p.bank_free[b])
            for j in range(2):
                i, h, blk = 2 * j + par, 4 * g + 2 * j + par, 2 * g + j
                o = p.bank[b][:, j * 64:j * 64 + 64]
                nc.tensor.matmul(o, lt[:, i, 1, :], U[:, i, :], start=True, stop=False)
                m = nc.tensor.matmul(o, lt[:, i, 3, :], v_rows[:, c, 64 * h:64 * h + 64], start=False, stop=c == 0)
                if c:
                    m = nc.tensor.matmul(o, ar[64 * par:64 * par + 64, blk, c, 1, :], state[64 * par:64 * par + 64, blk, :],
                                         start=False, stop=True)
            m = counted(m)
            dst = y[:, c, :].rearrange("p (h d) -> p h d", d=64)[:, 4 * g + par:4 * g + 4:2, :]
            y_ = A(nc.scalar.activation, dst, p.bank[b][:, 0:P].rearrange("p (k t) -> p k t", k=2), ACT.Copy, after=(m, dead))
            p.bank_free[b] = y_
            yt.append(y_)
        q["free"] = [PE.last(), V.last()]

    lg_, lg_ready, lg_b = gain_lnx_g
    lb_, lb_ready, lb_b = gain_lnx_b

    def heads_of(a):
        return a.rearrange("p (h d) -> p h d", d=64)

    rest_t = []
    for c in range(NT):
        rest = p.xn[:, c, 0:RW]
        b_ = G(nc.gpsimd.tensor_tensor, heads_of(rest), heads_of(v_rows[:, c, :]),
               p.rk_rows[:, c, :].unsqueeze(2).to_broadcast((P, RW_HEADS, 64)), ALU.mult, after=(rk_t, v_t, p.xn_free))
        b_ = G(nc.gpsimd.tensor_tensor, rest, rest, lb_, ALU.add, after=(b_, lb_ready))
        b_ = G(nc.gpsimd.tensor_tensor, rest, rest, gate[:, c, :], ALU.mult, after=(b_, gate_t))
        rest_t.append(G(nc.gpsimd.tensor_tensor, gate[:, c, :], gate[:, c, :], lg_, ALU.mult, after=(b_, lg_ready)))
    p.gain_free[lg_b] = p.gain_free[lb_b] = rest_t
    y_squares = in_channels_place("y_squares", 0, [P, 2, 4, 64])
    p.gn_free = [dead] * 2

    def finish_heads(q, c, g, yt):
        yc = heads_of(y[:, c, 256 * g:256 * g + 256])
        st_, sq_ = p.gn[:, 12 * q["n"]:12 * q["n"] + 12], y_squares[:, q["n"], :, :]

        def wide(a):
            return a.unsqueeze(2).to_broadcast((P, 4, 64))
        out = p.xn[:, c, 256 * g:256 * g + 256]
        a = V(nc.vector.tensor_reduce, out=st_[:, 0:4], in_=yc, axis=AX.X, op=ALU.add, after=(yt, p.gn_free[q["n"]]))
        a = V(nc.vector.tensor_scalar, st_[:, 4:8], st_[:, 0:4], 1.0 / 64, None, ALU.mult, after=(a,))
        a = V(nc.vector.tensor_tensor, yc, yc, wide(st_[:, 4:8]), ALU.subtract, after=(a,))
        s_ = A(nc.scalar.activation, sq_, yc, ACT.Square, scale=0.125, after=(a, p.gn_free[q["n"]]))
        yield
        s_ = V(nc.vector.tensor_reduce, out=st_[:, 8:12], in_=sq_, axis=AX.X, op=ALU.add, after=(s_,))
        s_ = p.power(st_[:, 8:12], LNX_EPS, s_)
        yield
        a = V(nc.vector.tensor_tensor, yc, yc, wide(st_[:, 8:12]), ALU.mult, after=(s_,))
        p.gn_free[q["n"]] = a
        a = V(nc.vector.tensor_tensor, y[:, c, 256 * g:256 * g + 256], y[:, c, 256 * g:256 * g + 256],
              gate[:, c, 256 * g:256 * g + 256], ALU.mult, after=(a, rest_t[c]))
        yield
        rows_done.append(V(nc.vector.tensor_tensor, out, out, y[:, c, 256 * g:256 * g + 256], ALU.add, after=(a, rest_t[c])))

    work_list = [(c, g) for c in range(NT) for g in range(3)]
    rows_done, unfinished = [], []

    def step(steps):
        for piece in list(steps):
            if next(piece, "end") == "end":
                steps.remove(piece)

    def chain(q, items):
        for c, g in items:
            yield from triangles(q, c, g)
            yield
            for level in range(1, 7):
                double_first(q, level)
                yield
                double_second(q, level)
                yield
            yield from solve(q, c, g)
            unfinished.append(finish_heads(q, c, g, q["y_t"]))
            yield

    chains = [chain(sets[0], work_list[0::2])]
    turns = 0
    while chains or unfinished:
        if turns == OFFSET:
            chains.append(chain(sets[1], work_list[1::2]))
        step(chains)
        step(unfinished)
        turns += 1
    gain_n2 = p.load_gain("a_norm2_g_2")
    p.keep_warm(30, 4)
    xt = p.to_channels(lambda tok, k: p.xn[:, tok, k * P:(k + 1) * P], KT, p.XH, p.XL, (rows_done, ma), p.xt_free,
                       defer=True)
    p.xn_free = xt
    rope = p.work("rope", 80, [P, 8, NT, 16])
    cosr, sinr = p.cosr, p.sinr
    angle, turns_, red = rope[:, 0, :, :], rope[:, 1, :, :], rope[:, 2, :, :]
    posf = V(nc.vector.tensor_copy, p.posf[:, :], p.posi[:, :], after=(pos_ready, rows_done))
    a = V(nc.vector.tensor_tensor, angle, p.posf[:, :].unsqueeze(2).to_broadcast((P, NT, 16)),
          p.freq[:, :].unsqueeze(1).to_broadcast((P, NT, 16)), ALU.mult, after=(posf,))
    magic = 12582912.0
    b_ = V(nc.vector.tensor_scalar, turns_, angle, 1.0 / (2 * math.pi), magic, ALU.mult, ALU.add, after=(a,))
    b_ = V(nc.vector.tensor_scalar, turns_, turns_, magic, None, ALU.subtract, after=(b_,))
    parts = (6.28125, 0.0019350051879882812, 2 * math.pi - 6.28125 - 0.0019350051879882812)
    src = angle
    for part in parts:
        a = V(nc.vector.scalar_tensor_tensor, out=red, in0=turns_, scalar=-part, in1=src, op0=ALU.mult, op1=ALU.add, after=(a, b_))
        src = red
    pi = 3.1415925
    a = V(nc.vector.tensor_scalar, red, red, pi, -pi, ALU.min, ALU.max, after=(a,))
    sin_t = A(nc.scalar.activation, sinr[:, :, :], red, ACT.Sin, after=(a,))
    c_ = A(nc.scalar.activation, rope[:, 3, :, :], red, ACT.Abs, after=(a,))
    c_ = V(nc.vector.tensor_scalar, rope[:, 3, :, :], rope[:, 3, :, :], -1.0, math.pi / 2, ALU.mult, ALU.add, after=(c_,))
    cos_t = A(nc.scalar.activation, cosr[:, :, :], rope[:, 3, :, :], ACT.Sin, after=(c_,))

    x_done = p.project_residual("a_w_out_2", X, xt)
    x_done = p.feed_forward(("a_ffn_gu_2",), "a_ffn_down_2", gain_n2, x_done)

    gain_kv, gain_b1 = p.load_gain("kv_norm_g_2"), p.load_gain("b_norm1_g_2")
    KH, KL = p.work("kv_channels_hi", 8, [P, KT, S], F32R), p.work("kv_channels_lo", 16, [P, KT, S], F32R)
    r = p.inv_rms(lambda tok: p.x[:, tok, :], D, EPS, x_done, p.rstd)
    kv_n = p.normalize(lambda tok: p.x[:, tok, :], lambda tok: p.xn[:, tok, :], D, gain_kv, p.rstd, r)
    p.keep_warm(18, 4)
    kv_x = p.to_channels(lambda tok, k: p.xn[:, tok, k * P:(k + 1) * P], KT, KH, KL, kv_n, defer=True)
    gain_lat = p.load_gain("kv_latent_g_2", 256)
    ckr = p.work("latent_rows", 24, [P, NT, 288])
    bproj = p.work("b_proj", 27, [P, NT, 768])
    causal = p.work("causal", 82, [P, 384])
    cz = G(nc.gpsimd.memset, causal[:, :], 0.0, after=(PE.last(), V.last(), A.last()))
    for c0, w, base_ in ((0, P, 0), (P, S, P)):
        cz = G(nc.gpsimd.affine_select, out=causal[:, c0:c0 + w], in_=causal[:, c0:c0 + w], compare_op=ALU.is_ge, fill=NEG,
               base=base_, pattern=[[-1, w]], channel_multiplier=1, after=(cz,))
    ckr_t, cq_t, qm_t = [], [], []
    LH, LL = p.work("latent_hi", 33, [P, 2, S], F32R), p.work("latent_lo", 35, [P, 2, S], F32R)
    QH, QL = p.work("q_latent_hi", 37, [P, 4, S], F32R), p.work("q_latent_lo", 41, [P, 4, S], F32R)
    kv_down = p.job("kv_w_down_2", (KH, KL), kv_x, KT, 0, 288, (0, 1), p.rows_of(at_tok(ckr), (0, 1), 288, ckr_t))
    next(kv_down)
    b_n = p.normalize(lambda tok: p.x[:, tok, :], lambda tok: p.xn[:, tok, :], D, gain_b1, p.rstd, r, kv_x)
    gain_q = p.load_gain("b_q_norm_g_2", 512)
    p.run(kv_down)
    b_x = p.to_channels(lambda tok, k: p.xn[:, tok, k * P:(k + 1) * P], KT, p.XH, p.XL, b_n, p.xt_free, defer=True)
    p.xn_free = b_x
    p.run(p.job("b_w_in_2", X, b_x, KT, 0, 512, (2, 3), p.rows_of(at_tok(bproj, (0, 512)), (2, 3), 512, cq_t)))
    lat = p.norm_to_channels(ckr, 256, gain_lat, EPS, LH, LL, [ckr_t] * NT)
    p.run(p.job("b_w_in_2", X, b_x, KT, 512, 256, (0, 1), p.rows_of(at_tok(bproj, (512, 768)), (0, 1), 256, qm_t)))
    qlat = p.norm_to_channels(bproj, 512, gain_q, EPS, QH, QL, [cq_t] * NT)
    kv = p.work("kv", 8, [P, NT, 2 * RW])
    q = p.work("q", 45, [P, NT, MLA_HEADS * QK])
    kv_t, q_t = [], []
    kv_dead = p.used_token(len(p.units) - 1)

    def kv_rows(done, c0, bank_ids, width):
        A.wait(kv_dead)
        V.wait(kv_dead)
        p.rows_of(at_tok(kv, (c0, c0 + width)), bank_ids, width, kv_t)(done)

    p.pending = [p.job("kv_w_up_2", (LH, LL), lat, 2, 0, 1024, (0, 1, 2, 3), lambda d: kv_rows(d, 0, (0, 1, 2, 3), 1024)),
                 p.job("kv_w_up_2", (LH, LL), lat, 2, 1024, 512, (0, 1), lambda d: kv_rows(d, 1024, (0, 1), 512))]
    p.pending += [p.job("b_q_up_2", (QH, QL), qlat, 4, c0, w, (0, 1), p.rows_of(at_tok(q, (c0, c0 + w)), (0, 1), w, q_t))
                  for c0, w in ((0, 512), (512, 512), (1024, 128))]
    tmp, kcat = p.work("rotate", 54.5 + 2, [P, 4, MLA_HEADS, 16]), p.work("k_cat", 60, [P, NT, MLA_HEADS * QK])

    def rotate(src, heads, ready):
        out, free = [], None
        for tok in range(NT):
            cb, sb_ = (x[:, tok, :].unsqueeze(1).to_broadcast((P, heads, 16)) for x in (cosr, sinr))
            t1, t2 = src[:, tok, :, 0:16], src[:, tok, :, 16:32]
            m = [V(nc.vector.tensor_tensor, tmp[:, i, 0:heads, :], x, w, ALU.mult, after=(ready, cos_t, sin_t, free))
                 for i, (x, w) in enumerate(((t1, cb), (t2, sb_), (t2, cb), (t1, sb_)))]
            out += [V(nc.vector.tensor_tensor, t1, tmp[:, 0, 0:heads, :], tmp[:, 1, 0:heads, :], ALU.subtract, after=m),
                    V(nc.vector.tensor_tensor, t2, tmp[:, 2, 0:heads, :], tmp[:, 3, 0:heads, :], ALU.add, after=m)]
            free = out[-2:]
        return out

    k_dead = [PE.last(), A.last()]
    k_turned = rotate(ckr[:, :, 256:288].unsqueeze(2), 1, ckr_t)
    k_rot = [G(nc.gpsimd.tensor_copy, kcat[:, tok, :].rearrange("p (h d) -> p h d", d=QK)[:, :, 64:96],
               ckr[:, tok, 256:288].unsqueeze(1).to_broadcast((P, MLA_HEADS, 32)), after=(k_turned, k_dead))
             for tok in range(NT)]
    qmT1 = p.work("memory_queries_1", 54.5, [P, 2, S])
    qm1 = heads_to_channels(512, qmT1, qm_t, n_blocks=2, src=bproj)
    mb = memory_attention(1, qmT1, qm1, "m1", between=lambda i: p.fill(1))
    p.fill_rest()

    kcat_h = kcat[:, :, :].rearrange("p t (h d) -> p t h d", d=QK)
    for tok in range(NT):
        k_rot.append(A(nc.scalar.activation, kcat_h[:, tok, :, 0:64],
                       kv[:, tok, :].rearrange("p (h d) -> p h d", d=P)[:, :, 0:64], ACT.Copy, after=(kv_t,)))
    q_rot = rotate(q[:, :, :].rearrange("p t (h d) -> p t h d", d=QK)[:, :, :, 64:96], MLA_HEADS, q_t)
    q96, k96 = p.work("q_channels", 20, [QK, MLA_HEADS, S]), p.work("k_channels", 69.5, [QK, MLA_HEADS, S])

    def to_heads(src, dst, ready, free):
        blocks = [(src[:, tok, QK * h:QK * (h + 1)], QK) for h in range(MLA_HEADS) for tok in range(NT)]
        return p.transposes(blocks, ready, lambda n, bank, done: p.copy(
            n, dst[:, 2 * n:2 * n + 2, :], bank[0:QK, :].rearrange("p (k t) -> p k t", k=2), (done, free)))
    heads_t = to_heads(kcat, k96, k_rot, None)
    heads_t += to_heads(q, q96, q_rot, [k_rot, heads_t])

    def qk_latent(h, bank, spans, off):
        for tok in range(NT):
            m = nc.tensor.matmul(bank[:, off[tok]:off[tok] + spans[tok]], q96[:, h, tok * P:(tok + 1) * P],
                                 k96[:, h, 0:spans[tok]], start=True, stop=True)
        return counted(m)

    p.bias_ready = cz
    ol = p.attention(list(range(MLA_HEADS)), qk_latent, (P, S), float(QK) ** -0.5, lambda h: causal[:, :],
                     lambda h, j: kv[:, j, P * h + 64:P * h + 128], 64, lambda i: p.xn[:, :, 64 * i:64 * i + 64],
                     [heads_t], "l", out_free=p.xn_free)
    gain_n3 = p.load_gain("b_norm2_g_2")
    xt = p.to_channels(lambda tok, k: p.xn[:, tok, k * P:(k + 1) * P], KT, p.XH, p.XL, (ol, mb),
                       p.used_token(len(p.units) - 1))
    p.xn_free = xt
    x_done = p.project_residual("b_w_out_2", X, xt)
    x_done = p.feed_forward(("b_ffn_gu_2",), "b_ffn_down_2", gain_n3, x_done)
    gain_last = p.load_gain("final_norm_g_2")
    r = p.inv_rms(lambda tok: p.x[:, tok, :], D, EPS, x_done, p.rstd)
    x_done = p.normalize(lambda tok: p.x[:, tok, :], lambda tok: p.x[:, tok, :], D, gain_last, p.rstd, r)
    SP.wait(x_done)
    nc.sync.dma_start(out_dram.rearrange("(t p) d -> p t d", p=P), p.x[:, :, :]).then_inc(io[0], 16)
    nc.sync.wait_ge(io[0], 32)
    return p.units


STREAMED = ("w_in", "w_ck", "w_cv", "w_out", "w_cq", "a_mem_kv_2", "b_mem_kv_2", "w_co", "w_gate", "w_up", "w_down",
            "a_w_in_2", "a_w_out_2", "a_ffn_gu_2", "a_ffn_down_2", "kv_w_down_2", "kv_w_up_2", "b_w_in_2", "b_q_up_2",
            "b_w_out_2", "b_ffn_gu_2", "b_ffn_down_2")
VECTORS = ("mix_norm_g", "moba_out_g", "diff_lambda", "diff_subln_g", "cross_norm_g", "mem_norm_g", "ffn_norm_g",
           "final_norm_g", "mem_norm_g_2", "a_norm1_g_2", "a_lnx_g_2", "a_lnx_b_2", "a_norm2_g_2", "kv_norm_g_2",
           "kv_latent_g_2", "b_norm1_g_2", "b_q_norm_g_2", "b_norm2_g_2", "final_norm_g_2")
PLAIN = ("x", "mem", "mem_2", "positions_2", "rel_bias_table", "a_shift_mu_2", "a_decay_bias_2", "a_aaa_bias_2",
         "a_k_k_2", "a_k_a_2", "a_r_k_2", "a_decay_up_2", "a_aaa_up_2", "a_gate_up_2")


def bucket_one_hot():
    dist = 255 - np.arange(384)
    n = np.maximum(dist, 0)
    ratio = np.log(np.maximum(n, 16).astype(np.float32) / np.float32(16)) / np.float32(math.log(8))
    large = np.minimum(16 + (ratio * np.float32(16)).astype(np.int32), 31)
    bucket = np.where(n < 16, n, large)
    hot = (bucket[None, :] == np.arange(33)[:, None]) & (dist >= 0)[None, :]
    hot[32] = dist < 0
    return hot.astype(np.float32)


def triangle_masks():
    r, c = np.arange(P)[:, None], np.arange(P)[None, :]
    masks = [r < c, r <= c, r < c, r <= c, r > c]
    for level in range(7):
        size = 1 << level
        masks.append((r // (2 * size) == c // (2 * size)) & (r // size > c // size))
    masks.append(masks[5].T)
    return np.stack(masks, axis=1).astype(np.float32)


def constants():
    half = 16
    inv_freq = np.power(10000.0, -np.arange(half, dtype=np.float64) / half).astype(np.float32)
    head_of = (np.arange(RW)[:, None] // 64 == np.arange(RW_HEADS)[None, :]).astype(np.float32)
    return {"bucket_one_hot": bucket_one_hot(), "triangle_masks": triangle_masks(), "inv_freq": inv_freq[None, :],
            "head_of": np.ascontiguousarray(head_of.reshape(RWB, P, RW_HEADS).transpose(1, 0, 2)),
            "head_of_t": np.ascontiguousarray(head_of.T)}


def place_unit(unit, spec, arrays):
    if spec[0] == "pair":
        _, names, pair, k0 = spec
        if len(names) == 2:
            gate, up = arrays[names[0]][0], arrays[names[1]][0]
        else:
            gate, up = arrays[names[0]][0][:, :FF], arrays[names[0]][0][:, FF:]
        v = unit.reshape(P, 4, 2, 256)
        for j, w in enumerate((gate, up)):
            v[:, :, j, :] = w[k0 * P:(k0 + 4) * P, 256 * pair:256 * pair + 256].reshape(4, P, 256).transpose(1, 0, 2)
        return
    _, name, k0, nk, c0, width, pitch = spec
    w = arrays[name].reshape(-1, arrays[name].shape[-1])
    v = unit[:, 0:nk * pitch].reshape(P, nk, pitch)
    v[:, :, 0:width] = w[k0 * P:(k0 + nk) * P, c0:c0 + width].reshape(nk, P, width).transpose(1, 0, 2)


FEED_FORWARD_UNITS = 2 * NPAIR + NPAIR
FIRST_UNITS = 2 * (6 + 2) + 2 * (2 + 2 + 2 + 2) + FEED_FORWARD_UNITS
LAYER_A_UNITS = 2 + (2 * 5 + 1) + 4 + FEED_FORWARD_UNITS
LAYER_B_UNITS = 2 + 2 + (2 + 1) + (1 + 1) + 3 + 4 + FEED_FORWARD_UNITS
TOTAL_UNITS = FIRST_UNITS + LAYER_A_UNITS + LAYER_B_UNITS


def kernel(**inputs):
    import concourse.bacc as bacc
    from concourse.bass_utils import run_bass_kernel_spmd

    nc = bacc.Bacc("TRN2", target_bir_lowering=False, num_devices=1)
    host = {n: np.ascontiguousarray(inputs[n]) for n in PLAIN}
    host.update({n: np.ascontiguousarray(inputs[n]).reshape(1, -1) for n in VECTORS})
    host.update(constants())
    for n in ("x", "mem", "mem_2"):
        host[n] = host[n].reshape(S, D)
    for n in ("a_decay_up_2", "a_aaa_up_2", "a_gate_up_2"):
        host[n] = host[n].reshape(host[n].shape[-2:])
    host["a_r_k_2"] = host["a_r_k_2"].reshape(1, RW)
    host["weights"] = np.zeros((TOTAL_UNITS, P, UNIT), np.float32)
    t = {n: nc.dram_tensor("in_" + n, a.shape, mybir.dt.from_np(a.dtype), kind="ExternalInput").ap()
         for n, a in host.items()}
    out = nc.dram_tensor("out", (S, D), F32, kind="ExternalOutput").ap()
    units = build(nc, t, out, TOTAL_UNITS)
    assert len(units) == TOTAL_UNITS, len(units)
    arrays = {n: np.asarray(inputs[n]) for n in STREAMED}
    for u, spec in enumerate(units):
        place_unit(host["weights"][u], spec, arrays)
    r = run_bass_kernel_spmd(nc, [{"in_" + n: a for n, a in host.items()}], core_ids=[0])
    return r.results[0]["out"].reshape(1, S, D)
```
